# Optimizing a Trainium2 kernel written in Bass

```python
import jax, jax.numpy as jnp
from jax import lax
import numpy as np

D_MODEL = 2048
BATCH = 1
SEQ = 256
DEPTH = 1

FOX_HEADS = 8
FOX_HEAD_DIM = 128
FOX_BLOCK = 128
GDN_HEADS = 8
GDN_HEAD_DIM = 128
GDN_CONV = 4
GDN_CHUNK = 64
MLSTM_HEADS = 8
MLSTM_QK_DIM = 64
MLSTM_V_DIM = 128
MLSTM_CHUNK = 64
D_FF = 5632
FFN_CONV = 3
N_BRANCH = 3
EPS = 1e-6

FOX_W = FOX_HEADS * FOX_HEAD_DIM
GDN_W = GDN_HEADS * GDN_HEAD_DIM
MLSTM_QK_W = MLSTM_HEADS * MLSTM_QK_DIM
MLSTM_V_W = MLSTM_HEADS * MLSTM_V_DIM

IN_SPLITS = (
    ("fox_q", FOX_W), ("fox_k", FOX_W), ("fox_v", FOX_W), ("fox_f", FOX_HEADS),
    ("gdn_qkv", 3 * GDN_W), ("gdn_z", GDN_W), ("gdn_b", GDN_HEADS), ("gdn_a", GDN_HEADS),
    ("ml_q", MLSTM_QK_W), ("ml_k", MLSTM_QK_W), ("ml_v", MLSTM_V_W),
    ("ml_i", MLSTM_HEADS), ("ml_f", MLSTM_HEADS), ("ml_o", MLSTM_V_W),
    ("gate", N_BRANCH * D_MODEL),
)
D_IN = sum(w for _, w in IN_SPLITS)

kernel_name = "hybrid_fox_gdn_mlstm_convffn"

def rmsnorm(x, g):
    x32 = x.astype(jnp.float32)
    y = x32 * lax.rsqrt(jnp.mean(x32 * x32, axis=-1, keepdims=True) + EPS)
    return (y * g.astype(jnp.float32)).astype(x.dtype)

def l2norm(x):
    return x * lax.rsqrt(jnp.sum(x * x, axis=-1, keepdims=True) + EPS)

def causal_dwconv(x, w):
    K = w.shape[0]
    S = x.shape[1]
    xp = jnp.pad(x, ((0, 0), (K - 1, 0), (0, 0)))
    return sum(xp[:, j:j + S] * w[j] for j in range(K))

def split_cols(h):
    out = {}
    off = 0
    for name, w in IN_SPLITS:
        out[name] = h[..., off:off + w]
        off += w
    return out

def to_chunks(x, L):
    B, S, H = x.shape[:3]
    rest = x.shape[3:]
    x = x.reshape((B, S // L, L, H) + rest)
    return x.transpose((1, 0, 3, 2) + tuple(range(4, x.ndim)))

def from_chunks(x):
    NC, B, H, L, d = x.shape
    return x.transpose(1, 0, 3, 2, 4).reshape(B, NC * L, H, d)

def fox_attention(q, k, v, log_f):
    B, S, H, Dh = q.shape
    F = jnp.cumsum(log_f, axis=1).transpose(0, 2, 1)
    kh = k.transpose(0, 2, 1, 3)
    vh = v.transpose(0, 2, 1, 3)
    NB = S // FOX_BLOCK
    qb = q.reshape(B, NB, FOX_BLOCK, H, Dh).transpose(1, 0, 3, 2, 4)
    Fb = F.reshape(B, H, NB, FOX_BLOCK).transpose(2, 0, 1, 3)
    kpos = jnp.arange(S)
    scale = Dh ** -0.5

    def block(args):
        qi, Fi, bi = args
        s = jnp.einsum('bhqd,bhkd->bhqk', qi, kh).astype(jnp.float32) * scale
        s = s + Fi[..., :, None] - F[:, :, None, :]
        qpos = bi * FOX_BLOCK + jnp.arange(FOX_BLOCK)
        s = jnp.where(kpos[None, :] <= qpos[:, None], s, -jnp.inf)
        p = jax.nn.softmax(s, axis=-1)
        return jnp.einsum('bhqk,bhkd->bhqd', p.astype(vh.dtype), vh)

    o = lax.map(block, (qb, Fb, jnp.arange(NB)))
    return o.transpose(1, 0, 3, 2, 4).reshape(B, S, H * Dh)

def gated_deltanet(q, k, v, beta, g):
    B, S, H, dk = q.shape
    dv = v.shape[-1]
    L = GDN_CHUNK
    q = l2norm(q) * dk ** -0.5
    k = l2norm(k)
    qc, kc, vc = to_chunks(q, L), to_chunks(k, L), to_chunks(v, L)
    bc = to_chunks(beta, L)
    gam = jnp.cumsum(to_chunks(g, L), axis=-1)
    tri = jnp.tril(jnp.ones((L, L), dtype=bool))
    decay = jnp.exp(jnp.where(tri, gam[..., :, None] - gam[..., None, :], -jnp.inf))
    kb = kc * bc[..., None]
    M = jnp.tril(jnp.einsum('nbhrd,nbhsd->nbhrs', kb, kc) * decay, -1)
    A = M + jnp.eye(L, dtype=M.dtype)
    rhs = jnp.concatenate([vc * bc[..., None], kb * jnp.exp(gam)[..., None]], axis=-1)
    X = lax.linalg.triangular_solve(A, rhs, left_side=True, lower=True, unit_diagonal=True)
    U, W = X[..., :dv], X[..., dv:]
    Aqk = jnp.einsum('nbhrd,nbhsd->nbhrs', qc, kc) * decay
    qg = qc * jnp.exp(gam)[..., None]
    kg = kc * jnp.exp(gam[..., -1:] - gam)[..., None]
    gL = jnp.exp(gam[..., -1])

    def step(St, xs):
        U_i, W_i, qg_i, kg_i, Aqk_i, gL_i = xs
        v_new = U_i - jnp.einsum('bhld,bhde->bhle', W_i, St)
        o = jnp.einsum('bhld,bhde->bhle', qg_i, St) + jnp.einsum('bhls,bhse->bhle', Aqk_i, v_new)
        St = St * gL_i[..., None, None] + jnp.einsum('bhld,bhle->bhde', kg_i, v_new)
        return St, o

    S0 = jnp.zeros((B, H, dk, dv), jnp.float32)
    _, o = lax.scan(step, S0, (U, W, qg, kg, Aqk, gL))
    return from_chunks(o)

def mlstm(q, k, v, i_pre, logf):
    B, S, H, dqk = q.shape
    dv = v.shape[-1]
    L = MLSTM_CHUNK
    q = q * dqk ** -0.5
    qc, kc, vc = to_chunks(q, L), to_chunks(k, L), to_chunks(v, L)
    ic = to_chunks(i_pre, L)
    bcum = jnp.cumsum(to_chunks(logf, L), axis=-1)
    tri = jnp.tril(jnp.ones((L, L), dtype=bool))
    Dm = jnp.where(tri, bcum[..., :, None] - bcum[..., None, :] + ic[..., None, :], -jnp.inf)
    Dmax = jnp.max(Dm, axis=-1)
    qk = jnp.einsum('nbhrd,nbhsd->nbhrs', qc, kc)

    def step(carry, xs):
        C, n, m = carry
        q_i, v_i, k_i, b_i, D_i, Dmax_i, qk_i = xs
        inter = b_i + m[..., None]
        m_r = jnp.maximum(inter, Dmax_i)
        w_inter = jnp.exp(inter - m_r)
        Wd = jnp.exp(D_i - m_r[..., None])
        Sm = Wd * qk_i
        num = w_inter[..., None] * jnp.einsum('bhld,bhde->bhle', q_i, C) + jnp.einsum('bhls,bhse->bhle', Sm, v_i)
        den = w_inter * jnp.einsum('bhld,bhd->bhl', q_i, n) + jnp.sum(Sm, axis=-1)
        h = num / jnp.maximum(jnp.abs(den), jnp.exp(-m_r))[..., None]
        wL = Wd[..., -1, :]
        C = w_inter[..., -1, None, None] * C + jnp.einsum('bhl,bhld,bhle->bhde', wL, k_i, v_i)
        n = w_inter[..., -1, None] * n + jnp.einsum('bhl,bhld->bhd', wL, k_i)
        return (C, n, m_r[..., -1]), h

    init = (jnp.zeros((B, H, dqk, dv), jnp.float32), jnp.zeros((B, H, dqk), jnp.float32),
            jnp.zeros((B, H), jnp.float32))
    _, h = lax.scan(step, init, (qc, vc, kc, bcum, Dm, Dmax, qk))
    return from_chunks(h)

def hybrid_layer(x, norm_mix_g, w_in, fox_f_bias, gdn_conv_w, gdn_a_log, gdn_dt_bias, gdn_norm_g,
                 ml_i_bias, ml_f_bias, ml_norm_g, gate_bias, w_fox_proj, w_gdn_proj, w_ml_proj,
                 w_out, norm_ffn_g, w_up, ffn_conv_w, w_down):
    B, S, D = x.shape
    f32 = jnp.float32
    xn = rmsnorm(x, norm_mix_g)
    p = split_cols(xn @ w_in)

    fq = p['fox_q'].reshape(B, S, FOX_HEADS, FOX_HEAD_DIM)
    fk = p['fox_k'].reshape(B, S, FOX_HEADS, FOX_HEAD_DIM)
    fv = p['fox_v'].reshape(B, S, FOX_HEADS, FOX_HEAD_DIM)
    fox_logf = jax.nn.log_sigmoid(p['fox_f'].astype(f32) + fox_f_bias.astype(f32))
    y_fox = fox_attention(fq, fk, fv, fox_logf)

    qkv = jax.nn.silu(causal_dwconv(p['gdn_qkv'], gdn_conv_w)).astype(f32)
    gq = qkv[..., :GDN_W].reshape(B, S, GDN_HEADS, GDN_HEAD_DIM)
    gk = qkv[..., GDN_W:2 * GDN_W].reshape(B, S, GDN_HEADS, GDN_HEAD_DIM)
    gv = qkv[..., 2 * GDN_W:].reshape(B, S, GDN_HEADS, GDN_HEAD_DIM)
    beta = jax.nn.sigmoid(p['gdn_b'].astype(f32))
    g = -jnp.exp(gdn_a_log.astype(f32)) * jax.nn.softplus(p['gdn_a'].astype(f32) + gdn_dt_bias.astype(f32))
    o_gdn = gated_deltanet(gq, gk, gv, beta, g)
    z = p['gdn_z'].astype(f32).reshape(B, S, GDN_HEADS, GDN_HEAD_DIM)
    y_gdn = (rmsnorm(o_gdn, gdn_norm_g) * jax.nn.silu(z)).reshape(B, S, GDN_W).astype(x.dtype)

    mq = p['ml_q'].astype(f32).reshape(B, S, MLSTM_HEADS, MLSTM_QK_DIM)
    mk = p['ml_k'].astype(f32).reshape(B, S, MLSTM_HEADS, MLSTM_QK_DIM)
    mv = p['ml_v'].astype(f32).reshape(B, S, MLSTM_HEADS, MLSTM_V_DIM)
    i_pre = p['ml_i'].astype(f32) + ml_i_bias.astype(f32)
    ml_logf = jax.nn.log_sigmoid(p['ml_f'].astype(f32) + ml_f_bias.astype(f32))
    h_tilde = mlstm(mq, mk, mv, i_pre, ml_logf)
    o_gate = jax.nn.sigmoid(p['ml_o'].astype(f32)).reshape(B, S, MLSTM_HEADS, MLSTM_V_DIM)
    y_ml = rmsnorm(o_gate * h_tilde, ml_norm_g).reshape(B, S, MLSTM_V_W).astype(x.dtype)

    gates = jax.nn.sigmoid(p['gate'].astype(f32) + gate_bias.astype(f32)).reshape(B, S, N_BRANCH, D)
    y = (gates[:, :, 0] * (y_fox @ w_fox_proj) + gates[:, :, 1] * (y_gdn @ w_gdn_proj)
         + gates[:, :, 2] * (y_ml @ w_ml_proj))
    x = x + y.astype(x.dtype) @ w_out

    xn = rmsnorm(x, norm_ffn_g)
    hid = causal_dwconv(xn @ w_up, ffn_conv_w)
    u, gt = hid[..., :D_FF], hid[..., D_FF:]
    return x + (jax.nn.silu(gt) * u) @ w_down

def setup_inputs(seed: int = 0) -> dict:
    key = jax.random.key(seed)
    ks = jax.random.split(key, 24)
    f32 = jnp.float32
    resid = (2 * DEPTH) ** -0.5

    def nrm(k, shape, scale):
        return jax.random.normal(k, shape, f32) * scale

    dt = jnp.exp(jax.random.uniform(ks[6], (DEPTH, GDN_HEADS), f32, np.log(1e-3), np.log(1e-1)))
    return {
        "x": nrm(ks[0], (BATCH, SEQ, D_MODEL), 1.0),
        "norm_mix_g": 1.0 + nrm(ks[1], (DEPTH, D_MODEL), 0.02),
        "w_in": nrm(ks[2], (DEPTH, D_MODEL, D_IN), D_MODEL ** -0.5),
        "fox_f_bias": 3.0 + nrm(ks[3], (DEPTH, FOX_HEADS), 0.5),
        "gdn_conv_w": nrm(ks[4], (DEPTH, GDN_CONV, 3 * GDN_W), GDN_CONV ** -0.5),
        "gdn_a_log": jnp.log(jax.random.uniform(ks[5], (DEPTH, GDN_HEADS), f32, 1.0, 16.0)),
        "gdn_dt_bias": dt + jnp.log(-jnp.expm1(-dt)),
        "gdn_norm_g": 1.0 + nrm(ks[7], (DEPTH, GDN_HEAD_DIM), 0.02),
        "ml_i_bias": nrm(ks[8], (DEPTH, MLSTM_HEADS), 0.1),
        "ml_f_bias": jax.random.uniform(ks[9], (DEPTH, MLSTM_HEADS), f32, 3.0, 6.0),
        "ml_norm_g": 1.0 + nrm(ks[10], (DEPTH, MLSTM_V_DIM), 0.02),
        "gate_bias": nrm(ks[11], (DEPTH, N_BRANCH * D_MODEL), 0.01),
        "w_fox_proj": nrm(ks[12], (DEPTH, FOX_W, D_MODEL), FOX_W ** -0.5),
        "w_gdn_proj": nrm(ks[13], (DEPTH, GDN_W, D_MODEL), GDN_W ** -0.5),
        "w_ml_proj": nrm(ks[14], (DEPTH, MLSTM_V_W, D_MODEL), MLSTM_V_W ** -0.5),
        "w_out": nrm(ks[15], (DEPTH, D_MODEL, D_MODEL), D_MODEL ** -0.5 * resid),
        "norm_ffn_g": 1.0 + nrm(ks[16], (DEPTH, D_MODEL), 0.02),
        "w_up": nrm(ks[17], (DEPTH, D_MODEL, 2 * D_FF), D_MODEL ** -0.5),
        "ffn_conv_w": nrm(ks[18], (DEPTH, FFN_CONV, 2 * D_FF), FFN_CONV ** -0.5),
        "w_down": nrm(ks[19], (DEPTH, D_FF, D_MODEL), D_FF ** -0.5 * resid),
        "norm_final_g": 1.0 + nrm(ks[20], (D_MODEL,), 0.02),
    }

def reference(x, norm_mix_g, w_in, fox_f_bias, gdn_conv_w, gdn_a_log, gdn_dt_bias, gdn_norm_g,
              ml_i_bias, ml_f_bias, ml_norm_g, gate_bias, w_fox_proj, w_gdn_proj, w_ml_proj,
              w_out, norm_ffn_g, w_up, ffn_conv_w, w_down, norm_final_g):
    for l in range(DEPTH):
        x = hybrid_layer(x, norm_mix_g[l], w_in[l], fox_f_bias[l], gdn_conv_w[l], gdn_a_log[l],
                         gdn_dt_bias[l], gdn_norm_g[l], ml_i_bias[l], ml_f_bias[l], ml_norm_g[l],
                         gate_bias[l], w_fox_proj[l], w_gdn_proj[l], w_ml_proj[l], w_out[l],
                         norm_ffn_g[l], w_up[l], ffn_conv_w[l], w_down[l])
    return rmsnorm(x, norm_final_g)


_drawn_inputs = setup_inputs


def setup_inputs(seed=0):
    import zlib

    import numpy as np

    out = dict(_drawn_inputs(seed))
    spreads = {}
    factors = {'gdn_norm_g': 28.934,
     'ml_i_bias': 64.0,
     'ml_norm_g': 36.689,
     'gate_bias': 8.0,
     'norm_ffn_g': 5.637,
     'norm_final_g': 23.796,
     'fox_f_bias': 26.544,
     'w_fox_proj': 2.902}
    for name, (base, spread) in spreads.items():
        noise = np.random.default_rng([zlib.crc32(name.encode()), seed]).standard_normal(out[name].shape)
        drawn = base * np.exp(spread * noise) if base else spread * noise
        out[name] = __import__('jax').numpy.asarray(drawn.astype(out[name].dtype))
    for name, factor in factors.items():
        out[name] = (out[name] * factor).astype(out[name].dtype)
    return out
```

```python
from contextlib import ExitStack

import concourse.bass as bass
from concourse import mybir

ALU = mybir.AluOpType
ACT = mybir.ActivationFunctionType
AX = mybir.AxisListType
F32 = mybir.dt.float32
F32R = mybir.dt.float32r

P = 128
SEQ = 256
D = 2048
KT = D // P
NT = SEQ // P
H = 8
HD = 128
L = 64
NC = SEQ // L
FF = 5632
FKT = FF // P
GROUPS = D // 256
EPS = 1e-6
NEG = -1e30

FOX_Q, FOX_K, FOX_V, FOX_F = 0, 1024, 2048, 3072
GDN_QKV, GDN_Z, GDN_B = 3080, 6152, 7176
ML_Q, ML_V, ML_I, ML_O, GATE = 7192, 8216, 9240, 9256, 10280

SLOTS = 4
CHUNK = 1024
UNIT = 4096

UNITS = [("small", 0, 0)]
UNITS += [("gdn", GDN_QKV + 256 * g, g) for g in range(12)]
UNITS += [("foxqk", FOX_Q + 256 * g, g) for g in range(8)]
UNITS += [("foxv", FOX_V + 512 * g, g) for g in range(2)]
UNITS += [("mlqk", ML_Q + 256 * g, g) for g in range(4)]
UNITS += [("mlv", ML_V + 512 * g, g) for g in range(2)]
UNITS += [("z", GDN_Z + 512 * g, g) for g in range(2)]
UNITS += [("mlo", ML_O + 512 * g, g) for g in range(2)]
UNIT_CHUNKS = {"small": 1, "gdn": 4, "foxqk": 4, "mlqk": 4, "foxv": 8, "mlv": 8, "z": 8, "mlo": 8}
CHUNKS = [(u, t) for u, (kind, _, _) in enumerate(UNITS) for t in range(UNIT_CHUNKS[kind])]
N1 = len(CHUNKS)


def last_chunk(kind, g):
    return max(c for c, (u, _) in enumerate(CHUNKS) if UNITS[u][0] == kind and UNITS[u][2] == g)


N2 = N1 + 18 * GROUPS
N3 = N2 + 2 * KT
N4 = N3 + 8 * (FF // 256)
N5 = N4 + 2 * FKT

LEVELS = 6


def plan_items():
    out = [(3, "cumsum", ())]
    for g in range(4, 12):
        out.append((last_chunk("gdn", g) + 3, "turn", (g,)))
    out.append((last_chunk("gdn", 3) + 5, "norm", (0,)))
    out.append((last_chunk("gdn", 7) + 5, "norm", (1,)))
    at = last_chunk("gdn", 11) + 4
    for tt in range(NT):
        out += [(at, "gam", (tt,)), (at + 2, "kk", (tt,)), (at + 3, "qk", (tt,))]
        at += 4
    for lv in range(LEVELS):
        row = [("solve_p", 0), ("solve_p", 1)]
        row += [("solve_x", 0)] * (lv < LEVELS - 1) + [("solve_xt", 0)]
        row += [("solve_x", 1)] * (lv < LEVELS - 1) + [("solve_xt", 1)]
        for name, tt in row:
            out.append((at, name, (tt, lv)))
            at += 1
    out += [(at, "wt", (0,)), (at + 1, "wt", (1,))]
    at += 3
    for c in range(NC):
        out += [(at, "vnew", (c,))]
        if c < NC - 1:
            out += [(at + 2, "ds", (c,))]
        out += [(at + 3, "o", (c,))]
        at += 4
    at = max(at, last_chunk("foxv", 1) + 2)
    for kt in range(NT):
        out.append((at + kt, "fbc", (kt,)))
    at += 4
    for hg in range(2):
        out += [(at, "s0", (hg,)), (at + 1, "s1", (hg,))]
        at += 2
    for hg in range(2):
        out += [(at + 1, "p0", (hg,)), (at + 2, "p1", (hg,))]
        at += 2
    for hg in range(2):
        out.append((at + 2 + hg, "pv", (hg,)))
    at += 4
    out.append((last_chunk("mlqk", 3) + 4, "mturn", ()))
    at = max(at, last_chunk("mlv", 1) + 1)
    for tt in range(NT):
        out.append((at, "vbc", (tt,)))
        at += 1
    at += 2
    for c in range(1, NC):
        out.append((at, "msel", (c,)))
        at += 1
    out.append((at + 1, "mtail", ()))
    at += 2
    for tt in range(NT):
        out += [(at, "mbc", (tt,)), (at + 2, "mqk", (tt,))]
        at += 2
    at += 1
    for c in range(NC):
        if c:
            out.append((at, "qc", (c,)))
        out += [(at, "dc", (c,)), (at + 1, "sv", (c,))]
        at += 2
    gy = max(last_chunk("z", 1) + 4, 0)
    out += [(gy, "gout", (0,)), (gy + 1, "gout", (1,))]
    at = max(at + 3, last_chunk("mlo", 1) + 3)
    out += [(at, "mout", (0,)), (at, "mout", (1,))]
    order = sorted(range(len(out)), key=lambda k: (min(out[k][0], N1 - 1), out[k][0], k))
    return [(min(out[k][0], N1 - 1), out[k][1], out[k][2]) for k in order]


ITEMS = plan_items()
ITEM = {(name, args): k for k, (_, name, args) in enumerate(ITEMS)}


def hybrid_layer_kernel(nc, x, norm_mix_g, w_in, fox_f_bias, gdn_conv_w, gdn_a_log, gdn_dt_bias, gdn_norm_g,
                        ml_i_bias, ml_f_bias, ml_norm_g, gate_bias, w_fox_proj, w_gdn_proj, w_ml_proj,
                        w_out, norm_ffn_g, w_up, ffn_conv_w, w_down, norm_final_g, out):
    ctx = ExitStack()
    with ctx:
        cursor = [nc.sbuf_base + (-nc.sbuf_base) % 64]

        def small(name, shape, dt=F32):
            n = 4
            for s in shape[1:]:
                n *= s
            at = cursor[0]
            cursor[0] += n + (-n) % 32
            return nc.alloc_sbuf_tensor_at(name, shape, dt, offset=at)

        raw = small("raw", [P, SLOTS, CHUNK])
        w_hi = small("w_hi", [P, SLOTS, CHUNK], F32R)
        w_lo = small("w_lo", [P, SLOTS, CHUNK], F32R)
        xnT = small("xnT", [P, KT, 2 * SEQ], F32R)
        ident = small("ident", [P, P])
        ones = small("ones", [P, P])
        upto = small("upto", [P, P])
        upto_c = small("upto_c", [P, P])
        same_c = small("same_c", [P, P])
        last_c = small("last_c", [P, P])
        sel = small("sel", [P, 2, P])
        level = small("level", [P, LEVELS, P])
        cols = small("cols", [P, 82])
        conv_c = small("conv_c", [P, 4, 24])
        fconv_c = small("fconv_c", [P, 3, 2 * FKT])
        bias5 = small("bias5", [P, 5, H])
        alog = small("alog", [P, H])
        pre5 = small("pre5", [P, NT, 5, H])
        soft = small("soft", [P, NT, 3, H])
        soft_n = small("soft_n", [P, NT, 3, H])
        soft_e = small("soft_e", [P, NT, 3, H])
        neg_a = small("neg_a", [P, H])
        lf = small("lf", [P, NT, H])
        gl = small("gl", [P, NT, 2, H])
        cum = small("cum", [P, NT, 2, H])
        tot = small("tot", [P, NT, 2, H])
        fcum = small("fcum", [P, NT, H])
        beta = small("beta", [P, NT, H])
        rn = small("rn", [P, 2, NT, H])
        eg = small("eg", [P, NT, H])
        c_m = small("c_m", [P, NT, H])
        c_w = small("c_w", [P, NT, H])
        c_k = small("c_k", [P, NT, H])
        e_last = small("e_last", [P, NC, H])
        tiny = small("tiny", [P, NT, H])
        vs = small("vs", [P, NT, H])
        dmax = small("dmax", [P, NT, H])
        inter = small("inter", [P, NT, H])
        m_t = small("m_t", [P, NT, H])
        w_int = small("w_int", [P, NT, H])
        w_int8 = small("w_int8", [P, NT, H])
        e_m = small("e_m", [P, NT, H])
        bm = small("bm", [P, NT, H])
        c_kw = small("c_kw", [P, NT, H])
        w_last = small("w_last", [P, NT, 2, H])
        n_st = small("n_st", [P, H // 2, 2])
        den = small("den", [P, NT, H])
        den2 = small("den2", [P, NT, H])
        rd = small("rd", [P, NT, H])
        fmax = small("fmax", [P, 2, 2, 4])
        fsum = small("fsum", [P, 2, 2, 4])
        ss = small("ss", [P, 4, H])
        rstd = small("rstd", [P, 4, H])
        eps_c = small("eps_c", [P, 2])
        arena = cursor[0] + (-cursor[0]) % 32

        def part(name, unit, shape, dt=F32, skip=0):
            n = 4
            for s in shape[1:]:
                n *= s
            assert arena + unit * UNIT + skip + n <= nc.sbuf_usable_end, (name, arena, nc.sbuf_usable_end)
            return nc.alloc_sbuf_tensor_at(name, shape, dt, offset=arena + unit * UNIT + skip)

        rows = part("rows", 0, [P, 5, P])
        x_in = part("x_in", 20, [P, NT, D])
        x_sq = part("x_sq", 14, [P, D])
        gq = part("gq", 0, [P, H, SEQ])
        gk = part("gk", 2, [P, H, SEQ])
        gkt = part("gkt", 4, [P, NT, H, HD])
        gvt = part("gvt", 6, [P, NT, H, HD])
        aqk = part("aqk", 8, [P, NT, H, P])
        nt_ = part("nt", 10, [P, NT, H, P])
        xm = part("xm", 12, [P, NT, H, P])
        xmt = part("xmt", 14, [P, NT, H, P])
        pm_ = part("pm", 16, [P, NT, H, P])
        wt = part("wt", 16, [P, NT, H, P])
        ed = part("ed", 18, [P, NT, H, P])
        sq = part("sq", 18, [P, H, SEQ])
        nlv = part("nlv", 18, [P, NT, H, P])
        st = part("st", 2, [P, H, HD])
        vn = part("vn", 3, [P, H, HD])
        kbg = part("kbg", 12, [P, NT, H, HD])
        pre = part("pre", 26, [P, 2, SEQ + 4])
        acc = part("acc", 26, [P, 2, SEQ], skip=2080)
        vT = part("vT", 27, [P, 2, SEQ], skip=32)
        fq = part("fq", 20, [P, H, SEQ])
        fk = part("fk", 22, [P, H, SEQ])
        fv = part("fv", 24, [P, NT, H, HD])
        mf0 = part("mf0", 0, [P, H, P])
        mf1 = part("mf1", 1, [P, H, SEQ])
        fr = part("fr", 14, [P, NT, H, P])
        p0 = part("p0", 3, [P, 2, 4, P])
        p1 = part("p1", 4, [P, 2, 4, SEQ])
        pt0 = part("pt0", 0, [P, 4, 2, SEQ])
        pt1 = part("pt1", 2, [P, 2, 4, P])
        mq = part("mq", 26, [P, H // 2, SEQ])
        mk = part("mk", 27, [P, H // 2, SEQ])
        mkt = part("mkt", 8, [P, NT, H, L])
        mv = part("mv", 9, [P, NT, H, HD])
        mr = part("mr", 0, [P, NT, H, P])
        me = part("me", 2, [P, NT, H, P])
        smt = part("smt", 4, [P, NT, H, P])
        c_st = part("c_st", 0, [P, H // 2, 2, HD])
        c_n = part("c_n", 2, [P, H // 2, HD])
        mt1 = part("mt1", 1, [P, H, HD])
        z = part("z", 20, [P, NT, H, HD])
        mo = part("mo", 22, [P, NT, H, HD])
        osq = part("osq", 24, [P, H, HD])
        y_gdn = part("y_gdn", 12, [P, H, 2 * SEQ], F32R)
        y_fox = part("y_fox", 16, [P, H, 2 * SEQ], F32R)
        y_ml = part("y_ml", 24, [P, H, 2 * SEQ], F32R)
        yT = part("yT", 0, [P, KT, SEQ])
        g_sum = part("g_sum", 4, [P, 2, SEQ])
        g_sig = part("g_sig", 4, [P, 2, SEQ], skip=2048)
        g_pr = part("g_pr", 5, [P, 2, SEQ])
        g_y = part("g_y", 5, [P, 2, SEQ], skip=2048)
        side = part("side", 6, [P, 2, 2 * SEQ], F32R)
        x1 = part("x1", 20, [P, NT, D])
        hT = part("hT", 8, [P, FKT, SEQ])
        upre = part("upre", 0, [P, 2, 2, SEQ + 2])
        uacc = part("uacc", 2, [P, 2, 2, SEQ])
        usil = part("usil", 4, [P, 2, SEQ])
        junk = part("junk", 0, [P, D])
        xs = part("xs", 2, [P, NT, D])
        gfin = part("gfin", 24, [P, D])
        ps = ctx.enter_context(nc.psum_tensor("ps", [P, 8, 512], F32))

        def sem(name):
            return ctx.enter_context(nc.semaphore(name))

        def per_slot(name):
            return [sem(f"{name}{s}") for s in range(SLOTS)]

        raw_loaded, hi_ready, lo_ready, chunk_used = (
            per_slot(n) for n in ("raw_loaded", "hi_ready", "lo_ready", "chunk_used"))
        pair_free = [sem(f"pair_free{p}") for p in range(2)]
        item_done = [sem(f"item_done{p}") for p in range(2)]
        item_free = [sem(f"item_free{p}") for p in range(2)]
        names = """x_loaded rows_loaded small_loaded x_again gfin_loaded stored consts rows_turned cols_ready
            sums_ready rstd_ready xs_ready xt_written xt_hi xt_ready
            dve_chain act_chain pool_chain pre5_ready soft_in soft_exp soft_out beta_exp neg_exp gates_ready
            conv_ready silu_ready sq_ready norm_in norm_root norm_out
            gr_ready gam_raw eg_ready e_masked e_exp dk_ready nt_raw nt_strict level_ready inv_start kbg_ready
            egq_raw qg_ready coef_in coef_exp coef_ready vb_ready kg_ready st_ready
            fr_ready mf_raw mf_ready smax_ready p_exp p_ready foxhi_ready
            mr_ready me_copied me_masked mrow_ready mstat_in mstat_exp mstat_ready mtail_in mtail_exp kw_ready
            mt_raw mt_masked mt_exp mstate_ready
            gsq_in gsq_done groot_in groot_done gy_ready ghi_ready msq_in msq_done mroot_in mroot_done my_ready
            mhi_ready
            gate_in gate_sig gate_free2 proj_free side_hi side_ready side_used
            rowbank_done x1_ready bank_read up_acc up_silu up_free h_ready
            fin_sums fin_root fin_ready""".split()
        S = {n: sem(n) for n in names}
        pair_read = [sem(f"pair_read{p}") for p in range(2)]
        up_read = [sem(f"up_read{p}") for p in range(2)]

        block = ctx.enter_context(nc.Block())

        def load(sp, c, it, dst, src):
            s = c % SLOTS
            if c >= SLOTS:
                sp.wait_ge(lo_ready[s], c // SLOTS + it)
            sp.dma_start(dst, src).then_inc(raw_loaded[s], 16)

        def split_hi(act, c, it=0):
            s, n = c % SLOTS, (640 if c == 0 else CHUNK)
            act.wait_ge(raw_loaded[s], 16 * (c // SLOTS + 1) + (32 if s == 0 else 0) + 16 * it)
            if c >= SLOTS:
                act.wait_ge(chunk_used[s], c // SLOTS + it)
            act.activation(w_hi[:, s, 0:n], raw[:, s, 0:n], ACT.Copy).then_inc(hi_ready[s], 1)

        def split_lo(eng, c, it=0):
            s, n = c % SLOTS, (640 if c == 0 else CHUNK)
            eng.wait_ge(hi_ready[s], c // SLOTS + 1 + it)
            eng.tensor_tensor(w_lo[:, s, 0:n], raw[:, s, 0:n], w_hi[:, s, 0:n],
                              ALU.subtract).then_inc(lo_ready[s], 1)

        def on_pool(c):
            return c % SLOTS == SLOTS - 1

        def chunk_done(eng, c, it=0):
            eng.wait_ge(chunk_used[c % SLOTS], c // SLOTS + 1 + it)

        def item_written(eng, k):
            eng.wait_ge(item_done[k % 2], k // 2 + 1)

        def item_read(eng, name, *args):
            k = ITEM[name, args]
            eng.wait_ge(item_free[k % 2], k // 2 + 1)

        def pair(k):
            b = 4 + 2 * (k % 2)
            return ps[:, b:b + 2, :]

        def heads(ap):
            return ap.rearrange("p a (h d) -> p (a h) d", d=P)

        def over_free(ap, n):
            return ap.unsqueeze(2).to_broadcast([ap.shape[0], ap.shape[1], n])

        def over_heads(ap, n):
            return ap.unsqueeze(1).to_broadcast([ap.shape[0], n, ap.shape[1]])

        def chunk_rows(c):
            return slice(L * (c % 2), L * (c % 2) + L), c // 2

        gam, bc_ = cum[:, :, 0, :], cum[:, :, 1, :]
        i_pre = pre5[:, :, 3, :]

        @block.sync
        def _(sp):
            xf = x.rearrange("b (t p) d -> p (b t) d", p=P)
            sp.dma_start(x_in[:, :, :], xf).then_inc(S["x_loaded"], 16)
            sp.dma_start(rows[0:16, 0, :], norm_mix_g.rearrange("a (t p) -> (a t) p", p=P)).then_inc(S["rows_loaded"], 16)
            sp.dma_start(rows[16:32, 0, :], norm_ffn_g.rearrange("a (t p) -> (a t) p", p=P)).then_inc(S["rows_loaded"], 16)
            sp.dma_start(rows[32:80, 0, :], gate_bias.rearrange("a (t p) -> (a t) p", p=P)).then_inc(S["rows_loaded"], 16)
            sp.dma_start(rows[80:81, 0, :], gdn_norm_g).then_inc(S["rows_loaded"], 16)
            sp.dma_start(rows[81:82, 0, :], ml_norm_g).then_inc(S["rows_loaded"], 16)
            sp.dma_start(rows[0:96, 1, :], gdn_conv_w.rearrange("a j (t p) -> (a j t) p", p=P)).then_inc(S["rows_loaded"], 16)
            fc = ffn_conv_w.rearrange("a j (t p) -> (a j t) p", p=P)
            for n in range(3):
                m = min(P, 264 - P * n)
                sp.dma_start(rows[0:m, 2 + n, :], fc[P * n:P * n + m, :]).then_inc(S["rows_loaded"], 16)
            w = w_in.rearrange("a (t p) n -> p (a t) n", p=P)
            r0 = raw[:, 0, 0:640].rearrange("p (t n) -> p t n", n=40)
            for col, n, dst in ((FOX_F, 8, 0), (GDN_B, 16, 8), (ML_I, 16, 24)):
                sp.dma_start(r0[:, :, dst:dst + n], w[:, :, col:col + n]).then_inc(raw_loaded[0], 16)

            def bias(dst, src):
                sp.dma_start(dst, src.partition_broadcast(P) if src.ndim == 1 else
                             src[0, :].partition_broadcast(P)).then_inc(S["small_loaded"], 16)

            sp.wait_ge(S["consts"], 1)
            bias(bias5[:, 0, :], fox_f_bias)
            bias(bias5[:, 2, :], gdn_dt_bias)
            bias(bias5[:, 3, :], ml_i_bias)
            bias(bias5[:, 4, :], ml_f_bias)
            bias(alog[:, :], gdn_a_log)

            for c in range(1, N1):
                u, t = CHUNKS[c]
                kind, col, _ = UNITS[u]
                if UNIT_CHUNKS[kind] == 4:
                    src, n = w[:, 4 * t:4 * t + 4, col:col + 256], 256
                else:
                    src, n = w[:, 2 * t:2 * t + 2, col:col + 512], 512
                load(sp, c, 0, raw[:, c % SLOTS, :].rearrange("p (t n) -> p t n", n=n), src)
            w_br = [m.rearrange("a (t p) n -> p (a t) n", p=P) for m in (w_fox_proj, w_gdn_proj, w_ml_proj)]
            with sp.Fori(1, GROUPS // 2 + 1) as i:
                c = N1
                for j in range(2):
                    for b in range(3):
                        for t in range(4):
                            load(sp, c, i * 9 - 9, raw[:, c % SLOTS, :].rearrange("p (t n) -> p t n", n=256),
                                 w[:, 4 * t:4 * t + 4, bass.ds(i * 512 + (GATE + b * D + j * 256 - 512), 256)])
                            c += 1
                        for t in range(2):
                            load(sp, c, i * 9 - 9, raw[:, c % SLOTS, :].rearrange("p (t n) -> p t n", n=256),
                                 w_br[b][:, 4 * t:4 * t + 4, bass.ds(i * 512 + (j * 256 - 512), 256)])
                            c += 1
            sp.wait_ge(item_free[0], (len(ITEMS) + 1) // 2)
            sp.wait_ge(item_free[1], len(ITEMS) // 2)
            sp.dma_start(x1[:, :, :], xf).then_inc(S["x_again"], 16)
            wo = w_out.rearrange("a k n -> (a k) n")
            with sp.Fori(1, KT // 2 + 1) as i:
                for j in range(4):
                    load(sp, N2 + j, i - 1, raw[:, (N2 + j) % SLOTS, :],
                         wo[bass.ds(i * 256 + (128 * (j // 2) - 256), P), CHUNK * (j % 2):CHUNK * (j % 2) + CHUNK])
            wu = w_up.rearrange("a (t p) n -> p (a t) n", p=P)
            with sp.Fori(1, FF // 512 + 1) as i:
                for j in range(16):
                    v, side_, t = j // 8, j // 4 % 2, j % 4
                    load(sp, N3 + j, i * 4 - 4, raw[:, (N3 + j) % SLOTS, :].rearrange("p (t n) -> p t n", n=256),
                         wu[:, 4 * t:4 * t + 4, bass.ds(i * 512 + (FF * side_ + 256 * v - 512), 256)])
            sp.dma_start(gfin[:, :], norm_final_g.partition_broadcast(P)).then_inc(S["gfin_loaded"], 16)
            wd = w_down.rearrange("a k n -> (a k) n")
            with sp.Fori(1, FKT // 2 + 1) as i:
                for j in range(4):
                    load(sp, N4 + j, i - 1, raw[:, (N4 + j) % SLOTS, :],
                         wd[bass.ds(i * 256 + (128 * (j // 2) - 256), P), CHUNK * (j % 2):CHUNK * (j % 2) + CHUNK])
            of = out.rearrange("b (t p) d -> p (b t) d", p=P)
            for tt in range(NT):
                sp.wait_ge(S["fin_ready"], tt + 1)
                sp.dma_start(of[:, tt, :], x1[:, tt, :]).then_inc(S["stored"], 16)
            sp.wait_ge(S["stored"], 16 * NT)

        @block.tensor
        def _(pe):
            def mm(o, l, r, start=True, stop=True):
                return pe.matmul(o, l, r, start=start, stop=stop)

            def columns(c, it, xh, kt0, nkt, b0):
                s = c % SLOTS
                pe.wait_ge(lo_ready[s], c // SLOTS + 1 + it)
                for t in range(4):
                    kt = kt0 + t
                    for b in range(2):
                        at = t * 256 + b * P
                        mm(ps[:, b0 + b, :], w_hi[:, s, at:at + P], xh[:, kt, :], kt == 0, False)
                        last = mm(ps[:, b0 + b, 0:SEQ], w_lo[:, s, at:at + P], xh[:, kt, 0:SEQ], False, kt == nkt - 1)
                last.then_inc(chunk_used[s], 1)

            def three(o, xh, tt, s, lo, hi, start, stop):
                mm(o, xh[:, tt * P:tt * P + P], w_hi[:, s, lo:hi], start, False)
                mm(o, xh[:, tt * P:tt * P + P], w_lo[:, s, lo:hi], False, False)
                return mm(o, xh[:, SEQ + tt * P:SEQ + tt * P + P], w_hi[:, s, lo:hi], False, stop)

            def tokens(c, kt0, b0):
                s = c % SLOTS
                pe.wait_ge(lo_ready[s], c // SLOTS + 1)
                for t in range(2):
                    for tt in range(NT):
                        last = three(ps[:, b0 + tt, :], xnT[:, kt0 + t, :], tt, s, 512 * t, 512 * t + 512,
                                     kt0 + t == 0, kt0 + t == KT - 1)
                last.then_inc(chunk_used[s], 1)

            def row_chunk(c, it, first, final):
                s, k2, half = c % SLOTS, (c - N2) // 2 % 2, (c - N2) % 2
                pe.wait_ge(lo_ready[s], c // SLOTS + 1 + it)
                for tt in range(NT):
                    for q in range(2):
                        last = three(ps[:, 4 * tt + 2 * half + q, :], side[:, k2, :], tt, s,
                                     512 * q, 512 * q + 512, first, final)
                last.then_inc(chunk_used[s], 1)

            def turn_x(n0, src):
                for q in range(4):
                    for t in range(4):
                        for tt in range(NT):
                            kt = 4 * q + t
                            last = pe.transpose(ps[:, 2 * q + t // 2, (t % 2) * SEQ + tt * P:(t % 2) * SEQ + tt * P + P],
                                                src[:, tt, kt * P:kt * P + P], ident[:, :])
                    last.then_inc(S["xt_written"], 1)

            def item(k):
                _, name, args = ITEMS[k]
                if k >= 2:
                    pe.wait_ge(item_free[k % 2], k // 2)
                o = pair(k)
                oh = heads(o)
                if name == "cumsum":
                    pe.wait_ge(S["gates_ready"], 2)
                    pe.wait_ge(S["consts"], 3)
                    g32 = gl[:, :, :, :].rearrange("p t a h -> p (t a h)")
                    mm(o[:, 0, 0:32], upto_c[:, :], g32)
                    mm(o[:, 0, 32:64], same_c[:, :], g32)
                    mm(o[:, 0, 64:72], upto[:, :], lf[:, 0, :])
                    mm(o[:, 0, 72:80], upto[:, :], lf[:, 1, :], True, False)
                    last = mm(o[:, 0, 72:80], ones[:, :], lf[:, 0, :], False, True)
                elif name == "turn":
                    g, = args
                    pe.wait_ge(S["silu_ready"], g + 1)
                    for b in range(2):
                        for tt in range(NT):
                            src = gk[:, 2 * (g - 4) + b, tt * P:tt * P + P] if g < 8 else vT[:, b, tt * P:tt * P + P]
                            last = pe.transpose(o[:, 0, (2 * b + tt) * P:(2 * b + tt + 1) * P], src, ident[:, :])
                elif name == "norm":
                    w, = args
                    pe.wait_ge(S["sq_ready"], w + 1)
                    for tt in range(NT):
                        for h in range(H):
                            last = mm(o[:, 0, tt * H + h:tt * H + h + 1], sq[:, h, tt * P:tt * P + P], ones[:, 0:1])
                elif name == "gam":
                    tt, = args
                    pe.wait_ge(S["gr_ready"], tt + 1)
                    for q in range(2):
                        last = mm(o[:, q, :], ones[:, :], nlv[:, tt, 4 * q:4 * q + 4, :].rearrange("p h d -> p (h d)"))
                elif name in ("kk", "qk"):
                    tt, = args
                    t = slice(tt * P, tt * P + P)
                    for h in range(H):
                        last = mm(oh[:, h, :], gk[:, h, t], (gk if name == "kk" else gq)[:, h, t])
                elif name == "solve_p":
                    tt, lv = args
                    pe.wait_ge(S["level_ready"], 2 * lv + tt + 1)
                    if lv == 0:
                        pe.wait_ge(S["inv_start"], 2)
                    else:
                        item_read(pe, "solve_x", tt, lv - 1)
                    for h in range(H):
                        last = mm(oh[:, h, :], nlv[:, tt, h, :], xm[:, tt, h, :])
                elif name == "solve_x":
                    tt, lv = args
                    item_read(pe, "solve_p", tt, lv)
                    if lv:
                        item_read(pe, "solve_xt", tt, lv - 1)
                    for h in range(H):
                        last = mm(oh[:, h, :], xmt[:, tt, h, :], pm_[:, tt, h, :])
                elif name == "solve_xt":
                    tt, lv = args
                    item_read(pe, "solve_p", tt, lv)
                    if lv:
                        item_read(pe, "solve_xt", tt, lv - 1)
                    for h in range(H):
                        last = mm(oh[:, h, :], pm_[:, tt, h, :], xmt[:, tt, h, :])
                elif name == "wt":
                    tt, = args
                    pe.wait_ge(S["kbg_ready"], tt + 1)
                    item_read(pe, "solve_xt", tt, LEVELS - 1)
                    for h in range(H):
                        last = mm(oh[:, h, :], kbg[:, tt, h, :], xmt[:, tt, h, :])
                elif name == "vnew":
                    c, = args
                    r, tt = chunk_rows(c)
                    if c == 0:
                        pe.wait_ge(S["vb_ready"], 2)
                        item_read(pe, "wt", 0)
                        item_read(pe, "wt", 1)
                    else:
                        pe.wait_ge(S["st_ready"], c)
                    for h in range(H):
                        last = mm(oh[r, h, :], xmt[r, tt, h, r], gvt[r, tt, h, :], True, c == 0)
                        if c:
                            last = mm(oh[r, h, :], wt[:, tt, h, r], st[:, h, :], False, True)
                elif name == "ds":
                    c, = args
                    r, tt = chunk_rows(c)
                    item_read(pe, "vnew", c)
                    pe.wait_ge(S["kg_ready"], 2)
                    for h in range(H):
                        last = mm(oh[:, h, :], gkt[r, tt, h, :], vn[r, h, :])
                elif name == "o":
                    c, = args
                    r, tt = chunk_rows(c)
                    item_read(pe, "vnew", c)
                    pe.wait_ge(S["qg_ready"], 2)
                    for h in range(H):
                        last = mm(oh[r, h, :], aqk[r, tt, h, r], vn[r, h, :], True, c == 0)
                        if c:
                            last = mm(oh[r, h, :], gq[:, h, c * L:c * L + L], st_old(c)[:, h, :], False, True)
                elif name == "fbc":
                    kt, = args
                    pe.wait_ge(S["fr_ready"], kt + 1)
                    for q in range(2):
                        last = mm(o[:, q, :], ones[:, :], fr[:, kt, 4 * q:4 * q + 4, :].rearrange("p h d -> p (h d)"))
                elif name == "s0":
                    hg, = args
                    for h in range(4):
                        last = mm(oh[:, h, :], fq[:, 4 * hg + h, 0:P], fk[:, 4 * hg + h, 0:P])
                elif name == "s1":
                    hg, = args
                    oq = o.rearrange("p a (h d) -> p (a h) d", d=SEQ)
                    for h in range(4):
                        last = mm(oq[:, h, :], fq[:, 4 * hg + h, P:SEQ], fk[:, 4 * hg + h, :])
                elif name == "p0":
                    hg, = args
                    pe.wait_ge(S["p_ready"], hg + 1)
                    oq = o.rearrange("p a (h d) -> p (a h) d", d=SEQ)
                    for h in range(4):
                        pe.transpose(oq[:, h, 0:P], p0[:, hg, h, :], ident[:, :])
                        last = pe.transpose(oq[:, h, P:SEQ], p1[:, hg, h, 0:P], ident[:, :])
                elif name == "p1":
                    hg, = args
                    for h in range(4):
                        last = pe.transpose(oh[:, h, :], p1[:, hg, h, P:SEQ], ident[:, :])
                elif name == "pv":
                    hg, = args
                    item_read(pe, "p0", hg)
                    item_read(pe, "p1", hg)
                    oq = o.rearrange("p a (h d) -> p (a h) d", d=SEQ)
                    for h in range(4):
                        mm(oq[:, h, :], fv[:, 0, 4 * hg + h, :], pt0[:, h, hg, :], True, False)
                        last = mm(oq[:, h, P:SEQ], fv[:, 1, 4 * hg + h, :], pt1[:, hg, h, :], False, True)
                elif name == "mturn":
                    for tt in range(NT):
                        for j in range(4):
                            last = pe.transpose(o[:, tt, j * P:j * P + P], mk[:, j, tt * P:tt * P + P], ident[:, :])
                elif name == "vbc":
                    tt, = args
                    pe.wait_ge(S["mr_ready"], tt + 1)
                    for q in range(2):
                        last = mm(o[:, q, :], ones[:, :], mr[:, tt, 4 * q:4 * q + 4, :].rearrange("p h d -> p (h d)"))
                elif name == "msel":
                    c, = args
                    pe.wait_ge(S["mrow_ready"], c)
                    last = mm(o[:, 0, 0:H], sel[:, (c - 1) % 2, :], m_t[:, (c - 1) // 2, :])
                elif name == "mtail":
                    pe.wait_ge(S["mstat_ready"], 1)
                    last = mm(o[:, 0, 0:16], last_c[:, :], bm[:, :, :].rearrange("p t h -> p (t h)"))
                    for b in range(2):
                        last = mm(o[:, 0, 16 + 16 * b:32 + 16 * b], sel[:, b, :], w_int[:, :, :].rearrange("p t h -> p (t h)"))
                elif name == "mbc":
                    tt, = args
                    pe.wait_ge(S["mr_ready"], 2 + tt + 1)
                    for q in range(2):
                        last = mm(o[:, q, :], ones[:, :], mr[:, tt, 4 * q:4 * q + 4, :].rearrange("p h d -> p (h d)"))
                elif name == "mqk":
                    tt, = args
                    for h in range(H):
                        r = slice(L * (h % 2), L * (h % 2) + L)
                        t = slice(tt * P, tt * P + P)
                        last = mm(oh[:, 4 * (h % 2) + h // 2, :], mk[r, h // 2, t], mq[r, h // 2, t])
                elif name == "qc":
                    c, = args
                    r, tt = chunk_rows(c)
                    pe.wait_ge(S["mstate_ready"], c)
                    for j in range(H // 2):
                        last = mm(oh[r, 2 * j:2 * j + 2, :], mq[:, j, c * L:c * L + L], c_st[:, j, :, :])
                elif name == "dc":
                    c, = args
                    r, tt = chunk_rows(c)
                    pe.wait_ge(S["kw_ready"], 2)
                    item_read(pe, "mqk", tt)
                    if c:
                        for j in range(H // 2):
                            mm(o[r, 1, 2 * j:2 * j + 2], mq[:, j, c * L:c * L + L], n_st[:, j, :])
                    for h in range(H):
                        g = slice(L * (h % 2), L * (h % 2) + L)
                        j = h // 2
                        mm(o[r, 1, 8 + h:9 + h], smt[r, tt, h, r], ones[r, 0:1])
                        mm(o[g, 1, 16 + j:17 + j], mkt[r, tt, h, :], ones[r, 0:1])
                        last = mm(o[g, 0, j * P:j * P + P], mkt[r, tt, h, :], mv[r, tt, h, :])
                elif name == "sv":
                    c, = args
                    r, tt = chunk_rows(c)
                    for h in range(H):
                        last = mm(oh[r, h, :], smt[r, tt, h, r], mv[r, tt, h, :])
                elif name in ("gout", "mout"):
                    half, = args
                    pe.wait_ge(S["gy_ready" if name == "gout" else "my_ready"], 2)
                    src = gvt if name == "gout" else mv
                    oq = o.rearrange("p a (h d) -> p (a h) d", d=SEQ)
                    for h in range(4):
                        for tt in range(NT):
                            last = pe.transpose(oq[:, h, tt * P:tt * P + P], src[:, tt, 4 * half + h, :], ident[:, :])
                last.then_inc(item_done[k % 2], 1)

            def st_old(c):
                return st

            pe.wait_ge(S["consts"], 2)
            pe.wait_ge(S["rows_loaded"], 16 * 9)
            for n, m in enumerate((82, 96, P, P, 8)):
                last = pe.transpose(ps[:, 4 + n // 4, (n % 4) * P:(n % 4) * P + m], rows[0:m, n, :], ident[0:m, 0:m])
            last.then_inc(S["rows_turned"], 1)
            pe.wait_ge(S["xs_ready"], 2)
            pe.wait_ge(S["cols_ready"], 1)
            turn_x(0, x_in)
            pe.wait_ge(S["xt_ready"], 4)

            k = 0
            for c, (u, t) in enumerate(CHUNKS):
                kind = UNITS[u][0]
                if t == 0 and u >= 2:
                    pe.wait_ge(pair_free[u % 2], u // 2)
                if kind == "small":
                    pe.wait_ge(lo_ready[0], 1)
                    for tt in range(NT):
                        for kt in range(KT):
                            last = three(ps[:, tt, 0:40], xnT[:, kt, :], tt, 0, 40 * kt, 40 * kt + 40,
                                         kt == 0, kt == KT - 1)
                    last.then_inc(chunk_used[0], 1)
                elif UNIT_CHUNKS[kind] == 4:
                    columns(c, 0, xnT, 4 * t, KT, 2 * (u % 2))
                else:
                    tokens(c, 2 * t, 2 * (u % 2))
                while k < len(ITEMS) and ITEMS[k][0] == c:
                    item(k)
                    k += 1
            assert k == len(ITEMS)
            for p in range(2):
                pe.wait_ge(pair_free[p], (len(UNITS) + 1 - p) // 2)
                pe.wait_ge(item_free[p], (len(ITEMS) + 1 - p) // 2)
            ys = (y_fox, y_gdn, y_ml)

            with pe.Fori(0, GROUPS // 2) as i:
                c = N1
                for q in range(6):
                    pe.wait_ge(pair_read[q % 2], i * 3 + (q // 2 + 1))
                    for t in range(4):
                        columns(c, i * 9, xnT, 4 * t, KT, 4 * (q % 2))
                        c += 1
                    for t in range(2):
                        columns(c, i * 9, ys[q % 3], 4 * t, H, 4 * (q % 2) + 2)
                        c += 1
            for p in range(2):
                pe.wait_ge(pair_read[p], 3 * (GROUPS // 2) + 1)
            for j in range(4):
                if j % 2 == 0:
                    pe.wait_ge(S["side_ready"], j // 2 + 1)
                row_chunk(N2 + j, 0, j < 2, False)
            with pe.Fori(0, KT // 2 - 2) as i:
                for j in range(4):
                    if j % 2 == 0:
                        pe.wait_ge(S["side_ready"], i * 2 + (j // 2 + 3))
                    row_chunk(N2 + 4 + j, i, False, False)
            for j in range(4):
                if j % 2 == 0:
                    pe.wait_ge(S["side_ready"], KT - 2 + j // 2 + 1)
                row_chunk(N2 + 2 * KT - 4 + j, 0, False, j >= 2)
            pe.wait_ge(S["bank_read"], 1)
            pe.wait_ge(S["xs_ready"], 4)
            turn_x(4, xs)
            pe.wait_ge(S["xt_ready"], 8)
            with pe.Fori(0, FF // 512) as i:
                for v in range(2):
                    pe.wait_ge(up_read[v], i + 1)
                    for j in range(8):
                        columns(N3 + 8 * v + j, i * 4, xnT, 4 * (j % 4), KT, 4 * v + 2 * (j // 4))
            for v in range(2):
                pe.wait_ge(up_read[v], FF // 512 + 1)
            for j in range(4):
                if j % 2 == 0:
                    pe.wait_ge(S["side_ready"], KT + j // 2 + 1)
                row_chunk(N4 + j, 0, j < 2, False)
            with pe.Fori(0, FKT // 2 - 2) as i:
                for j in range(4):
                    if j % 2 == 0:
                        pe.wait_ge(S["side_ready"], i * 2 + (KT + j // 2 + 3))
                    row_chunk(N4 + 4 + j, i, False, False)
            for j in range(4):
                if j % 2 == 0:
                    pe.wait_ge(S["side_ready"], KT + FKT - 2 + j // 2 + 1)
                row_chunk(N4 + 2 * FKT - 4 + j, 0, False, j >= 2)

        @block.scalar
        def _(act):
            order = [0]

            def chain(ins):
                order[0] += 1
                ins.then_inc(S["act_chain"], 1)
                act.wait_ge(S["act_chain"], order[0])

            def f(o, i, fn, **kw):
                return act.activation(o, i, fn, **kw)

            def flat(ap):
                return ap.rearrange("p h d -> p (h d)")

            def turn_x_hi(n0, col0):
                for q in range(4):
                    act.wait_ge(S["xt_written"], n0 + q + 1)
                    for t in range(4):
                        kt = 4 * q + t
                        last = f(xnT[:, kt, 0:SEQ], ps[:, 2 * q + t // 2, (t % 2) * SEQ:(t % 2) * SEQ + SEQ],
                                 ACT.Identity, scale=cols[:, col0 + kt:col0 + kt + 1], bias=0.0)
                    last.then_inc(S["xt_hi"], 1)

            def out_hi(k, half, y, col, ready):
                item_written(act, k)
                o = pair(k).rearrange("p a (h d) -> p (a h) d", d=SEQ)
                f(y[:, 4 * half:4 * half + 4, 0:SEQ], o, ACT.Identity,
                  **({"scale": cols[:, col:col + 1], "bias": 0.0} if col is not None else {"bias": 0.0})).then_inc(S[ready], 1)

            def item(k):
                _, name, args = ITEMS[k]
                o = pair(k)
                free = item_free[k % 2]
                if name == "turn":
                    g, = args
                    item_written(act, k)
                    dst = (gkt if g < 8 else gvt)[:, :, 2 * (g % 4):2 * (g % 4) + 2, :]
                    f(dst.rearrange("p t h d -> p h t d"), o[:, 0, :].rearrange("p (h t d) -> p h t d", h=2, t=2),
                      ACT.Copy).then_inc(free, 1)
                    if g == 7:
                        item_read(act, "norm", 0)
                        f(sq[:, :, :], gk[:, :, :], ACT.Square).then_inc(S["sq_ready"], 1)
                elif name == "norm":
                    w, = args
                    act.wait_ge(S["norm_in"], w + 1)
                    f(rn[:, w, :, :], rn[:, w, :, :], ACT.Sqrt).then_inc(S["norm_root"], 1)
                    if w == 1:
                        act.wait_ge(S["coef_in"], 1)
                        f(c_k[:, :, :], c_k[:, :, :], ACT.Exp)
                        f(eg[:, :, :], eg[:, :, :], ACT.Exp).then_inc(S["coef_exp"], 1)
                elif name == "gam":
                    tt, = args
                    act.wait_ge(S["gam_raw"], tt + 1)
                    f(pm_[:, tt, :, :], heads(o), ACT.Exp).then_inc(free, 1)
                    act.wait_ge(S["e_masked"], 2 * tt + 2)
                    f(ed[:, tt, :, :], ed[:, tt, :, :], ACT.Exp).then_inc(S["e_exp"], 1)
                elif name == "solve_p":
                    tt, lv = args
                    item_written(act, k)
                    if lv == 0:
                        act.wait_ge(S["qg_ready"], 2)
                        act.wait_ge(S["coef_ready"], 1)
                    for h in range(H):
                        last = f(pm_[:, tt, h, :], heads(o)[:, h, :], ACT.Identity, scale=c_m[:, tt, h:h + 1], bias=0.0)
                    last.then_inc(free, 1)
                elif name == "wt":
                    tt, = args
                    item_written(act, k)
                    f(wt[:, tt, :, :], heads(o), ACT.Copy, scale=-1.0).then_inc(free, 1)
                elif name == "vnew":
                    c, = args
                    r, tt = chunk_rows(c)
                    item_written(act, k)
                    if c >= 1:
                        item_read(act, "o", c - 1)
                    f(vn[r, :, :], heads(o)[r], ACT.Copy).then_inc(free, 1)
                elif name == "o":
                    c, = args
                    r, tt = chunk_rows(c)
                    item_written(act, k)
                    f(gvt[r, tt, :, :], heads(o)[r], ACT.Copy).then_inc(free, 1)
                elif name in ("s0", "s1"):
                    hg, = args
                    b, p, w = (0, p0, P) if name == "s0" else (1, p1, SEQ)
                    act.wait_ge(S["smax_ready"], 2 * hg + b + 1)
                    for h in range(4):
                        last = f(p[:, hg, h, :], p[:, hg, h, :], ACT.Exp, bias=fmax[:, hg, b, h:h + 1],
                                 accum_out=fsum[:, hg, b, h:h + 1])
                    last.then_inc(S["p_exp"], 1)
                elif name == "p0":
                    hg, = args
                    item_written(act, k)
                    f(pt0[:, :, hg, :], o.rearrange("p a (h d) -> p (a h) d", d=SEQ), ACT.Copy).then_inc(free, 1)
                elif name == "p1":
                    hg, = args
                    item_written(act, k)
                    f(flat(pt1[:, hg, :, :]), o[:, 0, :], ACT.Copy).then_inc(free, 1)
                elif name == "pv":
                    out_hi(k, args[0], y_fox, None, "foxhi_ready")
                elif name == "mturn":
                    item_written(act, k)
                    f(mkt[:, :, :, :].rearrange("p t h d -> p (t h d)"), o.rearrange("p a b -> p (a b)"), ACT.Copy).then_inc(free, 1)
                elif name == "vbc":
                    tt, = args
                    item_written(act, k)
                    f(me[:, tt, :, :], heads(o), ACT.Copy).then_inc(free, 1)
                elif name == "msel":
                    if args[0] == NC - 1:
                        act.wait_ge(S["mstat_in"], 1)
                        f(w_int[:, :, :], w_int[:, :, :], ACT.Exp)
                        f(e_m[:, :, :], m_t[:, :, :], ACT.Exp, scale=-1.0).then_inc(S["mstat_exp"], 1)
                elif name == "mtail":
                    act.wait_ge(S["mtail_in"], 1)
                    f(c_kw[:, :, :], c_kw[:, :, :], ACT.Exp).then_inc(S["mtail_exp"], 1)
                elif name == "mbc":
                    tt, = args
                    act.wait_ge(S["mt_masked"], tt + 1)
                    f(me[:, tt, :, :], me[:, tt, :, :], ACT.Exp).then_inc(S["mt_exp"], 1)
                elif name == "gout":
                    out_hi(k, args[0], y_gdn, 80, "ghi_ready")
                elif name == "mout":
                    out_hi(k, args[0], y_ml, 81, "mhi_ready")

            def unit(u):
                kind, _, g = UNITS[u]
                b0, free = 2 * (u % 2), pair_free[u % 2]
                if kind == "small":
                    act.wait_ge(S["soft_in"], 1)
                    f(soft_e[:, :, :, :], soft_n[:, :, :, :], ACT.Exp).then_inc(S["soft_exp"], 1)
                    f(beta[:, :, :], pre5[:, :, 1, :], ACT.Exp, scale=-1.0)
                    act.wait_ge(S["small_loaded"], 80)
                    f(neg_a[:, :], alog[:, :], ACT.Exp).then_inc(S["neg_exp"], 1)
                    act.wait_ge(S["soft_exp"], 1)
                    f(soft_e[:, :, :, :], soft_e[:, :, :, :], ACT.Ln, bias=eps_c[:, 1:2]).then_inc(S["soft_out"], 1)
                elif kind == "gdn":
                    act.wait_ge(S["conv_ready"], g + 1)
                    if g < 8:
                        dst = (gq if g < 4 else gk)[:, 2 * (g % 4):2 * (g % 4) + 2, :]
                    else:
                        if g > 8:
                            item_read(act, "turn", g - 1)
                        dst = vT[:, :, :]
                    if g == 0:
                        act.wait_ge(S["cols_ready"], 1)
                    f(dst, acc[:, :, :], ACT.Silu).then_inc(S["silu_ready"], 1)
                    if g == 3:
                        act.wait_ge(S["silu_ready"], 4)
                        f(sq[:, :, :], gq[:, :, :], ACT.Square).then_inc(S["sq_ready"], 1)
                elif kind in ("foxv", "mlv", "z", "mlo"):
                    chunk_done(act, CHUNKS.index((u, 7)))
                    if kind == "z" and g == 0:
                        item_read(act, "pv", 1)
                    dst = {"foxv": fv, "mlv": mv, "z": z, "mlo": mo}[kind]
                    fn = {"foxv": ACT.Copy, "mlv": ACT.Copy, "z": ACT.Silu, "mlo": ACT.Sigmoid}[kind]
                    f(dst[:, :, 4 * g:4 * g + 4, :].rearrange("p t h d -> p t (h d)"), ps[:, b0:b0 + 2, :], fn).then_inc(free, 1)

            def gdn_output():
                for tt in range(NT):
                    if tt == 1:
                        act.wait_ge(S["gsq_done"], 1)
                    else:
                        item_read(act, "o", NC - 1)
                        item_read(act, "pv", 1)
                    f(osq[:, :, :], gvt[:, tt, :, :], ACT.Square).then_inc(S["gsq_in"], 1)
                act.wait_ge(S["groot_in"], 1)
                f(rstd[:, 2:4, :], rstd[:, 2:4, :], ACT.Sqrt).then_inc(S["groot_done"], 1)

            def ml_output():
                for tt in range(NT):
                    act.wait_ge(S["msq_in"], tt + 1)
                    f(osq[:, :, :], mv[:, tt, :, :], ACT.Square).then_inc(S["msq_done"], 1)
                act.wait_ge(S["mroot_in"], 1)
                f(rstd[:, 2:4, :], rstd[:, 2:4, :], ACT.Sqrt).then_inc(S["mroot_done"], 1)

            for c in range(SLOTS):
                split_hi(act, c)
            act.wait_ge(S["x_loaded"], 16)
            for tt in range(NT):
                chain(f(x_sq[:, :], x_in[:, tt, :], ACT.Square, accum_out=ss[:, 0, tt:tt + 1]))
            act.wait_ge(S["consts"], 1)
            f(rstd[:, 0, 0:2], ss[:, 0, 0:2], ACT.Sqrt, scale=1.0 / D, bias=eps_c[:, 0:1]).then_inc(S["sums_ready"], 1)
            act.wait_ge(S["cols_ready"], 1)
            turn_x_hi(0, 0)

            k = 0
            for c, (u, t) in enumerate(CHUNKS):
                split_hi(act, c + SLOTS)
                if t == UNIT_CHUNKS[UNITS[u][0]] - 1:
                    unit(u)
                while k < len(ITEMS) and ITEMS[k][0] == c:
                    if ITEMS[k][1:] == ("gout", (0,)):
                        gdn_output()
                    if ITEMS[k][1:] == ("mout", (0,)):
                        ml_output()
                    item(k)
                    k += 1
            with act.Fori(0, GROUPS // 2) as i:
                c = N1
                for q in range(6):
                    for t in range(6):
                        split_hi(act, c + SLOTS, i * 9)
                        if t == 3:
                            act.wait_ge(S["gate_in"], i * 6 + (q + 1))
                            for b in range(2):
                                last = f(g_sig[:, b, :], g_sum[:, b, :], ACT.Sigmoid,
                                         bias=cols[:, bass.ds(i * 4 + (32 + 16 * (q % 3) + 2 * (q // 3) + b), 1)])
                            last.then_inc(S["gate_sig"], 1)
                        c += 1

            def side_hi(n, kt_ap, slot, it2):
                act.wait_ge(chunk_used[(n[0]) % SLOTS], n[0] // SLOTS + 1 + it2)
                f(side[:, slot, 0:SEQ], kt_ap, ACT.Copy).then_inc(S["side_hi"], 1)

            for kt in range(2):
                act.wait_ge(S["proj_free"], GROUPS * 3)
                f(side[:, kt, 0:SEQ], yT[:, kt, :], ACT.Copy).then_inc(S["side_hi"], 1)
            with act.Fori(0, KT // 2 - 1) as i:
                for j in range(4):
                    split_hi(act, N2 + SLOTS + j, i)
                    if j % 2:
                        side_hi((N2 + j,), yT[:, bass.ds(i * 2 + (2 + j // 2), 1), :].rearrange("p a b -> p (a b)"), j // 2, i)
            for j in range(4):
                split_hi(act, N3 + j)
            for tt in range(NT):
                act.wait_ge(S["x1_ready"], tt + 1)
                chain(f(junk[:, :], x1[:, tt, :], ACT.Square, accum_out=ss[:, 1, tt:tt + 1]))
                f(rstd[:, 1, tt:tt + 1], ss[:, 1, tt:tt + 1], ACT.Sqrt, scale=1.0 / D, bias=eps_c[:, 0:1]).then_inc(S["sums_ready"], 1)
            turn_x_hi(4, 16)
            with act.Fori(0, FF // 512) as i:
                for v in range(2):
                    for j in range(8):
                        split_hi(act, N3 + 8 * v + j + SLOTS, i * 4)
                    act.wait_ge(S["up_acc"], i * 2 + (v + 1))
                    f(usil[:, :, :], uacc[:, 1, :, :], ACT.Silu).then_inc(S["up_silu"], 1)
            for kt in range(2):
                f(side[:, kt, 0:SEQ], hT[:, kt, :], ACT.Copy).then_inc(S["side_hi"], 1)
            with act.Fori(0, FKT // 2 - 1) as i:
                for j in range(4):
                    split_hi(act, N4 + SLOTS + j, i)
                    if j % 2:
                        side_hi((N4 + j,), hT[:, bass.ds(i * 2 + (2 + j // 2), 1), :].rearrange("p a b -> p (a b)"), j // 2, i)
            for tt in range(NT):
                act.wait_ge(S["x1_ready"], NT + tt + 1)
                chain(f(junk[:, :], x1[:, tt, :], ACT.Square, accum_out=ss[:, 0, 2 + tt:3 + tt]))
                f(rstd[:, 0, 2 + tt:3 + tt], ss[:, 0, 2 + tt:3 + tt], ACT.Sqrt, scale=1.0 / D, bias=eps_c[:, 0:1]).then_inc(S["fin_root"], 1)

        @block.vector
        def _(dve):
            order = [0]

            def chain(ins):
                order[0] += 1
                ins.then_inc(S["dve_chain"], 1)
                dve.wait_ge(S["dve_chain"], order[0])

            tt_ = dve.tensor_tensor

            def turn_x_lo(n0, col0):
                for q in range(4):
                    dve.wait_ge(S["xt_hi"], n0 + q + 1)
                    for t in range(4):
                        kt = 4 * q + t
                        last = dve.scalar_tensor_tensor(
                            xnT[:, kt, SEQ:2 * SEQ], ps[:, 2 * q + t // 2, (t % 2) * SEQ:(t % 2) * SEQ + SEQ],
                            cols[:, col0 + kt:col0 + kt + 1], xnT[:, kt, 0:SEQ], ALU.mult, ALU.subtract)
                    last.then_inc(S["xt_ready"], 1)

            def out_lo(k, half, y, col, ready):
                dve.wait_ge(S[ready], half + 1)
                o = pair(k)
                for a in range(2):
                    q = 4 * half + 2 * a
                    last = dve.scalar_tensor_tensor(
                        y[:, q:q + 2, SEQ:2 * SEQ], o[:, a, :].rearrange("p (h d) -> p h d", d=SEQ),
                        cols[:, col:col + 1] if col is not None else 1.0, y[:, q:q + 2, 0:SEQ], ALU.mult, ALU.subtract)
                last.then_inc(item_free[k % 2], 1)

            def on_diagonal(dst, vec):
                return tt_(dst, over_heads(ident[:, :], H), over_free(vec, P), ALU.mult)

            def item(k):
                _, name, args = ITEMS[k]
                o = pair(k)
                oh = heads(o)
                free = item_free[k % 2]
                if name == "cumsum":
                    item_written(dve, k)
                    dve.tensor_copy(cum[:, :, :, :].rearrange("p t a h -> p (t a h)"), o[:, 0, 0:32])
                    dve.tensor_copy(tot[:, :, :, :].rearrange("p t a h -> p (t a h)"), o[:, 0, 32:64])
                    dve.tensor_copy(fcum[:, :, :].rearrange("p t h -> p (t h)"), o[:, 0, 64:80]).then_inc(free, 1)
                elif name == "norm":
                    w, = args
                    item_written(dve, k)
                    dve.tensor_scalar(rn[:, w, :, :].rearrange("p t h -> p (t h)"), o[:, 0, 0:16], EPS, None,
                                      ALU.add).then_inc(S["norm_in"], 1)
                    dve.wait_ge(S["norm_root"], w + 1)
                    chain(dve.reciprocal(rn[:, w, :, :], rn[:, w, :, :]))
                    if w == 0:
                        dve.tensor_scalar(rn[:, 0, :, :], rn[:, 0, :, :], HD ** -0.5, None, ALU.mult).then_inc(free, 1)
                    else:
                        item_read(dve, "cumsum")
                        chain(tt_(c_k[:, :, :], tot[:, :, 0, :], gam, ALU.subtract))
                        chain(tt_(c_m[:, :, :], beta[:, :, :], rn[:, 1, :, :], ALU.mult))
                        dve.tensor_copy(eg[:, :, :], gam).then_inc(S["coef_in"], 1)
                        dve.wait_ge(S["coef_exp"], 1)
                        tt_(c_w[:, :, :], c_m[:, :, :], eg[:, :, :], ALU.mult).then_inc(free, 1)
                        tt_(c_k[:, :, :], c_k[:, :, :], rn[:, 1, :, :], ALU.mult).then_inc(S["coef_ready"], 1)
                        dve.wait_ge(S["coef_ready"], 1)
                        for tt in range(NT):
                            on_diagonal(nlv[:, tt, :, :], cum[:, tt, 0, :]).then_inc(S["gr_ready"], 1)
                elif name == "gam":
                    tt, = args
                    item_written(dve, k)
                    tt_(ed[:, tt, :, :], oh, over_free(cum[:, tt, 0, :], P), ALU.subtract).then_inc(S["gam_raw"], 1)
                    dve.wait_ge(S["e_exp"], tt + 1)
                    tt_(ed[:, tt, :, :], ed[:, tt, :, :], over_free(rn[:, 1, tt, :], P), ALU.mult).then_inc(S["dk_ready"], 1)
                elif name == "kk":
                    tt, = args
                    item_written(dve, k)
                    dve.wait_ge(S["dk_ready"], tt + 1)
                    tt_(nt_[:, tt, :, :], oh, ed[:, tt, :, :], ALU.mult).then_inc(free, 1)
                elif name == "qk":
                    tt, = args
                    item_written(dve, k)
                    tt_(aqk[:, tt, :, :], oh, ed[:, tt, :, :], ALU.mult).then_inc(free, 1)
                    item_read(dve, "gam", tt)
                    q_t = gq[:, :, tt * P:tt * P + P]
                    for cb in range(2):
                        dve.tensor_copy(e_last[:, 2 * tt + cb, :], pm_[:, tt, :, L * cb + L - 1])
                    tt_(q_t, q_t, pm_[:, tt, :, :], ALU.mult).then_inc(S["qg_ready"], 1)
                    if tt == 1:
                        for t2 in range(NT):
                            dve.tensor_copy(xm[:, t2, :, :], over_heads(ident[:, :], H))
                            dve.tensor_copy(xmt[:, t2, :, :], over_heads(ident[:, :], H)).then_inc(S["inv_start"], 1)
                elif name in ("solve_x", "solve_xt"):
                    tt, lv = args
                    item_written(dve, k)
                    m = (xm if name == "solve_x" else xmt)[:, tt, :, :]
                    if name == "solve_xt" and lv < LEVELS - 1:
                        item_read(dve, "solve_x", tt, lv)
                    tt_(m, m, oh, ALU.subtract).then_inc(free, 1)
                elif name == "ds":
                    c, = args
                    item_written(dve, k)
                    if c == 0:
                        dve.tensor_copy(st[:, :, :], oh).then_inc(free, 1)
                        item_read(dve, "ds", c)
                        dve.sem_inc(S["st_ready"], 1)
                    else:
                        item_written(dve, ITEM["o", (c,)])
                        chain(tt_(st[:, :, :], st[:, :, :], over_free(e_last[:, c, :], HD), ALU.mult))
                        tt_(st[:, :, :], st[:, :, :], oh, ALU.add).then_inc(free, 1)
                        item_read(dve, "ds", c)
                        dve.sem_inc(S["st_ready"], 1)
                elif name == "fbc":
                    kt, = args
                    item_written(dve, k)
                    if kt == 0:
                        tt_(mf0[:, :, :], over_free(fcum[:, 0, :], P), oh, ALU.subtract)
                        tt_(mf1[:, :, 0:P], over_free(fcum[:, 1, :], P), oh, ALU.subtract).then_inc(free, 1)
                    else:
                        tt_(mf1[:, :, P:SEQ], over_free(fcum[:, 1, :], P), oh, ALU.subtract).then_inc(free, 1)
                elif name in ("s0", "s1"):
                    hg, = args
                    b, p, mf, w = (0, p0, mf0, P) if name == "s0" else (1, p1, mf1, SEQ)
                    item_written(dve, k)
                    dve.wait_ge(S["mf_ready"], 2)
                    for q in range(4 * w // 512):
                        n = 512 // w
                        last = dve.scalar_tensor_tensor(
                            p[:, hg, n * q:n * q + n, :].rearrange("p h d -> p (h d)"), o[:, q, :], HD ** -0.5,
                            mf[:, 4 * hg + n * q:4 * hg + n * q + n, :].rearrange("p h d -> p (h d)"), ALU.mult, ALU.add)
                    last.then_inc(free, 1)
                    item_read(dve, name, hg)
                    dve.tensor_reduce(fmax[:, hg, b, :], p[:, hg, :, :], AX.X, ALU.max,
                                      negate=True).then_inc(S["smax_ready"], 1)
                    if b == 1:
                        dve.wait_ge(S["p_exp"], 2 * hg + 2)
                        chain(dve.reciprocal(fsum[:, hg, :, :], fsum[:, hg, :, :]))
                        tt_(p0[:, hg, :, :], p0[:, hg, :, :], over_free(fsum[:, hg, 0, :], P), ALU.mult)
                        tt_(p1[:, hg, :, :], p1[:, hg, :, :], over_free(fsum[:, hg, 1, :], SEQ), ALU.mult).then_inc(S["p_ready"], 1)
                elif name == "pv":
                    out_lo(k, args[0], y_fox, None, "foxhi_ready")
                elif name == "vbc":
                    tt, = args
                    dve.wait_ge(S["me_masked"], tt + 1)
                    chain(dve.tensor_reduce(dmax[:, tt, :], me[:, tt, :, :], AX.X, ALU.max))
                    chain(tt_(dmax[:, tt, :], dmax[:, tt, :], cum[:, tt, 1, :], ALU.add))
                    if tt == 1:
                        r, t0 = chunk_rows(0)
                        chain(dve.tensor_copy(inter[r, 0, :], cum[r, 0, 1, :]))
                        dve.memset(m_t[64:128, 0, :], 0.0)
                        chain(dve.memset(m_t[:, 1, :], 0.0))
                        tt_(m_t[r, 0, :], inter[r, 0, :], dmax[r, 0, :], ALU.max).then_inc(S["mrow_ready"], 1)
                elif name == "msel":
                    c, = args
                    r, t0 = chunk_rows(c)
                    item_written(dve, k)
                    tt_(inter[r, t0, :], cum[r, t0, 1, :], o[r, 0, 0:H], ALU.add).then_inc(free, 1)
                    item_read(dve, "msel", c)
                    tt_(m_t[r, t0, :], inter[r, t0, :], dmax[r, t0, :], ALU.max).then_inc(S["mrow_ready"], 1)
                    if c == NC - 1:
                        dve.wait_ge(S["mrow_ready"], NC)
                        tt_(bm[:, :, :], bc_, m_t[:, :, :], ALU.subtract)
                        tt_(w_int[:, :, :], inter[:, :, :], m_t[:, :, :], ALU.subtract).then_inc(S["mstat_in"], 1)
                        dve.wait_ge(S["mstat_exp"], 1)
                        dve.tensor_scalar(w_int8[:, :, :], w_int[:, :, :], L ** -0.5, None, ALU.mult).then_inc(S["mstat_ready"], 1)
                        for tt in range(NT):
                            item_read(dve, "vbc", tt)
                            on_diagonal(mr[:, tt, :, :], bm[:, tt, :]).then_inc(S["mr_ready"], 1)
                elif name == "mtail":
                    item_written(dve, k)
                    dve.tensor_copy(w_last[:, :, :, :].rearrange("p t b h -> p b t h"),
                                    o[:, 0, 16:48].rearrange("p (b t h) -> p b t h", b=2, t=2))
                    tt_(c_kw[:, :, :], vs[:, :, :], o[:, 0, 0:16].rearrange("p (t h) -> p t h", t=2),
                        ALU.add).then_inc(S["mtail_in"], 1)
                    dve.wait_ge(S["mtail_in"], 1)
                    dve.sem_inc(free, 1)
                    dve.wait_ge(S["mtail_exp"], 1)
                    item_read(dve, "mturn")
                    for tt in range(NT):
                        tt_(mkt[:, tt, :, :], mkt[:, tt, :, :], over_free(c_kw[:, tt, :], L), ALU.mult).then_inc(S["kw_ready"], 1)
                elif name == "mbc":
                    tt, = args
                    item_written(dve, k)
                    tt_(me[:, tt, :, :], oh, over_free(vs[:, tt, :], P), ALU.add).then_inc(free, 1)
                elif name == "mqk":
                    tt, = args
                    item_written(dve, k)
                    dve.wait_ge(S["mt_exp"], tt + 1)
                    for q in range(2):
                        def odd(t):
                            return t[:, tt, :, :].rearrange("p (j b) d -> p j b d", b=2)[:, :, q, :]
                        last = dve.scalar_tensor_tensor(
                            odd(smt), o[:, q, :].rearrange("p (j d) -> p j d", d=P), L ** -0.5, odd(me), ALU.mult, ALU.mult)
                    last.then_inc(free, 1)
                elif name == "qc":
                    c, = args
                    r, tt = chunk_rows(c)
                    item_written(dve, k)
                    tt_(mt1[r, :, :], oh[r], over_free(w_int8[r, tt, :], HD), ALU.mult).then_inc(free, 1)
                elif name == "dc":
                    c, = args
                    r, tt = chunk_rows(c)
                    item_written(dve, k)
                    dcs = o[:, 0, :].rearrange("p (j d) -> p j d", d=HD)
                    if c == 0:
                        chain(dve.tensor_copy(den[r, tt, :], o[r, 1, 8:16]))
                        dve.memset(n_st[:, :, :], 0.0)
                        chain(dve.memset(c_st[:, :, :, :], 0.0))
                        for b in range(2):
                            g = slice(L * b, L * b + L)
                            dve.tensor_copy(n_st[g, :, b], o[g, 1, 16:20])
                            ins = dve.tensor_copy(c_st[g, :, b, :], dcs[g])
                        chain(ins)
                    else:
                        item_read(dve, "qc", c)
                        chain(tt_(den[r, tt, :], o[r, 1, 0:8], w_int8[r, tt, :], ALU.mult))
                        chain(tt_(den[r, tt, :], den[r, tt, :], o[r, 1, 8:16], ALU.add))
                        for b in range(2):
                            g = slice(L * b, L * b + L)
                            wl = w_last[g, tt, c % 2, :].rearrange("p (j b) -> p j b", b=2)[:, :, b]
                            tt_(c_n[g, :, :], c_st[g, :, b, :], over_free(wl, HD), ALU.mult)
                            chain(tt_(n_st[g, :, b], n_st[g, :, b], wl, ALU.mult))
                        for b in range(2):
                            g = slice(L * b, L * b + L)
                            tt_(n_st[g, :, b], n_st[g, :, b], o[g, 1, 16:20], ALU.add)
                            ins = tt_(c_st[g, :, b, :], c_n[g, :, :], dcs[g], ALU.add)
                        chain(ins)
                    dve.sem_inc(S["mstate_ready"], 1)
                    chain(dve.scalar_tensor_tensor(den2[r, tt, :], den[r, tt, :], -1.0, den[r, tt, :], ALU.mult, ALU.max))
                    chain(tt_(den2[r, tt, :], den2[r, tt, :], e_m[r, tt, :], ALU.max))
                    dve.reciprocal(rd[r, tt, :], den2[r, tt, :]).then_inc(free, 1)
                elif name == "sv":
                    c, = args
                    r, tt = chunk_rows(c)
                    item_written(dve, k)
                    if c == 0:
                        dve.tensor_copy(mv[r, tt, :, :], oh[r]).then_inc(free, 1)
                    else:
                        tt_(mv[r, tt, :, :], mt1[r, :, :], oh[r], ALU.add).then_inc(free, 1)
                elif name == "gout":
                    out_lo(k, args[0], y_gdn, 80, "ghi_ready")
                elif name == "mout":
                    out_lo(k, args[0], y_ml, 81, "mhi_ready")

            def unit(u):
                kind, _, g = UNITS[u]
                b0, free = 2 * (u % 2), pair_free[u % 2]
                if kind == "small":
                    chunk_done(dve, 0)
                    dve.wait_ge(S["small_loaded"], 80)
                    tt_(pre5[:, :, :, :].rearrange("p t a h -> p t (a h)"), ps[:, 0:2, 0:40],
                        over_heads(bias5[:, :, :].rearrange("p a h -> p (a h)"), NT), ALU.add).then_inc(free, 1)
                    dve.wait_ge(free, 1)
                    for n, (a, sgn) in enumerate(((0, -1.0), (2, 1.0), (4, -1.0))):
                        last = dve.tensor_scalar(soft[:, :, n, :], pre5[:, :, a, :], sgn, None, ALU.mult)
                    chain(last)
                    sf = soft[:, :, :, :].rearrange("p t a h -> p (t a h)")
                    sn = soft_n[:, :, :, :].rearrange("p t a h -> p (t a h)")
                    dve.scalar_tensor_tensor(sn, sf, -1.0, sf, ALU.mult, ALU.min).then_inc(S["soft_in"], 1)
                    dve.wait_ge(S["soft_out"], 1)
                    chain(dve.scalar_tensor_tensor(sf, sf, 0.0, soft_e[:, :, :, :].rearrange("p t a h -> p (t a h)"),
                                                   ALU.max, ALU.add))
                    dve.wait_ge(S["neg_exp"], 1)
                    dve.tensor_scalar(lf[:, :, :], soft[:, :, 0, :], -1.0, None, ALU.mult)
                    dve.tensor_scalar(gl[:, :, 1, :], soft[:, :, 2, :], -1.0, None, ALU.mult)
                    chain(dve.tensor_scalar(neg_a[:, :], neg_a[:, :], -1.0, None, ALU.mult))
                    tt_(gl[:, :, 0, :], soft[:, :, 1, :], over_heads(neg_a[:, :], NT), ALU.mult).then_inc(S["gates_ready"], 1)
                    chain(dve.tensor_scalar(beta[:, :, :], beta[:, :, :], 1.0, None, ALU.add))
                    dve.reciprocal(beta[:, :, :], beta[:, :, :]).then_inc(S["gates_ready"], 1)
                    dve.memset(pre[:, :, 0:3], 0.0)
                elif kind == "gdn":
                    chunk_done(dve, CHUNKS.index((u, 3)))
                    if g:
                        dve.wait_ge(S["silu_ready"], g)
                    v = ps[:, b0:b0 + 2, :]
                    dve.tensor_copy(acc[:, :, :], v[:, :, SEQ:2 * SEQ]).then_inc(S["up_free"], 1)
                    dve.wait_ge(S["up_free"], g + 1)
                    tt_(pre[:, :, 3:3 + SEQ], v[:, :, 0:SEQ], acc[:, :, :], ALU.add).then_inc(free, 1)
                    dve.wait_ge(free, u // 2 + 1)
                    for b in range(2):
                        n = 2 * g + b
                        chain(dve.tensor_scalar(acc[:, b, :], pre[:, b, 3:3 + SEQ], conv_c[:, 3, n:n + 1], None, ALU.mult))
                        for j in range(3):
                            ins = dve.scalar_tensor_tensor(acc[:, b, :], pre[:, b, j:j + SEQ], conv_c[:, j, n:n + 1],
                                                           acc[:, b, :], ALU.mult, ALU.add)
                            if b == 1 and j == 2:
                                ins.then_inc(S["conv_ready"], 1)
                                dve.wait_ge(S["conv_ready"], g + 1)
                            else:
                                chain(ins)
                elif kind in ("foxqk", "mlqk"):
                    chunk_done(dve, CHUNKS.index((u, 3)))
                    n = 4 if kind == "foxqk" else 2
                    if kind == "mlqk" and g == 0:
                        item_read(dve, "turn", 11)
                    dst = ((fq, fk) if kind == "foxqk" else (mq, mk))[g // n][:, 2 * (g % n):2 * (g % n) + 2, :]
                    v = ps[:, b0:b0 + 2, :]
                    if kind == "mlqk" and g in (0, 2):
                        pass
                    chain(dve.tensor_copy(dst, v[:, :, SEQ:2 * SEQ]))
                    tt_(dst, v[:, :, 0:SEQ], dst, ALU.add).then_inc(free, 1)

            def gdn_output():
                for tt in range(NT):
                    dve.wait_ge(S["gsq_in"], tt + 1)
                    dve.tensor_reduce(ss[:, 2 + tt, :], osq[:, :, :], AX.X, ALU.add).then_inc(S["gsq_done"], 1)
                dve.wait_ge(S["gsq_done"], 2)
                chain(tt_(rstd[:, 2:4, :], ss[:, 2:4, :], rn[:, 0, :, :], ALU.mult))
                chain(tt_(rstd[:, 2:4, :], rstd[:, 2:4, :], rn[:, 0, :, :], ALU.mult))
                dve.tensor_scalar(rstd[:, 2:4, :], rstd[:, 2:4, :], 1.0 / HD, EPS, ALU.mult, ALU.add).then_inc(S["groot_in"], 1)
                dve.wait_ge(S["groot_done"], 1)
                chain(dve.reciprocal(rstd[:, 2:4, :], rstd[:, 2:4, :]))
                chain(tt_(rstd[:, 2:4, :], rstd[:, 2:4, :], rn[:, 0, :, :], ALU.mult))
                dve.wait_ge(pair_free[(len(UNITS) - 3) % 2], (len(UNITS) - 3) // 2 + 1)
                dve.wait_ge(pair_free[(len(UNITS) - 4) % 2], (len(UNITS) - 4) // 2 + 1)
                for tt in range(NT):
                    chain(tt_(gvt[:, tt, :, :], gvt[:, tt, :, :], over_free(rstd[:, 2 + tt, :], HD), ALU.mult))
                    tt_(gvt[:, tt, :, :], gvt[:, tt, :, :], z[:, tt, :, :], ALU.mult).then_inc(S["gy_ready"], 1)

            def ml_output():
                dve.wait_ge(pair_free[(len(UNITS) - 1) % 2], (len(UNITS) - 1) // 2 + 1)
                dve.wait_ge(pair_free[(len(UNITS) - 2) % 2], (len(UNITS) - 2) // 2 + 1)
                item_read(dve, "sv", NC - 1)
                dve.wait_ge(S["gsq_done"], 2)
                for tt in range(NT):
                    tt_(mv[:, tt, :, :], mv[:, tt, :, :], mo[:, tt, :, :], ALU.mult).then_inc(S["msq_in"], 1)
                    dve.wait_ge(S["msq_done"], tt + 1)
                    chain(dve.tensor_reduce(ss[:, 2 + tt, :], osq[:, :, :], AX.X, ALU.add))
                chain(tt_(rstd[:, 2:4, :], ss[:, 2:4, :], rd[:, :, :], ALU.mult))
                chain(tt_(rstd[:, 2:4, :], rstd[:, 2:4, :], rd[:, :, :], ALU.mult))
                dve.tensor_scalar(rstd[:, 2:4, :], rstd[:, 2:4, :], 1.0 / HD, EPS, ALU.mult, ALU.add).then_inc(S["mroot_in"], 1)
                dve.wait_ge(S["mroot_done"], 1)
                chain(dve.reciprocal(rstd[:, 2:4, :], rstd[:, 2:4, :]))
                chain(tt_(rstd[:, 2:4, :], rstd[:, 2:4, :], rd[:, :, :], ALU.mult))
                for tt in range(NT):
                    tt_(mv[:, tt, :, :], mv[:, tt, :, :], over_free(rstd[:, 2 + tt, :], HD), ALU.mult).then_inc(S["my_ready"], 1)

            for c in range(SLOTS):
                if not on_pool(c):
                    split_lo(dve, c)
            dve.wait_ge(S["rows_turned"], 1)
            dve.tensor_copy(cols[:, :], ps[:, 4, 0:82])
            dve.tensor_copy(conv_c[:, :, :].rearrange("p a b -> p (a b)"), ps[:, 4, P:P + 96])
            fcc = fconv_c[:, :, :].rearrange("p a b -> p (a b)")
            dve.tensor_copy(fcc[:, 0:256], ps[:, 4, 256:512])
            dve.tensor_copy(fcc[:, 256:264], ps[:, 5, 0:8]).then_inc(S["cols_ready"], 1)
            dve.wait_ge(S["sums_ready"], 1)
            chain(dve.reciprocal(rstd[:, 0, 0:2], rstd[:, 0, 0:2]))
            for tt in range(NT):
                dve.tensor_scalar(x_in[:, tt, :], x_in[:, tt, :], rstd[:, 0, tt:tt + 1], None,
                                  ALU.mult).then_inc(S["xs_ready"], 1)
            turn_x_lo(0, 0)

            k = 0
            for c, (u, t) in enumerate(CHUNKS):
                if not on_pool(c + SLOTS):
                    split_lo(dve, c + SLOTS)
                if t == UNIT_CHUNKS[UNITS[u][0]] - 1:
                    unit(u)
                while k < len(ITEMS) and ITEMS[k][0] == c:
                    if ITEMS[k][1:] == ("gout", (0,)):
                        gdn_output()
                    if ITEMS[k][1:] == ("mout", (0,)):
                        ml_output()
                    item(k)
                    if ITEMS[k][1] == "solve_xt" and ITEMS[k][2] == (1, LEVELS - 1):
                        for tt in range(NT):
                            tt_(kbg[:, tt, :, :], gkt[:, tt, :, :], over_free(c_w[:, tt, :], HD), ALU.mult).then_inc(S["kbg_ready"], 1)
                            tt_(gvt[:, tt, :, :], gvt[:, tt, :, :], over_free(beta[:, tt, :], HD), ALU.mult).then_inc(S["vb_ready"], 1)
                        for tt in range(NT):
                            dve.wait_ge(S["kbg_ready"], tt + 1)
                            tt_(gkt[:, tt, :, :], gkt[:, tt, :, :], over_free(c_k[:, tt, :], HD), ALU.mult).then_inc(S["kg_ready"], 1)
                    if ITEMS[k][1] == "o" and ITEMS[k][2] == (NC - 1,):
                        for tt in range(NT):
                            on_diagonal(fr[:, tt, :, :], fcum[:, tt, :]).then_inc(S["fr_ready"], 1)
                    if ITEMS[k][1] == "pv" and ITEMS[k][2] == (1,):
                        chain(tt_(vs[:, :, :], i_pre, bc_, ALU.subtract))
                        for tt in range(NT):
                            on_diagonal(mr[:, tt, :, :], vs[:, tt, :]).then_inc(S["mr_ready"], 1)
                    k += 1
            for p in range(2):
                dve.wait_ge(item_free[p], (len(ITEMS) + 1 - p) // 2)
            for p in range(2):
                dve.sem_inc(pair_read[p], 1)
            with dve.Fori(0, GROUPS // 2) as i:
                c = N1
                for q in range(6):
                    b0, j, br = 4 * (q % 2), q // 3, q % 3
                    for t in range(6):
                        if not on_pool(c + SLOTS):
                            split_lo(dve, c + SLOTS, i * 9)
                        if t == 3:
                            chunk_done(dve, c, i * 9)
                            dve.wait_ge(S["gate_sig"], i * 6 + q) if q else None
                            dve.tensor_copy(g_pr[:, :, :], ps[:, b0:b0 + 2, SEQ:2 * SEQ]).then_inc(S["gate_free2"], 1)
                            dve.wait_ge(S["gate_free2"], i * 6 + (q + 1))
                            tt_(g_sum[:, :, :], ps[:, b0:b0 + 2, 0:SEQ], g_pr[:, :, :], ALU.add).then_inc(S["gate_in"], 1)
                        if t == 5:
                            chunk_done(dve, c, i * 9)
                            dve.wait_ge(S["gate_in"], i * 6 + (q + 1))
                            dve.tensor_copy(g_pr[:, :, :], ps[:, b0 + 2:b0 + 4, SEQ:2 * SEQ]).then_inc(S["norm_out"], 1)
                            dve.wait_ge(S["norm_out"], i * 12 + (2 * q + 1))
                            tt_(g_pr[:, :, :], ps[:, b0 + 2:b0 + 4, 0:SEQ], g_pr[:, :, :], ALU.add).then_inc(pair_read[q % 2], 1)
                            dve.wait_ge(pair_read[q % 2], i * 3 + (q // 2 + 2))
                            dve.wait_ge(S["gate_sig"], i * 6 + (q + 1))
                            y = yT[:, bass.ds(i * 4 + 2 * j, 2), :]
                            if br == 0:
                                tt_(y, g_pr[:, :, :], g_sig[:, :, :], ALU.mult).then_inc(S["norm_out"], 1)
                                dve.wait_ge(S["norm_out"], i * 12 + (2 * q + 2))
                                dve.sem_inc(S["proj_free"], 1)
                            else:
                                tt_(g_y[:, :, :], g_pr[:, :, :], g_sig[:, :, :], ALU.mult).then_inc(S["norm_out"], 1)
                                dve.wait_ge(S["norm_out"], i * 12 + (2 * q + 2))
                                tt_(y, y, g_y[:, :, :], ALU.add).then_inc(S["proj_free"], 1)
                                dve.wait_ge(S["proj_free"], i * 6 + (q + 1))
                        c += 1

            def side_lo(n, it, kt_ap, slot):
                dve.wait_ge(S["side_hi"], n + 1 + it)
                tt_(side[:, slot, SEQ:2 * SEQ], kt_ap, side[:, slot, 0:SEQ], ALU.subtract).then_inc(S["side_ready"], 1)

            for kt in range(2):
                side_lo(kt, 0, yT[:, kt, :], kt)
            with dve.Fori(0, KT // 2 - 1) as i:
                for j in range(4):
                    if not on_pool(N2 + SLOTS + j):
                        split_lo(dve, N2 + SLOTS + j, i)
                    if j % 2:
                        side_lo(2 + j // 2, i * 2, yT[:, bass.ds(i * 2 + (2 + j // 2), 1), :].rearrange("p a b -> p (a b)"), j // 2)
            for j in range(4):
                if not on_pool(N3 + j):
                    split_lo(dve, N3 + j)

            def add_rows(c_last, n0):
                dve.wait_ge(S["x_again"], 16)
                for j in range(2):
                    chunk_done(dve, c_last - j)
                for tt in range(NT):
                    tt_(x1[:, tt, :], x1[:, tt, :], ps[:, 4 * tt:4 * tt + 4, :].rearrange("p a b -> p (a b)"),
                        ALU.add).then_inc(S["x1_ready"], 1)

            add_rows(N3 - 1, 0)
            dve.wait_ge(S["x1_ready"], 2)
            dve.sem_inc(S["bank_read"], 1)
            for tt in range(NT):
                dve.wait_ge(S["sums_ready"], 2 + tt)
                chain(dve.reciprocal(rstd[:, 1, tt:tt + 1], rstd[:, 1, tt:tt + 1]))
                dve.tensor_scalar(xs[:, tt, :], x1[:, tt, :], rstd[:, 1, tt:tt + 1], None, ALU.mult).then_inc(S["xs_ready"], 1)
            turn_x_lo(4, 16)
            for v in range(2):
                dve.wait_ge(S["xt_ready"], 8)
                dve.memset(upre[:, v, :, 0:2], 0.0).then_inc(up_read[v], 1)
            with dve.Fori(0, FF // 512) as i:
                for v in range(2):
                    for j in range(8):
                        c = N3 + 8 * v + j
                        if not on_pool(c + SLOTS):
                            split_lo(dve, c + SLOTS, i * 4)
                        if j % 4 == 3:
                            w = j // 4
                            b0 = 4 * v + 2 * w
                            chunk_done(dve, c, i * 4)
                            n = i * 24 + 12 * v + 6 * w
                            dve.tensor_copy(uacc[:, w, :, :], ps[:, b0:b0 + 2, SEQ:2 * SEQ]).then_inc(S["up_free"], 1)
                            dve.wait_ge(S["up_free"], i * 24 + (12 + 12 * v + 6 * w + 1))
                            if w == 0:
                                tt_(upre[:, w, :, 2:2 + SEQ], ps[:, b0:b0 + 2, 0:SEQ], uacc[:, w, :, :], ALU.add).then_inc(S["up_free"], 1)
                                dve.wait_ge(S["up_free"], i * 24 + (12 + 12 * v + 6 * w + 2))
                            else:
                                tt_(upre[:, w, :, 2:2 + SEQ], ps[:, b0:b0 + 2, 0:SEQ], uacc[:, w, :, :], ALU.add).then_inc(up_read[v], 1)
                                dve.wait_ge(up_read[v], i + 2)
                                dve.sem_inc(S["up_free"], 1)
                            for tap in (2, 1, 0):
                                for b in range(2):
                                    at = i * 4 + (tap * 2 * FKT + FKT * w + 2 * v + b)
                                    cw = fcc[:, bass.ds(at, 1)]
                                    src = upre[:, w, b, tap:tap + SEQ]
                                    if tap == 2:
                                        ins = dve.tensor_scalar(uacc[:, w, b, :], src, cw, None, ALU.mult)
                                    else:
                                        ins = dve.scalar_tensor_tensor(uacc[:, w, b, :], src, cw, uacc[:, w, b, :], ALU.mult, ALU.add)
                                if tap:
                                    ins.then_inc(S["up_free"], 1)
                                    dve.wait_ge(S["up_free"], i * 24 + (12 + 12 * v + 6 * w + 5 - tap))
                                elif w == 0:
                                    ins.then_inc(S["up_free"], 1)
                                    dve.wait_ge(S["up_free"], i * 24 + (12 + 12 * v + 6 * w + 5))
                                else:
                                    ins.then_inc(S["up_acc"], 1)
                            if w == 0:
                                dve.sem_inc(S["up_free"], 1)
                            else:
                                dve.wait_ge(S["up_silu"], i * 2 + (v + 1))
                                tt_(hT[:, bass.ds(i * 4 + 2 * v, 2), :], uacc[:, 0, :, :], usil[:, :, :], ALU.mult).then_inc(S["up_free"], 1)
                                dve.wait_ge(S["up_free"], i * 24 + (12 + 12 * v + 6 * w + 5))
                                dve.sem_inc(S["up_free"], 1)
            for kt in range(2):
                side_lo(KT + kt, 0, hT[:, kt, :], kt)
            with dve.Fori(0, FKT // 2 - 1) as i:
                for j in range(4):
                    if not on_pool(N4 + SLOTS + j):
                        split_lo(dve, N4 + SLOTS + j, i)
                    if j % 2:
                        side_lo(KT + 2 + j // 2, i * 2, hT[:, bass.ds(i * 2 + (2 + j // 2), 1), :].rearrange("p a b -> p (a b)"), j // 2)
            add_rows(N5 - 1, 2)
            dve.wait_ge(S["gfin_loaded"], 16)
            for tt in range(NT):
                dve.wait_ge(S["fin_root"], tt + 1)
                chain(dve.reciprocal(rstd[:, 0, 2 + tt:3 + tt], rstd[:, 0, 2 + tt:3 + tt]))
                dve.scalar_tensor_tensor(x1[:, tt, :], x1[:, tt, :], rstd[:, 0, 2 + tt:3 + tt], gfin[:, :],
                                         ALU.mult, ALU.mult).then_inc(S["fin_ready"], 1)

        @block.gpsimd
        def _(pool):
            order = [0]

            def chain(ins):
                order[0] += 1
                ins.then_inc(S["pool_chain"], 1)
                pool.wait_ge(S["pool_chain"], order[0])

            def keep(t, cmp, base, pattern, chan, fill=0.0):
                chain(pool.affine_select(out=t, in_=t, compare_op=cmp, fill=fill, base=base, pattern=pattern,
                                         channel_multiplier=chan))

            pool.memset(eps_c[:, 0:1], EPS)
            pool.memset(eps_c[:, 1:2], 1.0)
            chain(pool.memset(bias5[:, :, :], 0.0))
            chain(pool.memset(ident[:, :], 0.0))
            pool.memset(tiny[:, :, :], 0.0).then_inc(S["consts"], 1)
            keep(ident[:, :], ALU.not_equal, 0, [[-1, P]], 1, fill=1.0)
            pool.memset(ones[:, :], 1.0).then_inc(S["consts"], 1)
            split_lo(pool, SLOTS - 1)
            chain(pool.memset(upto[:, :], 1.0))
            keep(upto[:, :], ALU.is_ge, 0, [[1, P]], -1)
            two = [[-L, 2], [0, L]]
            for t in (same_c, upto_c, last_c):
                chain(pool.memset(t[:, :], 1.0))
                v = t[:, :].rearrange("p (c r) -> p c r", c=2)
                if t is last_c:
                    keep(v, ALU.is_equal, -(L - 1), two, 1)
                else:
                    keep(v, ALU.is_ge, 0, two, 1)
                    keep(v, ALU.is_ge, L - 1, [[L, 2], [0, L]], -1)
            keep(upto_c[:, :], ALU.is_ge, 0, [[1, P]], -1)
            for b in range(2):
                chain(pool.memset(sel[:, b, :], 1.0))
                keep(sel[:, b, :], ALU.is_equal, -(L * b + L - 1), [[0, P]], 1)
            for lv in range(LEVELS):
                b = 1 << lv
                n = P // (2 * b)
                chain(pool.memset(level[:, lv, :], 1.0))
                v = level[:, lv, :].rearrange("p (n w) -> p n w", w=2 * b)
                keep(v, ALU.is_ge, 0, [[-2 * b, n], [0, 2 * b]], 1)
                keep(v, ALU.is_ge, b - 1, [[2 * b, n], [0, 2 * b]], -1)
                keep(v, ALU.is_ge, -b, [[0, n], [1, 2 * b]], 0)
            chain(pool.memset(tiny[:, 1, :], 0.0))
            pool.memset(tiny[:, 1, :], 0.0).then_inc(S["consts"], 1)

            def masked(lv, tt):
                pool.tensor_tensor(nlv[:, tt, :, :], nt_[:, tt, :, :], over_heads(level[:, lv, :], H),
                                   ALU.mult).then_inc(S["level_ready"], 1)

            def item(k):
                _, name, args = ITEMS[k]
                if name == "norm" and args == (1,):
                    pass
                elif name == "gam":
                    tt, = args
                    pool.wait_ge(S["gam_raw"], tt + 1)
                    e = ed[:, tt, :, :]
                    pool.affine_select(out=e, in_=e, compare_op=ALU.is_ge, fill=NEG, base=0,
                                       pattern=[[0, H], [1, P]], channel_multiplier=-1).then_inc(S["e_masked"], 1)
                    pool.wait_ge(S["e_masked"], 2 * tt + 1)
                    pool.memset(ed[0:L, tt, :, L:P], NEG).then_inc(S["e_masked"], 1)
                    pool.wait_ge(S["e_masked"], 2 * tt + 2)
                elif name == "qk":
                    tt, = args
                    item_read(pool, "kk", tt)
                    n = nt_[:, tt, :, :]
                    chain(pool.affine_select(out=n, in_=n, compare_op=ALU.is_ge, fill=0.0, base=-1,
                                             pattern=[[0, H], [1, P]], channel_multiplier=-1))
                    item_read(pool, "qk", tt)
                    if tt == 1:
                        for t2 in range(NT):
                            masked(0, t2)
                elif name == "solve_p":
                    tt, lv = args
                    if lv < LEVELS - 1:
                        item_written(pool, k)
                        masked(lv + 1, tt)
                elif name == "fbc" and args == (1,):
                    for kt in range(NT):
                        item_read(pool, "fbc", kt)
                    m = mf0[:, :, :]
                    pool.affine_select(out=m, in_=m, compare_op=ALU.is_ge, fill=NEG, base=0,
                                       pattern=[[0, H], [-1, P]], channel_multiplier=1).then_inc(S["mf_ready"], 1)
                    m = mf1[:, :, P:SEQ]
                    pool.affine_select(out=m, in_=m, compare_op=ALU.is_ge, fill=NEG, base=0,
                                       pattern=[[0, H], [-1, P]], channel_multiplier=1).then_inc(S["mf_ready"], 1)
                elif name == "vbc":
                    tt, = args
                    item_read(pool, "vbc", tt)
                    e = me[:, tt, :, :]
                    chain(pool.affine_select(out=e, in_=e, compare_op=ALU.is_ge, fill=NEG, base=0,
                                             pattern=[[0, H], [-1, P]], channel_multiplier=1))
                    pool.memset(me[L:P, tt, :, 0:L], NEG).then_inc(S["me_masked"], 1)
                    pool.wait_ge(S["me_masked"], tt + 1)
                elif name == "mbc":
                    tt, = args
                    item_read(pool, "mbc", tt)
                    e = me[:, tt, :, :]
                    chain(pool.affine_select(out=e, in_=e, compare_op=ALU.is_ge, fill=NEG, base=0,
                                             pattern=[[0, H], [1, P]], channel_multiplier=-1))
                    pool.memset(me[0:L, tt, :, L:P], NEG).then_inc(S["mt_masked"], 1)
                    pool.wait_ge(S["mt_masked"], tt + 1)

            k = 0
            for c in range(N1):
                if on_pool(c + SLOTS):
                    split_lo(pool, c + SLOTS)
                while k < len(ITEMS) and ITEMS[k][0] == c:
                    item(k)
                    k += 1
            for first, rounds, per in ((N1, GROUPS // 2, 36), (N2, KT // 2 - 1, 4), (N3 - 4, 1, 4),
                                       (N3, FF // 512, 16), (N4, FKT // 2 - 1, 4)):
                todo = [first + j + SLOTS for j in range(per) if on_pool(first + j + SLOTS)]
                if rounds == 1:
                    for c in todo:
                        split_lo(pool, c)
                else:
                    with pool.Fori(0, rounds) as i:
                        for c in todo:
                            split_lo(pool, c, i * (per // SLOTS))


_INS = ['x', 'norm_mix_g', 'w_in', 'fox_f_bias', 'gdn_conv_w', 'gdn_a_log', 'gdn_dt_bias', 'gdn_norm_g',
        'ml_i_bias', 'ml_f_bias', 'ml_norm_g', 'gate_bias', 'w_fox_proj', 'w_gdn_proj', 'w_ml_proj',
        'w_out', 'norm_ffn_g', 'w_up', 'ffn_conv_w', 'w_down', 'norm_final_g']
_OUTS = [((1, SEQ, D), 'float32')]


def kernel(**inputs):
    import numpy as _np
    import concourse.bacc as _bacc
    from concourse import mybir as _mybir
    from concourse.bass_utils import run_bass_kernel_spmd as _run

    nc = _bacc.Bacc("TRN2", target_bir_lowering=False, num_devices=1)
    arrays, args = {}, []
    for name in _INS:
        a = _np.ascontiguousarray(inputs[name])
        arrays[f"in_{name}_dram"] = a
        args.append(nc.dram_tensor(f"in_{name}_dram", a.shape, _mybir.dt.from_np(a.dtype), kind="ExternalInput").ap())
    for i, (shape, dtype) in enumerate(_OUTS):
        dt = _mybir.dt.from_np(_np.dtype(dtype))
        args.append(nc.dram_tensor(f"out_{i}_dram", shape, dt, kind="ExternalOutput").ap())
    hybrid_layer_kernel(nc, *args)
    r = _run(nc, [arrays], core_ids=[0])
    return r.results[0]["out_0_dram"]
```

```python
from contextlib import ExitStack

import concourse.bass as bass
from concourse import mybir

ALU = mybir.AluOpType
ACT = mybir.ActivationFunctionType
AX = mybir.AxisListType
F32 = mybir.dt.float32
F32R = mybir.dt.float32r

P = 128
SEQ = 256
D = 2048
KT = D // P
NT = SEQ // P
H = 8
HD = 128
L = 64
NC = SEQ // L
FF = 5632
FKT = FF // P
GROUPS = D // 256
EPS = 1e-6
NEG = -1e30

FOX_Q, FOX_K, FOX_V, FOX_F = 0, 1024, 2048, 3072
GDN_QKV, GDN_Z, GDN_B = 3080, 6152, 7176
ML_Q, ML_V, ML_I, ML_O, GATE = 7192, 8216, 9240, 9256, 10280

SLOTS = 4
CHUNK = 1024
UNIT = 4096

UNITS = [("small", 0, 0)]
UNITS += [("gdn", GDN_QKV + 256 * g, g) for g in range(12)]
UNITS += [("foxqk", FOX_Q + 256 * g, g) for g in range(8)]
UNITS += [("foxv", FOX_V + 512 * g, g) for g in range(2)]
UNITS += [("mlqk", ML_Q + 256 * g, g) for g in range(4)]
UNITS += [("mlv", ML_V + 512 * g, g) for g in range(2)]
UNITS += [("z", GDN_Z + 512 * g, g) for g in range(2)]
UNITS += [("mlo", ML_O + 512 * g, g) for g in range(2)]
for _g in range(GROUPS):
    UNITS += [("gate", GATE + 256 * _g, _g), ("proj", 256 * _g, _g)]
UNIT_CHUNKS = {"small": 1, "gdn": 4, "foxqk": 4, "mlqk": 4, "foxv": 8, "mlv": 8, "z": 8, "mlo": 8, "gate": 4, "proj": 2}
CHUNKS = [(u, t) for u, (kind, _, _) in enumerate(UNITS) for t in range(UNIT_CHUNKS[kind])]
N1 = len(CHUNKS)


def last_chunk(kind, g):
    return max(c for c, (u, _) in enumerate(CHUNKS) if UNITS[u][0] == kind and UNITS[u][2] == g)


N2 = N1 + 12 * GROUPS
N3 = N2 + 2 * KT
N4 = N3 + 8 * (FF // 256)
N5 = N4 + 2 * FKT

LEVELS = 6


def plan_items():
    out = [(5, "cumsum", ())]
    for g in range(4, 12):
        out.append((last_chunk("gdn", g) + 3, "turn", (g,)))
    out.append((last_chunk("gdn", 3) + 5, "norm", (0,)))
    out.append((last_chunk("gdn", 7) + 5, "norm", (1,)))
    at = last_chunk("gdn", 11) + 5
    for tt in range(NT):
        out += [(at, "gam", (tt,)), (at + 2, "kk", (tt,)), (at + 3, "qk", (tt,))]
        at += 4
    for lv in range(LEVELS):
        row = [("solve_p", 0), ("solve_p", 1)]
        row += [("solve_x", 0)] * (lv < LEVELS - 1) + [("solve_xt", 0)]
        row += [("solve_x", 1)] * (lv < LEVELS - 1) + [("solve_xt", 1)]
        for name, tt in row:
            out.append((at, name, (tt, lv)))
            at += 1
    out += [(at, "wt", (0,)), (at + 1, "wt", (1,))]
    at += 3
    for c in range(NC):
        out += [(at, "vnew", (c,))]
        if c < NC - 1:
            out += [(at + 2, "ds", (c,))]
        out += [(at + 3, "o", (c,))]
        at += 4
    at = max(at, last_chunk("foxv", 1) + 2)
    for kt in range(NT):
        out.append((at + 2 * kt, "fbc", (kt,)))
    at += 5
    for hg in range(2):
        out += [(at, "s0", (hg,)), (at + 1, "s1", (hg,))]
        at += 2
    for hg in range(2):
        out += [(at + 1, "p0", (hg,)), (at + 2, "p1", (hg,))]
        at += 3
    for hg in range(2):
        out.append((at + 2 + hg, "pv", (hg,)))
    at += 4
    out.append((last_chunk("mlqk", 3) + 4, "mturn", ()))
    at = max(at, last_chunk("mlv", 1) + 1)
    for tt in range(NT):
        out.append((at, "vbc", (tt,)))
        at += 2
    at += 2
    for c in range(1, NC):
        out.append((at, "msel", (c,)))
        at += 1
    out.append((at + 1, "mtail", ()))
    at += 2
    for tt in range(NT):
        out += [(at, "mbc", (tt,)), (at + 2, "mqk", (tt,))]
        at += 2
    at += 1
    for c in range(NC):
        if c:
            out.append((at, "qc", (c,)))
        out += [(at, "dc", (c,)), (at + 2, "sv", (c,))]
        at += 5
    gy = last_chunk("z", 1) + 5
    out += [(gy, "gout", (0,)), (gy + 1, "gout", (1,))]
    my = max(at, last_chunk("mlo", 1) + 1)
    out += [(my + 13, "mout", (0,)), (my + 14, "mout", (1,))]
    steps = [(gy - 7 + n, "gdn_out", n) for n in range(7)] + [(my + 2 * n, "ml_out", n) for n in range(6)]
    order = sorted(range(len(out)), key=lambda k: (min(out[k][0], N1 - 1), out[k][0], k))
    return [(min(out[k][0], N1 - 1), out[k][1], out[k][2]) for k in order], steps


ITEMS, STEPS = plan_items()
ITEM = {(name, args): k for k, (_, name, args) in enumerate(ITEMS)}


def hybrid_layer_kernel(nc, x, norm_mix_g, w_in, fox_f_bias, gdn_conv_w, gdn_a_log, gdn_dt_bias, gdn_norm_g,
                        ml_i_bias, ml_f_bias, ml_norm_g, gate_bias, w_fox_proj, w_gdn_proj, w_ml_proj,
                        w_out, norm_ffn_g, w_up, ffn_conv_w, w_down, norm_final_g, out):
    ctx = ExitStack()
    with ctx:
        cursor = [nc.sbuf_base + (-nc.sbuf_base) % 64]

        def small(name, shape, dt=F32):
            n = 4
            for s in shape[1:]:
                n *= s
            at = cursor[0]
            cursor[0] += n + (-n) % 32
            return nc.alloc_sbuf_tensor_at(name, shape, dt, offset=at)

        raw = small("raw", [P, SLOTS, CHUNK])
        w_hi = small("w_hi", [P, SLOTS, CHUNK], F32R)
        w_lo = small("w_lo", [P, SLOTS, CHUNK], F32R)
        xnT = small("xnT", [P, KT, 2 * SEQ], F32R)
        ident = small("ident", [P, P])
        ones = small("ones", [P, P])
        upto = small("upto", [P, P])
        upto_c = small("upto_c", [P, P])
        same_c = small("same_c", [P, P])
        last_c = small("last_c", [P, P])
        sel = small("sel", [P, 2, P])
        level = small("level", [P, LEVELS, P])
        cols = small("cols", [P, 82])
        conv_c = small("conv_c", [P, 4, 24])
        fconv_c = small("fconv_c", [P, 3, 2 * FKT])
        bias5 = small("bias5", [P, 5, H])
        alog = small("alog", [P, H])
        pre5 = small("pre5", [P, NT, 5, H])
        soft = small("soft", [P, NT, 3, H])
        soft_n = small("soft_n", [P, NT, 3, H])
        soft_e = small("soft_e", [P, NT, 3, H])
        neg_a = small("neg_a", [P, H])
        lf = small("lf", [P, NT, H])
        gl = small("gl", [P, NT, 2, H])
        cum = small("cum", [P, NT, 2, H])
        tot = small("tot", [P, NT, 2, H])
        fcum = small("fcum", [P, NT, H])
        beta = small("beta", [P, NT, H])
        rn = small("rn", [P, 2, NT, H])
        eg = small("eg", [P, NT, H])
        c_m = small("c_m", [P, NT, H])
        c_w = small("c_w", [P, NT, H])
        c_k = small("c_k", [P, NT, H])
        e_last = small("e_last", [P, NC, H])
        tiny = small("tiny", [P, NT, H])
        vs = small("vs", [P, NT, H])
        dmax = small("dmax", [P, NT, H])
        inter = small("inter", [P, NT, H])
        m_t = small("m_t", [P, NT, H])
        w_int = small("w_int", [P, NT, H])
        w_int8 = small("w_int8", [P, NT, H])
        e_m = small("e_m", [P, NT, H])
        bm = small("bm", [P, NT, H])
        c_kw = small("c_kw", [P, NT, H])
        w_last = small("w_last", [P, NT, 2, H])
        n_st = small("n_st", [P, H // 2, 2])
        den = small("den", [P, NT, H])
        den2 = small("den2", [P, NT, H])
        rd = small("rd", [P, NT, H])
        fmax = small("fmax", [P, 2, 2, 4])
        fsum = small("fsum", [P, 2, 2, 4])
        ss = small("ss", [P, 4, H])
        rstd = small("rstd", [P, 4, H])
        eps_c = small("eps_c", [P, 2])
        spare = small("spare", [P, 2])
        norm_b = small("norm_b", [P, 2, NT])
        arena = cursor[0] + (-cursor[0]) % 32

        def part(name, unit, shape, dt=F32, skip=0):
            n = 4
            for s in shape[1:]:
                n *= s
            assert arena + unit * UNIT + skip + n <= nc.sbuf_usable_end, (name, arena, nc.sbuf_usable_end)
            return nc.alloc_sbuf_tensor_at(name, shape, dt, offset=arena + unit * UNIT + skip)

        rows = part("rows", 0, [P, 5, P])
        x_in = part("x_in", 20, [P, NT, D])
        x_sq = part("x_sq", 14, [P, D])
        gq = part("gq", 0, [P, H, SEQ])
        gk = part("gk", 2, [P, H, SEQ])
        gkt = part("gkt", 4, [P, NT, H, HD])
        gvt = part("gvt", 6, [P, NT, H, HD])
        aqk = part("aqk", 8, [P, NT, H, P])
        nt_ = part("nt", 10, [P, NT, H, P])
        xm = part("xm", 12, [P, NT, H, P])
        xmt = part("xmt", 14, [P, NT, H, P])
        pm_ = part("pm", 16, [P, NT, H, P])
        wt = part("wt", 16, [P, NT, H, P])
        ed = part("ed", 18, [P, NT, H, P])
        sq = part("sq", 18, [P, H, SEQ])
        nlv = part("nlv", 18, [P, NT, H, P])
        st = part("st", 2, [P, H, HD])
        vn = part("vn", 3, [P, H, HD])
        kbg = part("kbg", 12, [P, NT, H, HD])
        pre = part("pre", 26, [P, 2, SEQ + 4])
        acc = part("acc", 26, [P, 2, SEQ], skip=2080)
        vT = part("vT", 27, [P, 2, SEQ], skip=32)
        fq = part("fq", 20, [P, H, SEQ])
        fk = part("fk", 22, [P, H, SEQ])
        fv = part("fv", 24, [P, NT, H, HD])
        mf0 = part("mf0", 0, [P, H, P])
        mf1 = part("mf1", 1, [P, H, SEQ])
        fr = part("fr", 14, [P, NT, H, P])
        p0 = part("p0", 3, [P, 2, 4, P])
        p1 = part("p1", 4, [P, 2, 4, SEQ])
        pt0 = part("pt0", 0, [P, 4, 2, SEQ])
        pt1 = part("pt1", 2, [P, 2, 4, P])
        feat = part("feat", 27, [P, SEQ], skip=32)
        mq = part("mq", 26, [P, H // 2, SEQ])
        mk = part("mk", 27, [P, H // 2, SEQ])
        mkt = part("mkt", 8, [P, NT, H, L])
        mv = part("mv", 9, [P, NT, H, HD])
        mr = part("mr", 0, [P, NT, H, P])
        me = part("me", 2, [P, NT, H, P])
        smt = part("smt", 4, [P, NT, H, P])
        c_st = part("c_st", 0, [P, H // 2, 2, HD])
        c_n = part("c_n", 2, [P, H // 2, HD])
        mt1 = part("mt1", 1, [P, H, HD])
        z = part("z", 20, [P, NT, H, HD])
        mo = part("mo", 6, [P, NT, H, HD])
        osq = part("osq", 11, [P, H, HD])
        y_gdn = part("y_gdn", 12, [P, H, 2 * SEQ], F32R)
        y_fox = part("y_fox", 16, [P, H, 2 * SEQ], F32R)
        y_ml = part("y_ml", 0, [P, H, 2 * SEQ], F32R)
        yT = part("yT", 20, [P, KT, SEQ])
        g_sum = part("g_sum", 24, [P, 2, SEQ])
        g_sig = part("g_sig", 24, [P, 2, SEQ], skip=2048)
        g_pr = part("g_pr", 25, [P, 2, SEQ])
        g_y = part("g_y", 25, [P, 2, SEQ], skip=2048)
        side = part("side", 26, [P, 2, 2 * SEQ], F32R)
        x1 = part("x1", 4, [P, NT, D])
        hT = part("hT", 8, [P, FKT, SEQ])
        upre = part("upre", 0, [P, 2, 2, SEQ + 2])
        uacc = part("uacc", 2, [P, 2, 2, SEQ])
        usil = part("usil", 3, [P, 2, SEQ])
        junk = part("junk", 0, [P, D])
        xs = part("xs", 20, [P, NT, D])
        gffn = part("gffn", 16, [P, D])
        gfin = part("gfin", 24, [P, D])
        ps = ctx.enter_context(nc.psum_tensor("ps", [P, 8, 512], F32))

        def sem(name):
            return ctx.enter_context(nc.semaphore(name))

        def per_slot(name):
            return [sem(f"{name}{s}") for s in range(SLOTS)]

        raw_loaded, hi_ready, lo_ready, chunk_used = (
            per_slot(n) for n in ("raw_loaded", "hi_ready", "lo_ready", "chunk_used"))
        pair_free = [sem(f"pair_free{p}") for p in range(2)]
        item_done = [sem(f"item_done{p}") for p in range(2)]
        item_free = [sem(f"item_free{p}") for p in range(2)]
        names = """rows_loaded small_loaded x_again gffn_loaded gfin_loaded stored consts rows_turned cols_ready
            sums_ready rstd_ready xs_ready xt_written xt_hi xt_ready
            dve_chain act_chain pool_chain feat_ready feat_turned soft_in soft_exp soft_out beta_exp neg_exp gates_ready
            conv_ready silu_ready sq_ready norm_in norm_root norm_out
            gr_ready gam_raw eg_ready e_masked e_exp dk_ready nt_raw nt_strict level_ready inv_start kbg_ready
            egq_raw qg_ready coef_in coef_exp coef_ready vb_ready kg_ready st_ready
            fr_ready mf_raw mf_ready smax_ready p_exp p_ready foxhi_ready
            mr_ready me_copied me_masked mrow_ready mstat_in mstat_exp mstat_ready mtail_in mtail_exp kw_ready
            mt_raw mt_masked mt_exp mstate_ready
            gsq_in gsq_done groot_in groot_done gy_ready ghi_ready msq_in msq_done mroot_in mroot_done my_ready
            mhi_ready
            gate_in gate_sig y_ready side_hi side_ready side_used
            quarter_done x1_ready xs_pool gate_pre up_tap gate_conv u_conv up_silu h_ready
            """.split()
        S = {n: sem(n) for n in names}
        x_loaded = [sem(f"x_loaded{tt}") for tt in range(NT)]
        pair_read = [sem(f"pair_read{p}") for p in range(2)]
        up_read = [sem(f"up_read{p}") for p in range(2)]

        block = ctx.enter_context(nc.Block())

        def load(sp, c, it, dst, src):
            s = c % SLOTS
            if c >= SLOTS:
                sp.wait_ge(lo_ready[s], c // SLOTS + it)
            sp.dma_start(dst, src).then_inc(raw_loaded[s], 16)

        def split_hi(act, c, it=0):
            s, n = c % SLOTS, (640 if c == 0 else CHUNK)
            act.wait_ge(raw_loaded[s], 16 * (c // SLOTS + 1) + (32 if s == 0 else 0) + 16 * it)
            if c >= SLOTS:
                act.wait_ge(chunk_used[s], c // SLOTS + it)
            act.activation(w_hi[:, s, 0:n], raw[:, s, 0:n], ACT.Copy).then_inc(hi_ready[s], 1)

        def split_lo(eng, c, it=0):
            s, n = c % SLOTS, (640 if c == 0 else CHUNK)
            eng.wait_ge(hi_ready[s], c // SLOTS + 1 + it)
            eng.tensor_tensor(w_lo[:, s, 0:n], raw[:, s, 0:n], w_hi[:, s, 0:n],
                              ALU.subtract).then_inc(lo_ready[s], 1)

        def on_pool(c):
            return c % SLOTS == SLOTS - 1

        def chunk_done(eng, c, it=0):
            eng.wait_ge(chunk_used[c % SLOTS], c // SLOTS + 1 + it)

        def item_written(eng, k):
            eng.wait_ge(item_done[k % 2], k // 2 + 1)

        def item_read(eng, name, *args):
            k = ITEM[name, args]
            eng.wait_ge(item_free[k % 2], k // 2 + 1)

        def units_read(eng, kind):
            for u, unit_ in enumerate(UNITS):
                if unit_[0] == kind:
                    eng.wait_ge(pair_free[u % 2], u // 2 + 1)

        def pair(k):
            b = 4 + 2 * (k % 2)
            return ps[:, b:b + 2, :]

        def quarter_written(eng, p, c0, tt, half):
            if tt == 0:
                eng.wait_ge(S["quarter_done"], 2 * p + half + 1)
            else:
                chunk_done(eng, c0 + 2 + half)

        TURNS = ((0, 0), (0, 1), (1, 0), (1, 1), (0, 2), (1, 2), (0, 3), (1, 3))

        def turned(tt, n, lo=0):
            return (xnT[:, 4 * n:4 * n + 4, lo + tt * P:lo + tt * P + P],
                    ps[:, 4 * tt + n, :].rearrange("p (k d) -> p k d", d=P))

        def heads(ap):
            return ap.rearrange("p a (h d) -> p (a h) d", d=P)

        def over_free(ap, n):
            return ap.unsqueeze(2).to_broadcast([ap.shape[0], ap.shape[1], n])

        def over_heads(ap, n):
            return ap.unsqueeze(1).to_broadcast([ap.shape[0], n, ap.shape[1]])

        def chunk_rows(c):
            return slice(L * (c % 2), L * (c % 2) + L), c // 2

        gam, bc_ = cum[:, :, 0, :], cum[:, :, 1, :]
        i_pre = pre5[:, :, 3, :]

        @block.sync
        def _(sp):
            xf = x.rearrange("b (t p) d -> p (b t) d", p=P)
            for tt in range(NT):
                sp.dma_start(x_in[:, tt, :], xf[:, tt, :]).then_inc(x_loaded[tt], 16)
            sp.dma_start(rows[0:16, 0, :], norm_mix_g.rearrange("a (t p) -> (a t) p", p=P)).then_inc(S["rows_loaded"], 16)
            sp.dma_start(rows[16:32, 0, :], norm_ffn_g.rearrange("a (t p) -> (a t) p", p=P)).then_inc(S["rows_loaded"], 16)
            sp.dma_start(rows[32:80, 0, :], gate_bias.rearrange("a (t p) -> (a t) p", p=P)).then_inc(S["rows_loaded"], 16)
            sp.dma_start(rows[80:81, 0, :], gdn_norm_g).then_inc(S["rows_loaded"], 16)
            sp.dma_start(rows[81:82, 0, :], ml_norm_g).then_inc(S["rows_loaded"], 16)
            sp.dma_start(rows[0:96, 1, :], gdn_conv_w.rearrange("a j (t p) -> (a j t) p", p=P)).then_inc(S["rows_loaded"], 16)
            fc = ffn_conv_w.rearrange("a j (t p) -> (a j t) p", p=P)
            for n in range(3):
                m = min(P, 264 - P * n)
                sp.dma_start(rows[0:m, 2 + n, :], fc[P * n:P * n + m, :]).then_inc(S["rows_loaded"], 16)
            w = w_in.rearrange("a (t p) n -> p (a t) n", p=P)
            w_br = [m.rearrange("a (t p) n -> p (a t) n", p=P) for m in (w_fox_proj, w_gdn_proj, w_ml_proj)]
            r0 = raw[:, 0, 0:640].rearrange("p (t n) -> p t n", n=40)
            for col, n, dst in ((FOX_F, 8, 0), (GDN_B, 16, 8), (ML_I, 16, 24)):
                sp.dma_start(r0[:, :, dst:dst + n], w[:, :, col:col + n]).then_inc(raw_loaded[0], 16)

            def bias(dst, src):
                sp.dma_start(dst, src.partition_broadcast(P) if src.ndim == 1 else
                             src[0, :].partition_broadcast(P)).then_inc(S["small_loaded"], 16)

            sp.wait_ge(S["consts"], 1)
            bias(bias5[:, 0, :], fox_f_bias)
            bias(bias5[:, 2, :], gdn_dt_bias)
            bias(bias5[:, 3, :], ml_i_bias)
            bias(bias5[:, 4, :], ml_f_bias)
            bias(alog[:, :], gdn_a_log)

            for c in range(1, N1):
                u, t = CHUNKS[c]
                kind, col, _ = UNITS[u]
                if UNIT_CHUNKS[kind] <= 4:
                    src, n = (w_br[0] if kind == "proj" else w)[:, 4 * t:4 * t + 4, col:col + 256], 256
                else:
                    src, n = w[:, 2 * t:2 * t + 2, col:col + 512], 512
                load(sp, c, 0, raw[:, c % SLOTS, :].rearrange("p (t n) -> p t n", n=n), src)
            with sp.Fori(1, GROUPS // 2 + 1) as i:
                c = N1
                for j in range(2):
                    for b in range(1, 3):
                        for t in range(4):
                            load(sp, c, i * 6 - 6, raw[:, c % SLOTS, :].rearrange("p (t n) -> p t n", n=256),
                                 w[:, 4 * t:4 * t + 4, bass.ds(i * 512 + (GATE + b * D + j * 256 - 512), 256)])
                            c += 1
                        for t in range(2):
                            load(sp, c, i * 6 - 6, raw[:, c % SLOTS, :].rearrange("p (t n) -> p t n", n=256),
                                 w_br[b][:, 4 * t:4 * t + 4, bass.ds(i * 512 + (j * 256 - 512), 256)])
                            c += 1
            sp.wait_ge(item_free[0], (len(ITEMS) + 1) // 2)
            sp.wait_ge(item_free[1], len(ITEMS) // 2)
            sp.dma_start(x1[:, :, :], xf).then_inc(S["x_again"], 16)
            sp.dma_start(gffn[:, :], norm_ffn_g[0, :].partition_broadcast(P)).then_inc(S["gffn_loaded"], 16)
            wo = w_out.rearrange("a k n -> (a k) n")
            with sp.Fori(1, KT // 2 + 1) as i:
                for j in range(4):
                    load(sp, N2 + j, i - 1, raw[:, (N2 + j) % SLOTS, :],
                         wo[bass.ds(i * 256 + (128 * (j // 2) - 256), P), CHUNK * (j % 2):CHUNK * (j % 2) + CHUNK])
            wu = w_up.rearrange("a (t p) n -> p (a t) n", p=P)
            with sp.Fori(1, FF // 512 + 1) as i:
                for j in range(16):
                    v, side_, t = j // 8, 1 - j // 4 % 2, j % 4
                    load(sp, N3 + j, i * 4 - 4, raw[:, (N3 + j) % SLOTS, :].rearrange("p (t n) -> p t n", n=256),
                         wu[:, 4 * t:4 * t + 4, bass.ds(i * 512 + (FF * side_ + 256 * v - 512), 256)])
            sp.dma_start(gfin[:, :], norm_final_g.partition_broadcast(P)).then_inc(S["gfin_loaded"], 16)
            wd = w_down.rearrange("a k n -> (a k) n")
            with sp.Fori(1, FKT // 2 + 1) as i:
                for j in range(4):
                    load(sp, N4 + j, i - 1, raw[:, (N4 + j) % SLOTS, :],
                         wd[bass.ds(i * 256 + (128 * (j // 2) - 256), P), CHUNK * (j % 2):CHUNK * (j % 2) + CHUNK])
            of = out.rearrange("b (t p) d -> p (b t) d", p=P)
            sp.wait_ge(S["xs_ready"], 7)
            sp.wait_ge(S["xs_pool"], 3)
            sp.dma_start(of[:, 0, :], xs[:, 0, :]).then_inc(S["stored"], 16)
            sp.wait_ge(S["xs_ready"], 9)
            sp.dma_start(of[:, 1, 0:1024], xs[:, 1, 0:1024]).then_inc(S["stored"], 16)
            sp.wait_ge(S["xs_ready"], 10)
            sp.wait_ge(S["xs_pool"], 4)
            sp.dma_start(of[:, 1, 1024:D], xs[:, 1, 1024:D]).then_inc(S["stored"], 16)
            sp.wait_ge(S["stored"], 16 * 3)

        @block.tensor
        def _(pe):
            def mm(o, l, r, start=True, stop=True):
                return pe.matmul(o, l, r, start=start, stop=stop)

            def columns(c, it, xh, kt0, nkt, b0):
                s = c % SLOTS
                pe.wait_ge(lo_ready[s], c // SLOTS + 1 + it)
                for t in range(4):
                    kt = kt0 + t
                    for b in range(2):
                        at = t * 256 + b * P
                        mm(ps[:, b0 + b, :], w_hi[:, s, at:at + P], xh[:, kt, :], kt == 0, False)
                        last = mm(ps[:, b0 + b, 0:SEQ], w_lo[:, s, at:at + P], xh[:, kt, 0:SEQ], False, kt == nkt - 1)
                last.then_inc(chunk_used[s], 1)

            def three(o, xh, tt, s, lo, hi, start, stop):
                mm(o, xh[:, tt * P:tt * P + P], w_hi[:, s, lo:hi], start, False)
                mm(o, xh[:, tt * P:tt * P + P], w_lo[:, s, lo:hi], False, False)
                return mm(o, xh[:, SEQ + tt * P:SEQ + tt * P + P], w_hi[:, s, lo:hi], False, stop)

            def tokens(c, kt0, b0):
                s = c % SLOTS
                pe.wait_ge(lo_ready[s], c // SLOTS + 1)
                for t in range(2):
                    for tt in range(NT):
                        last = three(ps[:, b0 + tt, :], xnT[:, kt0 + t, :], tt, s, 512 * t, 512 * t + 512,
                                     kt0 + t == 0, kt0 + t == KT - 1)
                last.then_inc(chunk_used[s], 1)

            def row_chunk(c, it, first, upper_free=None):
                s, k2, half = c % SLOTS, (c - N2) // 2 % 2, (c - N2) % 2
                pe.wait_ge(lo_ready[s], c // SLOTS + 1 + it)
                for tt in range(NT):
                    if tt == 1 and upper_free is not None:
                        pe.wait_ge(*upper_free)
                    for q in range(2):
                        last = three(ps[:, 4 * tt + 2 * half + q, :], side[:, k2, :], tt, s,
                                     512 * q, 512 * q + 512, first, False)
                last.then_inc(chunk_used[s], 1)

            def last_rows(c0, n):
                order = [(0, k2, half) for k2 in range(2) for half in range(2)]
                order += [(1, k2, half) for half in range(2) for k2 in range(2)]
                for tt, k2, half in order:
                    c = c0 + 2 * k2 + half
                    s = c % SLOTS
                    if tt == 0:
                        if half == 0:
                            pe.wait_ge(S["side_ready"], n - 1 + k2)
                        pe.wait_ge(lo_ready[s], c // SLOTS + 1)
                    for q in range(2):
                        last = three(ps[:, 4 * tt + 2 * half + q, :], side[:, k2, :], tt, s,
                                     512 * q, 512 * q + 512, False, k2 == 1)
                    if tt == 1:
                        last.then_inc(chunk_used[s], 1)
                    elif k2 == 1:
                        last.then_inc(S["quarter_done"], 1)

            def item(k):
                _, name, args = ITEMS[k]
                if k >= 2:
                    pe.wait_ge(item_free[k % 2], k // 2)
                o = pair(k)
                oh = heads(o)
                if name == "cumsum":
                    pe.wait_ge(S["gates_ready"], 2)
                    pe.wait_ge(S["consts"], 3)
                    g32 = gl[:, :, :, :].rearrange("p t a h -> p (t a h)")
                    mm(o[:, 0, 0:32], upto_c[:, :], g32)
                    mm(o[:, 0, 32:64], same_c[:, :], g32)
                    mm(o[:, 0, 64:72], upto[:, :], lf[:, 0, :])
                    mm(o[:, 0, 72:80], upto[:, :], lf[:, 1, :], True, False)
                    last = mm(o[:, 0, 72:80], ones[:, :], lf[:, 0, :], False, True)
                elif name == "turn":
                    g, = args
                    pe.wait_ge(S["silu_ready"], g + 1)
                    for b in range(2):
                        for tt in range(NT):
                            src = gk[:, 2 * (g - 4) + b, tt * P:tt * P + P] if g < 8 else vT[:, b, tt * P:tt * P + P]
                            last = pe.transpose(o[:, 0, (2 * b + tt) * P:(2 * b + tt + 1) * P], src, ident[:, :])
                elif name == "norm":
                    w, = args
                    pe.wait_ge(S["sq_ready"], w + 1)
                    for tt in range(NT):
                        for h in range(H):
                            last = mm(o[:, 0, tt * H + h:tt * H + h + 1], sq[:, h, tt * P:tt * P + P], ones[:, 0:1])
                elif name == "gam":
                    tt, = args
                    pe.wait_ge(S["gr_ready"], tt + 1)
                    for q in range(2):
                        last = mm(o[:, q, :], ones[:, :], nlv[:, tt, 4 * q:4 * q + 4, :].rearrange("p h d -> p (h d)"))
                elif name in ("kk", "qk"):
                    tt, = args
                    t = slice(tt * P, tt * P + P)
                    for h in range(H):
                        last = mm(oh[:, h, :], gk[:, h, t], (gk if name == "kk" else gq)[:, h, t])
                elif name == "solve_p":
                    tt, lv = args
                    pe.wait_ge(S["level_ready"], 2 * lv + tt + 1)
                    if lv == 0:
                        pe.wait_ge(S["inv_start"], 2)
                    else:
                        item_read(pe, "solve_x", tt, lv - 1)
                    for h in range(H):
                        last = mm(oh[:, h, :], nlv[:, tt, h, :], xm[:, tt, h, :])
                elif name == "solve_x":
                    tt, lv = args
                    item_read(pe, "solve_p", tt, lv)
                    if lv:
                        item_read(pe, "solve_xt", tt, lv - 1)
                    for h in range(H):
                        last = mm(oh[:, h, :], xmt[:, tt, h, :], pm_[:, tt, h, :])
                elif name == "solve_xt":
                    tt, lv = args
                    item_read(pe, "solve_p", tt, lv)
                    if lv:
                        item_read(pe, "solve_xt", tt, lv - 1)
                    for h in range(H):
                        last = mm(oh[:, h, :], pm_[:, tt, h, :], xmt[:, tt, h, :])
                elif name == "wt":
                    tt, = args
                    pe.wait_ge(S["kbg_ready"], tt + 1)
                    item_read(pe, "solve_xt", tt, LEVELS - 1)
                    for h in range(H):
                        last = mm(oh[:, h, :], kbg[:, tt, h, :], xmt[:, tt, h, :])
                elif name == "vnew":
                    c, = args
                    r, tt = chunk_rows(c)
                    if c == 0:
                        pe.wait_ge(S["vb_ready"], 2)
                        item_read(pe, "wt", 0)
                        item_read(pe, "wt", 1)
                    else:
                        pe.wait_ge(S["st_ready"], c)
                    for h in range(H):
                        last = mm(oh[r, h, :], xmt[r, tt, h, r], gvt[r, tt, h, :], True, c == 0)
                        if c:
                            last = mm(oh[r, h, :], wt[:, tt, h, r], st[:, h, :], False, True)
                elif name == "ds":
                    c, = args
                    r, tt = chunk_rows(c)
                    item_read(pe, "vnew", c)
                    pe.wait_ge(S["kg_ready"], 2)
                    for h in range(H):
                        last = mm(oh[:, h, :], gkt[r, tt, h, :], vn[r, h, :])
                elif name == "o":
                    c, = args
                    r, tt = chunk_rows(c)
                    item_read(pe, "vnew", c)
                    pe.wait_ge(S["qg_ready"], 2)
                    for h in range(H):
                        last = mm(oh[r, h, :], aqk[r, tt, h, r], vn[r, h, :], True, c == 0)
                        if c:
                            last = mm(oh[r, h, :], gq[:, h, c * L:c * L + L], st_old(c)[:, h, :], False, True)
                elif name == "fbc":
                    kt, = args
                    pe.wait_ge(S["fr_ready"], kt + 1)
                    for q in range(2):
                        last = mm(o[:, q, :], ones[:, :], fr[:, kt, 4 * q:4 * q + 4, :].rearrange("p h d -> p (h d)"))
                elif name == "s0":
                    hg, = args
                    for h in range(4):
                        last = mm(oh[:, h, :], fq[:, 4 * hg + h, 0:P], fk[:, 4 * hg + h, 0:P])
                elif name == "s1":
                    hg, = args
                    oq = o.rearrange("p a (h d) -> p (a h) d", d=SEQ)
                    for h in range(4):
                        last = mm(oq[:, h, :], fq[:, 4 * hg + h, P:SEQ], fk[:, 4 * hg + h, :])
                elif name == "p0":
                    hg, = args
                    pe.wait_ge(S["p_ready"], hg + 1)
                    oq = o.rearrange("p a (h d) -> p (a h) d", d=SEQ)
                    for h in range(4):
                        pe.transpose(oq[:, h, 0:P], p0[:, hg, h, :], ident[:, :])
                        last = pe.transpose(oq[:, h, P:SEQ], p1[:, hg, h, 0:P], ident[:, :])
                elif name == "p1":
                    hg, = args
                    for h in range(4):
                        last = pe.transpose(oh[:, h, :], p1[:, hg, h, P:SEQ], ident[:, :])
                elif name == "pv":
                    hg, = args
                    item_read(pe, "p0", hg)
                    item_read(pe, "p1", hg)
                    oq = o.rearrange("p a (h d) -> p (a h) d", d=SEQ)
                    for h in range(4):
                        mm(oq[:, h, :], fv[:, 0, 4 * hg + h, :], pt0[:, h, hg, :], True, False)
                        last = mm(oq[:, h, P:SEQ], fv[:, 1, 4 * hg + h, :], pt1[:, hg, h, :], False, True)
                elif name == "mturn":
                    for tt in range(NT):
                        for j in range(4):
                            last = pe.transpose(o[:, tt, j * P:j * P + P], mk[:, j, tt * P:tt * P + P], ident[:, :])
                elif name == "vbc":
                    tt, = args
                    pe.wait_ge(S["mr_ready"], tt + 1)
                    for q in range(2):
                        last = mm(o[:, q, :], ones[:, :], mr[:, tt, 4 * q:4 * q + 4, :].rearrange("p h d -> p (h d)"))
                elif name == "msel":
                    c, = args
                    pe.wait_ge(S["mrow_ready"], c)
                    last = mm(o[:, 0, 0:H], sel[:, (c - 1) % 2, :], m_t[:, (c - 1) // 2, :])
                elif name == "mtail":
                    pe.wait_ge(S["mstat_ready"], 1)
                    last = mm(o[:, 0, 0:16], last_c[:, :], bm[:, :, :].rearrange("p t h -> p (t h)"))
                    for b in range(2):
                        last = mm(o[:, 0, 16 + 16 * b:32 + 16 * b], sel[:, b, :], w_int[:, :, :].rearrange("p t h -> p (t h)"))
                elif name == "mbc":
                    tt, = args
                    pe.wait_ge(S["mr_ready"], 2 + tt + 1)
                    for q in range(2):
                        last = mm(o[:, q, :], ones[:, :], mr[:, tt, 4 * q:4 * q + 4, :].rearrange("p h d -> p (h d)"))
                elif name == "mqk":
                    tt, = args
                    for h in range(H):
                        r = slice(L * (h % 2), L * (h % 2) + L)
                        t = slice(tt * P, tt * P + P)
                        last = mm(oh[:, 4 * (h % 2) + h // 2, :], mk[r, h // 2, t], mq[r, h // 2, t])
                elif name == "qc":
                    c, = args
                    r, tt = chunk_rows(c)
                    pe.wait_ge(S["mstate_ready"], c)
                    for j in range(H // 2):
                        last = mm(oh[r, 2 * j:2 * j + 2, :], mq[:, j, c * L:c * L + L], c_st[:, j, :, :])
                elif name == "dc":
                    c, = args
                    r, tt = chunk_rows(c)
                    pe.wait_ge(S["kw_ready"], 2)
                    item_read(pe, "mqk", tt)
                    if c:
                        for j in range(H // 2):
                            mm(o[r, 1, 2 * j:2 * j + 2], mq[:, j, c * L:c * L + L], n_st[:, j, :])
                    for h in range(H):
                        g = slice(L * (h % 2), L * (h % 2) + L)
                        j = h // 2
                        mm(o[r, 1, 8 + h:9 + h], smt[r, tt, h, r], ones[r, 0:1])
                        mm(o[g, 1, 16 + j:17 + j], mkt[r, tt, h, :], ones[r, 0:1])
                        last = mm(o[g, 0, j * P:j * P + P], mkt[r, tt, h, :], mv[r, tt, h, :])
                elif name == "sv":
                    c, = args
                    r, tt = chunk_rows(c)
                    for h in range(H):
                        last = mm(oh[r, h, :], smt[r, tt, h, r], mv[r, tt, h, :])
                elif name in ("gout", "mout"):
                    half, = args
                    pe.wait_ge(S["gy_ready" if name == "gout" else "my_ready"], 2)
                    src = gvt if name == "gout" else mv
                    oq = o.rearrange("p a (h d) -> p (a h) d", d=SEQ)
                    for h in range(4):
                        for tt in range(NT):
                            last = pe.transpose(oq[:, h, tt * P:tt * P + P], src[:, tt, 4 * half + h, :], ident[:, :])
                last.then_inc(item_done[k % 2], 1)

            def st_old(c):
                return st

            pe.wait_ge(S["consts"], 2)
            pe.wait_ge(S["rows_loaded"], 16 * 9)
            for n, m in enumerate((82, 96, P, P, 8)):
                last = pe.transpose(ps[:, 4 + n // 4, (n % 4) * P:(n % 4) * P + m], rows[0:m, n, :], ident[0:m, 0:m])
            last.then_inc(S["rows_turned"], 1)
            for tt in range(NT):
                pe.wait_ge(S["xs_ready"], tt + 1)
                for q in range(4):
                    if q == 2 and tt == 0:
                        pe.wait_ge(S["cols_ready"], 1)
                    for t in range(4):
                        kt = 4 * q + t
                        last = pe.transpose(ps[:, 2 * q + t // 2, (t % 2) * SEQ + tt * P:(t % 2) * SEQ + tt * P + P],
                                            x_in[:, tt, kt * P:kt * P + P], ident[:, :])
                    if tt == NT - 1:
                        last.then_inc(S["xt_written"], 1)

            k = 0
            for c, (u, t) in enumerate(CHUNKS):
                kind = UNITS[u][0]
                if t == 0 and u >= 2:
                    pe.wait_ge(pair_free[u % 2], u // 2)
                if kind == "small":
                    pe.wait_ge(lo_ready[0], 1)
                    for kt in range(KT):
                        if kt % 4 == 0:
                            pe.wait_ge(S["xt_ready"], kt // 4 + 1)
                        mm(ps[0:40, 0, :], w_hi[:, 0, 40 * kt:40 * kt + 40], xnT[:, kt, :], kt == 0, False)
                        last = mm(ps[0:40, 0, 0:SEQ], w_lo[:, 0, 40 * kt:40 * kt + 40], xnT[:, kt, 0:SEQ], False, kt == KT - 1)
                    last.then_inc(chunk_used[0], 1)
                elif kind == "proj":
                    if c == CHUNKS.index((u, 0)) and UNITS[u][2] == 0:
                        item_read(pe, "pv", 0)
                        item_read(pe, "pv", 1)
                    columns(c, 0, y_fox, 4 * t, H, 2 * (u % 2))
                elif UNIT_CHUNKS[kind] == 4:
                    columns(c, 0, xnT, 4 * t, KT, 2 * (u % 2))
                else:
                    tokens(c, 2 * t, 2 * (u % 2))
                if c == 1:
                    pe.wait_ge(S["feat_ready"], 1)
                    for tt in range(NT):
                        last = pe.transpose(ps[:, 1, 40 * tt:40 * tt + 40], feat[0:40, tt * P:tt * P + P], ident[0:40, 0:40])
                    last.then_inc(S["feat_turned"], 1)
                while k < len(ITEMS) and ITEMS[k][0] == c:
                    item(k)
                    k += 1
            assert k == len(ITEMS)
            for p in range(2):
                pe.wait_ge(pair_free[p], (len(UNITS) + 1 - p) // 2)
                pe.wait_ge(item_free[p], (len(ITEMS) + 1 - p) // 2)
            with pe.Fori(0, GROUPS // 2) as i:
                c = N1
                for q in range(4):
                    pe.wait_ge(pair_read[q % 2], i * 2 + (q // 2 + 1))
                    for t in range(4):
                        columns(c, i * 6, xnT, 4 * t, KT, 4 * (q % 2))
                        c += 1
                    for t in range(2):
                        columns(c, i * 6, (y_gdn, y_ml)[q % 2], 4 * t, H, 4 * (q % 2) + 2)
                        c += 1
            pe.wait_ge(pair_read[0], 2 * (GROUPS // 2) + 1)
            for j in range(4):
                if j % 2 == 0:
                    pe.wait_ge(S["side_ready"], j // 2 + 1)
                row_chunk(N2 + j, 0, j < 2, (pair_read[1], 2 * (GROUPS // 2) + 1) if j == 0 else None)
            with pe.Fori(0, KT // 2 - 2) as i:
                for j in range(4):
                    if j % 2 == 0:
                        pe.wait_ge(S["side_ready"], i * 2 + (j // 2 + 3))
                    row_chunk(N2 + 4 + j, i, False)
            last_rows(N3 - 4, KT)
            for tt in range(NT):
                pe.wait_ge(S["x1_ready"], 2 * tt + 2)
                for n in range(4):
                    if tt == 0:
                        pe.wait_ge(*((S["xs_ready"], 3) if n < 2 else (S["xs_pool"], 1)))
                    else:
                        pe.wait_ge(*((S["xs_ready"], 4 + n) if n < 3 else (S["xs_pool"], 2)))
                    for t in range(4):
                        kt = 4 * n + t
                        last = pe.transpose(ps[:, 4 * tt + n, t * P:t * P + P], xs[:, tt, kt * P:kt * P + P], ident[:, :])
                    last.then_inc(S["xt_written"], 1)
            with pe.Fori(0, FF // 512) as i:
                for v in range(2):
                    pe.wait_ge(up_read[v], i + 1)
                    for j in range(8):
                        if v == 0 and j < 4:
                            pe.wait_ge(S["xt_ready"], 4 + (3, 4, 6, 8)[j])
                        columns(N3 + 8 * v + j, i * 4, xnT, 4 * (j % 4), KT, 4 * v + 2 * (j // 4))
            pe.wait_ge(up_read[0], FF // 512 + 1)
            for j in range(4):
                if j % 2 == 0:
                    pe.wait_ge(S["side_ready"], KT + j // 2 + 1)
                row_chunk(N4 + j, 0, j < 2, (up_read[1], FF // 512 + 1) if j == 0 else None)
            with pe.Fori(0, FKT // 2 - 2) as i:
                for j in range(4):
                    if j % 2 == 0:
                        pe.wait_ge(S["side_ready"], i * 2 + (KT + j // 2 + 3))
                    row_chunk(N4 + 4 + j, i, False)
            last_rows(N5 - 4, KT + FKT)

        @block.scalar
        def _(act):
            order = [0]

            def chain(ins):
                order[0] += 1
                ins.then_inc(S["act_chain"], 1)
                act.wait_ge(S["act_chain"], order[0])

            def f(o, i, fn, **kw):
                return act.activation(o, i, fn, **kw)

            def flat(ap):
                return ap.rearrange("p h d -> p (h d)")

            def turn_x_hi():
                for q in range(4):
                    act.wait_ge(S["xt_written"], q + 1)
                    for t in range(4):
                        kt = 4 * q + t
                        last = f(xnT[:, kt, 0:SEQ], ps[:, 2 * q + t // 2, (t % 2) * SEQ:(t % 2) * SEQ + SEQ],
                                 ACT.Identity, scale=cols[:, kt:kt + 1], bias=0.0)
                    last.then_inc(S["xt_hi"], 1)
                    if q < 3:
                        split_hi(act, q + 1)

            def out_hi(k, half, y, col, ready):
                item_written(act, k)
                o = pair(k).rearrange("p a (h d) -> p (a h) d", d=SEQ)
                f(y[:, 4 * half:4 * half + 4, 0:SEQ], o, ACT.Identity,
                  **({"scale": cols[:, col:col + 1], "bias": 0.0} if col is not None else {"bias": 0.0})).then_inc(S[ready], 1)

            def item(k):
                _, name, args = ITEMS[k]
                o = pair(k)
                free = item_free[k % 2]
                if name == "turn":
                    g, = args
                    item_written(act, k)
                    dst = (gkt if g < 8 else gvt)[:, :, 2 * (g % 4):2 * (g % 4) + 2, :]
                    f(dst.rearrange("p t h d -> p h t d"), o[:, 0, :].rearrange("p (h t d) -> p h t d", h=2, t=2),
                      ACT.Copy).then_inc(free, 1)
                    if g == 7:
                        item_read(act, "norm", 0)
                        f(sq[:, :, :], gk[:, :, :], ACT.Square).then_inc(S["sq_ready"], 1)
                elif name == "norm":
                    w, = args
                    act.wait_ge(S["norm_in"], w + 1)
                    f(rn[:, w, :, :], rn[:, w, :, :], ACT.Sqrt).then_inc(S["norm_root"], 1)
                    if w == 1:
                        act.wait_ge(S["coef_in"], 1)
                        f(c_k[:, :, :], c_k[:, :, :], ACT.Exp)
                        f(eg[:, :, :], eg[:, :, :], ACT.Exp).then_inc(S["coef_exp"], 1)
                elif name == "gam":
                    tt, = args
                    act.wait_ge(S["gam_raw"], tt + 1)
                    f(pm_[:, tt, :, :], heads(o), ACT.Exp).then_inc(free, 1)
                    act.wait_ge(S["e_masked"], 2 * tt + 2)
                    f(ed[:, tt, :, :], ed[:, tt, :, :], ACT.Exp).then_inc(S["e_exp"], 1)
                elif name == "solve_p":
                    tt, lv = args
                    item_written(act, k)
                    if lv == 0:
                        act.wait_ge(S["qg_ready"], 2)
                        act.wait_ge(S["coef_ready"], 1)
                    for h in range(H):
                        last = f(pm_[:, tt, h, :], heads(o)[:, h, :], ACT.Identity, scale=c_m[:, tt, h:h + 1], bias=0.0)
                    last.then_inc(free, 1)
                elif name == "wt":
                    tt, = args
                    item_written(act, k)
                    f(wt[:, tt, :, :], heads(o), ACT.Copy, scale=-1.0).then_inc(free, 1)
                elif name == "vnew":
                    c, = args
                    r, tt = chunk_rows(c)
                    item_written(act, k)
                    if c >= 1:
                        item_read(act, "o", c - 1)
                    f(vn[r, :, :], heads(o)[r], ACT.Copy).then_inc(free, 1)
                elif name == "o":
                    c, = args
                    r, tt = chunk_rows(c)
                    item_written(act, k)
                    f(gvt[r, tt, :, :], heads(o)[r], ACT.Copy).then_inc(free, 1)
                elif name in ("s0", "s1"):
                    hg, = args
                    b, p, w = (0, p0, P) if name == "s0" else (1, p1, SEQ)
                    act.wait_ge(S["smax_ready"], 2 * hg + b + 1)
                    for h in range(4):
                        last = f(p[:, hg, h, :], p[:, hg, h, :], ACT.Exp, bias=fmax[:, hg, b, h:h + 1],
                                 accum_out=fsum[:, hg, b, h:h + 1])
                    last.then_inc(S["p_exp"], 1)
                elif name == "p0":
                    hg, = args
                    item_written(act, k)
                    f(pt0[:, :, hg, :], o.rearrange("p a (h d) -> p (a h) d", d=SEQ), ACT.Copy).then_inc(free, 1)
                elif name == "p1":
                    hg, = args
                    item_written(act, k)
                    f(flat(pt1[:, hg, :, :]), o[:, 0, :], ACT.Copy).then_inc(free, 1)
                elif name == "pv":
                    out_hi(k, args[0], y_fox, None, "foxhi_ready")
                elif name == "mturn":
                    item_written(act, k)
                    f(mkt[:, :, :, :].rearrange("p t h d -> p (t h d)"), o.rearrange("p a b -> p (a b)"), ACT.Copy).then_inc(free, 1)
                elif name == "vbc":
                    tt, = args
                    item_written(act, k)
                    f(me[:, tt, :, :], heads(o), ACT.Copy).then_inc(free, 1)
                elif name == "msel":
                    if args[0] == NC - 1:
                        act.wait_ge(S["mstat_in"], 1)
                        f(w_int[:, :, :], w_int[:, :, :], ACT.Exp)
                        f(e_m[:, :, :], m_t[:, :, :], ACT.Exp, scale=-1.0).then_inc(S["mstat_exp"], 1)
                elif name == "mtail":
                    act.wait_ge(S["mtail_in"], 1)
                    f(c_kw[:, :, :], c_kw[:, :, :], ACT.Exp).then_inc(S["mtail_exp"], 1)
                elif name == "mbc":
                    tt, = args
                    act.wait_ge(S["mt_masked"], tt + 1)
                    f(me[:, tt, :, :], me[:, tt, :, :], ACT.Exp).then_inc(S["mt_exp"], 1)
                elif name == "gout":
                    out_hi(k, args[0], y_gdn, 80, "ghi_ready")
                elif name == "mout":
                    out_hi(k, args[0], y_ml, 81, "mhi_ready")

            def unit(u):
                kind, _, g = UNITS[u] if u is not None else ("softplus", 0, 0)
                b0, free = (2 * (u % 2), pair_free[u % 2]) if u is not None else (0, None)
                if kind == "small":
                    pass
                elif kind == "softplus":
                    act.wait_ge(S["soft_in"], 1)
                    f(soft_e[:, :, :, :], soft_n[:, :, :, :], ACT.Exp).then_inc(S["soft_exp"], 1)
                    f(beta[:, :, :], pre5[:, :, 1, :], ACT.Exp, scale=-1.0)
                    act.wait_ge(S["small_loaded"], 80)
                    f(neg_a[:, :], alog[:, :], ACT.Exp).then_inc(S["neg_exp"], 1)
                    act.wait_ge(S["soft_exp"], 1)
                    f(soft_e[:, :, :, :], soft_e[:, :, :, :], ACT.Ln, bias=eps_c[:, 1:2]).then_inc(S["soft_out"], 1)
                elif kind == "gdn":
                    act.wait_ge(S["conv_ready"], g + 1)
                    if g < 8:
                        dst = (gq if g < 4 else gk)[:, 2 * (g % 4):2 * (g % 4) + 2, :]
                    else:
                        if g > 8:
                            item_read(act, "turn", g - 1)
                        dst = vT[:, :, :]
                    if g == 0:
                        act.wait_ge(S["cols_ready"], 1)
                    f(dst, acc[:, :, :], ACT.Silu).then_inc(S["silu_ready"], 1)
                    if g == 3:
                        act.wait_ge(S["silu_ready"], 4)
                        f(sq[:, :, :], gq[:, :, :], ACT.Square).then_inc(S["sq_ready"], 1)
                elif kind in ("foxv", "mlv", "z", "mlo"):
                    chunk_done(act, CHUNKS.index((u, 7)))
                    if kind == "z" and g == 0:
                        item_read(act, "pv", 1)
                    if kind == "mlo" and g == 0:
                        item_read(act, "gout", 1)
                    dst = {"foxv": fv, "mlv": mv, "z": z, "mlo": mo}[kind]
                    fn = {"foxv": ACT.Copy, "mlv": ACT.Copy, "z": ACT.Silu, "mlo": ACT.Sigmoid}[kind]
                    f(dst[:, :, 4 * g:4 * g + 4, :].rearrange("p t h d -> p t (h d)"), ps[:, b0:b0 + 2, :], fn).then_inc(free, 1)
                elif kind == "gate":
                    act.wait_ge(S["gate_in"], g + 1)
                    for b in range(2):
                        last = f(g_sig[:, b, :], g_sum[:, b, :], ACT.Sigmoid, bias=cols[:, 32 + 2 * g + b:33 + 2 * g + b])
                    last.then_inc(S["gate_sig"], 1)

            def step(name, n):
                if name == "gdn_out" and n < 2:
                    if n:
                        act.wait_ge(S["gsq_done"], 1)
                    else:
                        item_read(act, "o", NC - 1)
                    f(osq[:, :, :], gvt[:, n, :, :], ACT.Square).then_inc(S["gsq_in"], 1)
                elif name == "gdn_out" and n == 2:
                    act.wait_ge(S["groot_in"], 1)
                    f(rstd[:, 2:4, :], rstd[:, 2:4, :], ACT.Sqrt).then_inc(S["groot_done"], 1)
                elif name == "ml_out" and n < 2:
                    act.wait_ge(S["msq_in"], n + 1)
                    f(osq[:, :, :], mv[:, n, :, :], ACT.Square).then_inc(S["msq_done"], 1)
                elif name == "ml_out" and n == 3:
                    act.wait_ge(S["mroot_in"], 1)
                    f(rstd[:, 2:4, :], rstd[:, 2:4, :], ACT.Sqrt).then_inc(S["mroot_done"], 1)

            act.wait_ge(S["consts"], 1)
            f(spare[:, :], eps_c[:, :], ACT.Sqrt)
            for tt in range(NT):
                act.wait_ge(x_loaded[tt], 16)
                chain(f(x_sq[:, :], x_in[:, tt, :], ACT.Square, accum_out=ss[:, 0, tt:tt + 1]))
                f(rstd[:, 0, tt:tt + 1], ss[:, 0, tt:tt + 1], ACT.Sqrt, scale=1.0 / D, bias=eps_c[:, 0:1]).then_inc(S["sums_ready"], 1)
            split_hi(act, 0)
            act.wait_ge(S["cols_ready"], 1)
            turn_x_hi()

            k = 0
            for c, (u, t) in enumerate(CHUNKS):
                split_hi(act, c + SLOTS)
                if t == UNIT_CHUNKS[UNITS[u][0]] - 1:
                    unit(u)
                if c == 1:
                    unit(None)
                while k < len(ITEMS) and ITEMS[k][0] == c:
                    item(k)
                    k += 1
                for _, name, n in (e for e in STEPS if e[0] == c):
                    step(name, n)
            def side_first(src, ready):
                act.wait_ge(*ready)
                for kt in range(2):
                    f(side[:, kt, 0:SEQ], src[:, kt, :], ACT.Copy).then_inc(S["side_hi"], 1)

            def side_hi(c, it, kt_ap, slot):
                act.wait_ge(chunk_used[c % SLOTS], c // SLOTS + 1 + it)
                f(side[:, slot, 0:SEQ], kt_ap, ACT.Copy).then_inc(S["side_hi"], 1)

            def gates_round(i, last=False):
                if last:
                    side_first(yT, (S["y_ready"], GROUPS + 8))
                c = N1
                for q in range(4):
                    for t in range(6):
                        split_hi(act, c + SLOTS, i * 6)
                        if t == 3:
                            act.wait_ge(S["gate_in"], i * 4 + (GROUPS + q + 1))
                            for b in range(2):
                                ins = f(g_sig[:, b, :], g_sum[:, b, :], ACT.Sigmoid,
                                        bias=cols[:, bass.ds(i * 4 + (48 + 16 * (q % 2) + 2 * (q // 2) + b), 1)])
                            ins.then_inc(S["gate_sig"], 1)
                        c += 1

            with act.Fori(0, GROUPS // 2 - 1) as i:
                gates_round(i)
            gates_round(GROUPS // 2 - 1, last=True)

            def norm_rows(p, after):
                f(spare[:, :], eps_c[:, :], ACT.Sqrt)
                for tt in range(NT):
                    sums = ss[:, 1, 4 * p + 2 * tt:4 * p + 2 * tt + 2]
                    for half in range(2):
                        act.wait_ge(S["x1_ready"], 4 * p + 2 * tt + half + 1)
                        chain(f(junk[:, 0:CHUNK], x1[:, tt, CHUNK * half:CHUNK * half + CHUNK], ACT.Square,
                                accum_out=sums[:, half:half + 1]))
                        if half == 0:
                            chain(f(norm_b[:, p, tt:tt + 1], sums[:, 0:1], ACT.Identity, scale=1.0 / D, bias=eps_c[:, 0:1]))
                    f(rstd[:, 1, 2 * p + tt:2 * p + tt + 1], sums[:, 1:2], ACT.Sqrt, scale=1.0 / D,
                      bias=norm_b[:, p, tt:tt + 1]).then_inc(S["sums_ready"], 1)
                    if tt == 0:
                        after()

            with act.Fori(0, KT // 2 - 1) as i:
                for j in range(4):
                    split_hi(act, N2 + SLOTS + j, i)
                    if j % 2:
                        side_hi(N2 + j, i, yT[:, bass.ds(i * 2 + (2 + j // 2), 1), :].rearrange("p a b -> p (a b)"), j // 2)
            norm_rows(0, lambda: [split_hi(act, N3), split_hi(act, N3 + 2)])
            for n, (tt, b) in enumerate(TURNS):
                act.wait_ge(S["xt_written"], 4 + 4 * tt + b + 1)
                dst, src = turned(tt, b)
                f(dst, src, ACT.Copy).then_inc(S["xt_hi"], 1)
                if n in (2, 3):
                    split_hi(act, N3 + 2 * n - 3)

            def up_round(i, last=False):
                if last:
                    side_first(hT, (S["h_ready"], 1))
                for v in range(2):
                    for j in range(8):
                        split_hi(act, N3 + 8 * v + j + SLOTS, i * 4)
                        if j == 4:
                            act.wait_ge(S["gate_conv"], i * 2 + (v + 1))
                            f(usil[:, :, :], uacc[:, 0, :, :], ACT.Silu).then_inc(S["up_silu"], 1)

            with act.Fori(0, FF // 512 - 1) as i:
                up_round(i)
            up_round(FF // 512 - 1, last=True)
            with act.Fori(0, FKT // 2 - 1) as i:
                for j in range(4):
                    split_hi(act, N4 + SLOTS + j, i)
                    if j % 2:
                        side_hi(N4 + j, i, hT[:, bass.ds(i * 2 + (2 + j // 2), 1), :].rearrange("p a b -> p (a b)"), j // 2)
            norm_rows(1, lambda: None)

        @block.vector
        def _(dve):
            order = [0]

            def chain(ins):
                order[0] += 1
                ins.then_inc(S["dve_chain"], 1)
                dve.wait_ge(S["dve_chain"], order[0])

            tt_ = dve.tensor_tensor

            def turn_x_lo():
                for q in range(4):
                    dve.wait_ge(S["xt_hi"], q + 1)
                    for t in range(4):
                        kt = 4 * q + t
                        last = dve.scalar_tensor_tensor(
                            xnT[:, kt, SEQ:2 * SEQ], ps[:, 2 * q + t // 2, (t % 2) * SEQ:(t % 2) * SEQ + SEQ],
                            cols[:, kt:kt + 1], xnT[:, kt, 0:SEQ], ALU.mult, ALU.subtract)
                    last.then_inc(S["xt_ready"], 1)
                    if q < 2:
                        split_lo(dve, q + 1)

            def out_lo(k, half, y, col, ready):
                dve.wait_ge(S[ready], half + 1)
                o = pair(k)
                for a in range(2):
                    q = 4 * half + 2 * a
                    last = dve.scalar_tensor_tensor(
                        y[:, q:q + 2, SEQ:2 * SEQ], o[:, a, :].rearrange("p (h d) -> p h d", d=SEQ),
                        cols[:, col:col + 1] if col is not None else 1.0, y[:, q:q + 2, 0:SEQ], ALU.mult, ALU.subtract)
                last.then_inc(item_free[k % 2], 1)

            def on_diagonal(dst, vec):
                return tt_(dst, over_heads(ident[:, :], H), over_free(vec, P), ALU.mult)

            def both_parts(dst, b0):
                return dve.tensor_reduce(dst, ps[:, b0:b0 + 2, :].rearrange("p b (s t) -> p b t s", s=2), AX.X, ALU.add)

            def item(k):
                _, name, args = ITEMS[k]
                o = pair(k)
                oh = heads(o)
                free = item_free[k % 2]
                if name == "cumsum":
                    item_written(dve, k)
                    dve.tensor_copy(cum[:, :, :, :].rearrange("p t a h -> p (t a h)"), o[:, 0, 0:32])
                    dve.tensor_copy(tot[:, :, :, :].rearrange("p t a h -> p (t a h)"), o[:, 0, 32:64])
                    dve.tensor_copy(fcum[:, :, :].rearrange("p t h -> p (t h)"), o[:, 0, 64:80]).then_inc(free, 1)
                elif name == "norm":
                    w, = args
                    item_written(dve, k)
                    dve.tensor_scalar(rn[:, w, :, :].rearrange("p t h -> p (t h)"), o[:, 0, 0:16], EPS, None,
                                      ALU.add).then_inc(S["norm_in"], 1)
                    dve.wait_ge(S["norm_root"], w + 1)
                    chain(dve.reciprocal(rn[:, w, :, :], rn[:, w, :, :]))
                    if w == 0:
                        dve.tensor_scalar(rn[:, 0, :, :], rn[:, 0, :, :], HD ** -0.5, None, ALU.mult).then_inc(free, 1)
                    else:
                        item_read(dve, "cumsum")
                        chain(tt_(c_k[:, :, :], tot[:, :, 0, :], gam, ALU.subtract))
                        chain(tt_(c_m[:, :, :], beta[:, :, :], rn[:, 1, :, :], ALU.mult))
                        dve.tensor_copy(eg[:, :, :], gam).then_inc(S["coef_in"], 1)
                        dve.wait_ge(S["coef_exp"], 1)
                        tt_(c_w[:, :, :], c_m[:, :, :], eg[:, :, :], ALU.mult).then_inc(free, 1)
                        tt_(c_k[:, :, :], c_k[:, :, :], rn[:, 1, :, :], ALU.mult).then_inc(S["coef_ready"], 1)
                        dve.wait_ge(S["coef_ready"], 1)
                        for tt in range(NT):
                            on_diagonal(nlv[:, tt, :, :], cum[:, tt, 0, :]).then_inc(S["gr_ready"], 1)
                elif name == "gam":
                    tt, = args
                    item_written(dve, k)
                    tt_(ed[:, tt, :, :], oh, over_free(cum[:, tt, 0, :], P), ALU.subtract).then_inc(S["gam_raw"], 1)
                    dve.wait_ge(S["e_exp"], tt + 1)
                    tt_(ed[:, tt, :, :], ed[:, tt, :, :], over_free(rn[:, 1, tt, :], P), ALU.mult).then_inc(S["dk_ready"], 1)
                elif name == "kk":
                    tt, = args
                    item_written(dve, k)
                    dve.wait_ge(S["dk_ready"], tt + 1)
                    tt_(nt_[:, tt, :, :], oh, ed[:, tt, :, :], ALU.mult).then_inc(free, 1)
                elif name == "qk":
                    tt, = args
                    item_written(dve, k)
                    tt_(aqk[:, tt, :, :], oh, ed[:, tt, :, :], ALU.mult).then_inc(free, 1)
                    item_read(dve, "gam", tt)
                    q_t = gq[:, :, tt * P:tt * P + P]
                    for cb in range(2):
                        dve.tensor_copy(e_last[:, 2 * tt + cb, :], pm_[:, tt, :, L * cb + L - 1])
                    tt_(q_t, q_t, pm_[:, tt, :, :], ALU.mult).then_inc(S["qg_ready"], 1)
                elif name in ("solve_x", "solve_xt"):
                    tt, lv = args
                    item_written(dve, k)
                    m = (xm if name == "solve_x" else xmt)[:, tt, :, :]
                    if name == "solve_xt" and lv < LEVELS - 1:
                        item_read(dve, "solve_x", tt, lv)
                    tt_(m, m, oh, ALU.subtract).then_inc(free, 1)
                elif name == "ds":
                    c, = args
                    item_written(dve, k)
                    if c == 0:
                        dve.tensor_copy(st[:, :, :], oh).then_inc(free, 1)
                        item_read(dve, "ds", c)
                        dve.sem_inc(S["st_ready"], 1)
                    else:
                        item_written(dve, ITEM["o", (c,)])
                        chain(tt_(st[:, :, :], st[:, :, :], over_free(e_last[:, c, :], HD), ALU.mult))
                        tt_(st[:, :, :], st[:, :, :], oh, ALU.add).then_inc(free, 1)
                        item_read(dve, "ds", c)
                        dve.sem_inc(S["st_ready"], 1)
                elif name == "fbc":
                    kt, = args
                    item_written(dve, k)
                    if kt == 0:
                        tt_(mf0[:, :, :], over_free(fcum[:, 0, :], P), oh, ALU.subtract)
                        tt_(mf1[:, :, 0:P], over_free(fcum[:, 1, :], P), oh, ALU.subtract).then_inc(free, 1)
                    else:
                        tt_(mf1[:, :, P:SEQ], over_free(fcum[:, 1, :], P), oh, ALU.subtract).then_inc(free, 1)
                elif name in ("s0", "s1"):
                    hg, = args
                    b, p, mf, w = (0, p0, mf0, P) if name == "s0" else (1, p1, mf1, SEQ)
                    item_written(dve, k)
                    dve.wait_ge(S["mf_ready"], 2)
                    for q in range(4 * w // 512):
                        n = 512 // w
                        last = dve.scalar_tensor_tensor(
                            p[:, hg, n * q:n * q + n, :].rearrange("p h d -> p (h d)"), o[:, q, :], HD ** -0.5,
                            mf[:, 4 * hg + n * q:4 * hg + n * q + n, :].rearrange("p h d -> p (h d)"), ALU.mult, ALU.add)
                    last.then_inc(free, 1)
                    item_read(dve, name, hg)
                    dve.tensor_reduce(fmax[:, hg, b, :], p[:, hg, :, :], AX.X, ALU.max,
                                      negate=True).then_inc(S["smax_ready"], 1)
                    if b == 1:
                        dve.wait_ge(S["p_exp"], 2 * hg + 2)
                        chain(dve.reciprocal(fsum[:, hg, :, :], fsum[:, hg, :, :]))
                        tt_(p0[:, hg, :, :], p0[:, hg, :, :], over_free(fsum[:, hg, 0, :], P), ALU.mult)
                        tt_(p1[:, hg, :, :], p1[:, hg, :, :], over_free(fsum[:, hg, 1, :], SEQ), ALU.mult).then_inc(S["p_ready"], 1)
                elif name == "pv":
                    out_lo(k, args[0], y_fox, None, "foxhi_ready")
                elif name == "vbc":
                    tt, = args
                    dve.wait_ge(S["me_masked"], tt + 1)
                    chain(dve.tensor_reduce(dmax[:, tt, :], me[:, tt, :, :], AX.X, ALU.max))
                    chain(tt_(dmax[:, tt, :], dmax[:, tt, :], cum[:, tt, 1, :], ALU.add))
                    if tt == 1:
                        r, t0 = chunk_rows(0)
                        chain(dve.tensor_copy(inter[r, 0, :], cum[r, 0, 1, :]))
                        dve.memset(m_t[64:128, 0, :], 0.0)
                        chain(dve.memset(m_t[:, 1, :], 0.0))
                        tt_(m_t[r, 0, :], inter[r, 0, :], dmax[r, 0, :], ALU.max).then_inc(S["mrow_ready"], 1)
                elif name == "msel":
                    c, = args
                    r, t0 = chunk_rows(c)
                    item_written(dve, k)
                    tt_(inter[r, t0, :], cum[r, t0, 1, :], o[r, 0, 0:H], ALU.add).then_inc(free, 1)
                    item_read(dve, "msel", c)
                    tt_(m_t[r, t0, :], inter[r, t0, :], dmax[r, t0, :], ALU.max).then_inc(S["mrow_ready"], 1)
                    if c == NC - 1:
                        dve.wait_ge(S["mrow_ready"], NC)
                        tt_(bm[:, :, :], bc_, m_t[:, :, :], ALU.subtract)
                        tt_(w_int[:, :, :], inter[:, :, :], m_t[:, :, :], ALU.subtract).then_inc(S["mstat_in"], 1)
                        dve.wait_ge(S["mstat_exp"], 1)
                        dve.tensor_scalar(w_int8[:, :, :], w_int[:, :, :], L ** -0.5, None, ALU.mult).then_inc(S["mstat_ready"], 1)
                        for tt in range(NT):
                            item_read(dve, "vbc", tt)
                            on_diagonal(mr[:, tt, :, :], bm[:, tt, :]).then_inc(S["mr_ready"], 1)
                elif name == "mtail":
                    item_written(dve, k)
                    dve.tensor_copy(w_last[:, :, :, :].rearrange("p t b h -> p b t h"),
                                    o[:, 0, 16:48].rearrange("p (b t h) -> p b t h", b=2, t=2))
                    tt_(c_kw[:, :, :], vs[:, :, :], o[:, 0, 0:16].rearrange("p (t h) -> p t h", t=2),
                        ALU.add).then_inc(S["mtail_in"], 1)
                    dve.wait_ge(S["mtail_in"], 1)
                    dve.sem_inc(free, 1)
                    dve.wait_ge(S["mtail_exp"], 1)
                    item_read(dve, "mturn")
                    for tt in range(NT):
                        tt_(mkt[:, tt, :, :], mkt[:, tt, :, :], over_free(c_kw[:, tt, :], L), ALU.mult).then_inc(S["kw_ready"], 1)
                elif name == "mbc":
                    tt, = args
                    item_written(dve, k)
                    tt_(me[:, tt, :, :], oh, over_free(vs[:, tt, :], P), ALU.add).then_inc(free, 1)
                elif name == "mqk":
                    tt, = args
                    item_written(dve, k)
                    dve.wait_ge(S["mt_exp"], tt + 1)
                    for q in range(2):
                        def odd(t):
                            return t[:, tt, :, :].rearrange("p (j b) d -> p j b d", b=2)[:, :, q, :]
                        last = dve.scalar_tensor_tensor(
                            odd(smt), o[:, q, :].rearrange("p (j d) -> p j d", d=P), L ** -0.5, odd(me), ALU.mult, ALU.mult)
                    last.then_inc(free, 1)
                elif name == "qc":
                    c, = args
                    r, tt = chunk_rows(c)
                    item_written(dve, k)
                    tt_(mt1[r, :, :], oh[r], over_free(w_int8[r, tt, :], HD), ALU.mult).then_inc(free, 1)
                elif name == "dc":
                    c, = args
                    r, tt = chunk_rows(c)
                    item_written(dve, k)
                    dcs = o[:, 0, :].rearrange("p (j d) -> p j d", d=HD)
                    if c == 0:
                        chain(dve.tensor_copy(den[r, tt, :], o[r, 1, 8:16]))
                        dve.memset(n_st[:, :, :], 0.0)
                        chain(dve.memset(c_st[:, :, :, :], 0.0))
                        for b in range(2):
                            g = slice(L * b, L * b + L)
                            dve.tensor_copy(n_st[g, :, b], o[g, 1, 16:20])
                            ins = dve.tensor_copy(c_st[g, :, b, :], dcs[g])
                        chain(ins)
                    else:
                        item_read(dve, "qc", c)
                        chain(tt_(den[r, tt, :], o[r, 1, 0:8], w_int8[r, tt, :], ALU.mult))
                        chain(tt_(den[r, tt, :], den[r, tt, :], o[r, 1, 8:16], ALU.add))
                        for b in range(2):
                            g = slice(L * b, L * b + L)
                            wl = w_last[g, tt, c % 2, :].rearrange("p (j b) -> p j b", b=2)[:, :, b]
                            tt_(c_n[g, :, :], c_st[g, :, b, :], over_free(wl, HD), ALU.mult)
                            chain(tt_(n_st[g, :, b], n_st[g, :, b], wl, ALU.mult))
                        for b in range(2):
                            g = slice(L * b, L * b + L)
                            tt_(n_st[g, :, b], n_st[g, :, b], o[g, 1, 16:20], ALU.add)
                            ins = tt_(c_st[g, :, b, :], c_n[g, :, :], dcs[g], ALU.add)
                        chain(ins)
                    dve.sem_inc(S["mstate_ready"], 1)
                    chain(dve.scalar_tensor_tensor(den2[r, tt, :], den[r, tt, :], -1.0, den[r, tt, :], ALU.mult, ALU.max))
                    chain(tt_(den2[r, tt, :], den2[r, tt, :], e_m[r, tt, :], ALU.max))
                    dve.reciprocal(rd[r, tt, :], den2[r, tt, :]).then_inc(free, 1)
                elif name == "sv":
                    c, = args
                    r, tt = chunk_rows(c)
                    item_written(dve, k)
                    if c == 0:
                        dve.tensor_copy(mv[r, tt, :, :], oh[r]).then_inc(free, 1)
                    else:
                        tt_(mv[r, tt, :, :], mt1[r, :, :], oh[r], ALU.add).then_inc(free, 1)
                elif name == "gout":
                    out_lo(k, args[0], y_gdn, 80, "ghi_ready")
                elif name == "mout":
                    out_lo(k, args[0], y_ml, 81, "mhi_ready")

            def scalar_gates():
                dve.wait_ge(S["small_loaded"], 80)
                dve.wait_ge(S["feat_turned"], 1)
                tt_(pre5[:, :, :, :].rearrange("p t a h -> p t (a h)"), ps[:, 1, 0:80].rearrange("p (t n) -> p t n", n=40),
                    over_heads(bias5[:, :, :].rearrange("p a h -> p (a h)"), NT), ALU.add).then_inc(pair_free[0], 1)
                dve.wait_ge(pair_free[0], 1)
                for n, (a, sgn) in enumerate(((0, -1.0), (2, 1.0), (4, -1.0))):
                    last = dve.tensor_scalar(soft[:, :, n, :], pre5[:, :, a, :], sgn, None, ALU.mult)
                chain(last)
                sf = soft[:, :, :, :].rearrange("p t a h -> p (t a h)")
                sn = soft_n[:, :, :, :].rearrange("p t a h -> p (t a h)")
                dve.scalar_tensor_tensor(sn, sf, -1.0, sf, ALU.mult, ALU.min).then_inc(S["soft_in"], 1)
                dve.wait_ge(S["soft_out"], 1)
                chain(dve.scalar_tensor_tensor(sf, sf, 0.0, soft_e[:, :, :, :].rearrange("p t a h -> p (t a h)"),
                                               ALU.max, ALU.add))
                dve.wait_ge(S["neg_exp"], 1)
                dve.tensor_scalar(lf[:, :, :], soft[:, :, 0, :], -1.0, None, ALU.mult)
                dve.tensor_scalar(gl[:, :, 1, :], soft[:, :, 2, :], -1.0, None, ALU.mult)
                chain(dve.tensor_scalar(neg_a[:, :], neg_a[:, :], -1.0, None, ALU.mult))
                tt_(gl[:, :, 0, :], soft[:, :, 1, :], over_heads(neg_a[:, :], NT), ALU.mult).then_inc(S["gates_ready"], 1)
                chain(dve.tensor_scalar(beta[:, :, :], beta[:, :, :], 1.0, None, ALU.add))
                dve.reciprocal(beta[:, :, :], beta[:, :, :]).then_inc(S["gates_ready"], 1)
                dve.memset(pre[:, :, 0:3], 0.0)

            def unit(u):
                kind, _, g = UNITS[u]
                b0, free = 2 * (u % 2), pair_free[u % 2]
                if kind == "small":
                    chunk_done(dve, 0)
                    dve.tensor_reduce(feat[0:40, :], ps[0:40, 0, :].rearrange("p (s t) -> p t s", s=2), AX.X,
                                      ALU.add).then_inc(S["feat_ready"], 1)
                elif kind == "gdn":
                    chunk_done(dve, CHUNKS.index((u, 3)))
                    if g:
                        dve.wait_ge(S["silu_ready"], g)
                    both_parts(pre[:, :, 3:3 + SEQ], b0).then_inc(free, 1)
                    dve.wait_ge(free, u // 2 + 1)
                    for j in (3, 2, 1, 0):
                        for b in range(2):
                            n = 2 * g + b
                            if j == 3:
                                ins = dve.tensor_scalar(acc[:, b, :], pre[:, b, 3:3 + SEQ], conv_c[:, 3, n:n + 1], None, ALU.mult)
                            else:
                                ins = dve.scalar_tensor_tensor(acc[:, b, :], pre[:, b, j:j + SEQ], conv_c[:, j, n:n + 1],
                                                               acc[:, b, :], ALU.mult, ALU.add)
                        if j:
                            chain(ins)
                    ins.then_inc(S["conv_ready"], 1)
                elif kind in ("foxqk", "mlqk"):
                    chunk_done(dve, CHUNKS.index((u, 3)))
                    n = 4 if kind == "foxqk" else 2
                    if kind == "mlqk" and g == 0:
                        item_read(dve, "turn", 11)
                    dst = ((fq, fk) if kind == "foxqk" else (mq, mk))[g // n][:, 2 * (g % n):2 * (g % n) + 2, :]
                    both_parts(dst, b0).then_inc(free, 1)
                elif kind == "gate":
                    chunk_done(dve, CHUNKS.index((u, 3)))
                    if g:
                        dve.wait_ge(S["gate_sig"], g)
                    both_parts(g_sum[:, :, :], b0).then_inc(free, 1)
                    dve.wait_ge(free, u // 2 + 1)
                    dve.sem_inc(S["gate_in"], 1)
                elif kind == "proj":
                    chunk_done(dve, CHUNKS.index((u, 1)))
                    both_parts(g_pr[:, :, :], b0).then_inc(free, 1)
                    dve.wait_ge(free, u // 2 + 1)
                    dve.wait_ge(S["gate_sig"], g + 1)
                    tt_(yT[:, 2 * g:2 * g + 2, :], g_pr[:, :, :], g_sig[:, :, :], ALU.mult).then_inc(S["y_ready"], 1)

            def root_mean(r, root_in, root_done):
                chain(tt_(rstd[:, 2:4, :], ss[:, 2:4, :], r, ALU.mult))
                chain(tt_(rstd[:, 2:4, :], rstd[:, 2:4, :], r, ALU.mult))
                dve.tensor_scalar(rstd[:, 2:4, :], rstd[:, 2:4, :], 1.0 / HD, EPS, ALU.mult, ALU.add).then_inc(root_in, 1)
                dve.wait_ge(root_done, 1)
                chain(dve.reciprocal(rstd[:, 2:4, :], rstd[:, 2:4, :]))
                chain(tt_(rstd[:, 2:4, :], rstd[:, 2:4, :], r, ALU.mult))

            def step(name, n):
                if name == "gdn_out":
                    tt = (n - 3) % 2
                    o = gvt[:, tt, :, :]
                    if n < 2:
                        dve.wait_ge(S["gsq_in"], n + 1)
                        dve.tensor_reduce(ss[:, 2 + n, :], osq[:, :, :], AX.X, ALU.add).then_inc(S["gsq_done"], 1)
                    elif n == 2:
                        dve.wait_ge(S["gsq_done"], 2)
                        root_mean(rn[:, 0, :, :], S["groot_in"], S["groot_done"])
                    elif n < 5:
                        chain(tt_(o, o, over_free(rstd[:, 2 + tt, :], HD), ALU.mult))
                    else:
                        if n == 5:
                            units_read(dve, "z")
                        tt_(o, o, z[:, tt, :, :], ALU.mult).then_inc(S["gy_ready"], 1)
                else:
                    if n == 0:
                        units_read(dve, "mlo")
                        item_read(dve, "sv", NC - 1)
                    if n in (1, 2):
                        dve.wait_ge(S["msq_done"], n)
                        chain(dve.tensor_reduce(ss[:, 1 + n, :], osq[:, :, :], AX.X, ALU.add))
                    if n < 2:
                        tt_(mv[:, n, :, :], mv[:, n, :, :], mo[:, n, :, :], ALU.mult).then_inc(S["msq_in"], 1)
                    elif n == 3:
                        root_mean(rd[:, :, :], S["mroot_in"], S["mroot_done"])
                    elif n > 3:
                        tt_(mv[:, n - 4, :, :], mv[:, n - 4, :, :], over_free(rstd[:, n - 2, :], HD), ALU.mult).then_inc(S["my_ready"], 1)

            fcc = fconv_c[:, :, :].rearrange("p a b -> p (a b)")
            for tt in range(NT):
                dve.wait_ge(S["sums_ready"], tt + 1)
                chain(dve.reciprocal(rstd[:, 0, tt:tt + 1], rstd[:, 0, tt:tt + 1]))
                dve.tensor_scalar(x_in[:, tt, :], x_in[:, tt, :], rstd[:, 0, tt:tt + 1], None,
                                  ALU.mult).then_inc(S["xs_ready"], 1)
                if tt == 0:
                    dve.wait_ge(S["rows_turned"], 1)
                    dve.tensor_copy(cols[:, :], ps[:, 4, 0:82])
                    dve.tensor_copy(conv_c[:, :, :].rearrange("p a b -> p (a b)"), ps[:, 4, P:P + 96])
                    dve.tensor_copy(fcc[:, 0:256], ps[:, 4, 256:512])
                    dve.tensor_copy(fcc[:, 256:264], ps[:, 5, 0:8]).then_inc(S["cols_ready"], 1)
            split_lo(dve, 0)
            turn_x_lo()

            k = 0
            for c, (u, t) in enumerate(CHUNKS):
                if not on_pool(c + SLOTS):
                    split_lo(dve, c + SLOTS)
                if t == UNIT_CHUNKS[UNITS[u][0]] - 1:
                    unit(u)
                if c == 1:
                    scalar_gates()
                if 20 <= c < 20 + NT:
                    dve.tensor_copy(xm[:, c - 20, :, :], over_heads(ident[:, :], H))
                    dve.tensor_copy(xmt[:, c - 20, :, :], over_heads(ident[:, :], H)).then_inc(S["inv_start"], 1)
                while k < len(ITEMS) and ITEMS[k][0] == c:
                    item(k)
                    if ITEMS[k][1] == "solve_xt" and ITEMS[k][2] == (1, LEVELS - 1):
                        for tt in range(NT):
                            tt_(kbg[:, tt, :, :], gkt[:, tt, :, :], over_free(c_w[:, tt, :], HD), ALU.mult).then_inc(S["kbg_ready"], 1)
                            tt_(gvt[:, tt, :, :], gvt[:, tt, :, :], over_free(beta[:, tt, :], HD), ALU.mult).then_inc(S["vb_ready"], 1)
                        for tt in range(NT):
                            dve.wait_ge(S["kbg_ready"], tt + 1)
                            tt_(gkt[:, tt, :, :], gkt[:, tt, :, :], over_free(c_k[:, tt, :], HD), ALU.mult).then_inc(S["kg_ready"], 1)
                    if ITEMS[k][1] == "o" and ITEMS[k][2] == (NC - 1,):
                        for tt in range(NT):
                            on_diagonal(fr[:, tt, :, :], fcum[:, tt, :]).then_inc(S["fr_ready"], 1)
                    if ITEMS[k][1] == "pv" and ITEMS[k][2] == (1,):
                        chain(tt_(vs[:, :, :], i_pre, bc_, ALU.subtract))
                        for tt in range(NT):
                            on_diagonal(mr[:, tt, :, :], vs[:, tt, :]).then_inc(S["mr_ready"], 1)
                    k += 1
                for _, name, n in (e for e in STEPS if e[0] == c):
                    step(name, n)
            for p in range(2):
                dve.wait_ge(item_free[p], (len(ITEMS) + 1 - p) // 2)
            for p in range(2):
                dve.sem_inc(pair_read[p], 1)
            def side_lo(n, it, kt_ap, slot):
                dve.wait_ge(S["side_hi"], n + 1 + it)
                tt_(side[:, slot, SEQ:2 * SEQ], kt_ap, side[:, slot, 0:SEQ], ALU.subtract).then_inc(S["side_ready"], 1)

            def gates_round(i, last=False):
                if last:
                    for kt in range(2):
                        side_lo(kt, 0, yT[:, kt, :], kt)
                c = N1
                for q in range(4):
                    b0, j = 4 * (q % 2), q // 2
                    for t in range(6):
                        if t == 3:
                            chunk_done(dve, c, i * 6)
                            dve.wait_ge(S["gate_sig"], i * 4 + (GROUPS + q))
                            both_parts(g_sum[:, :, :], b0).then_inc(S["gate_in"], 1)
                        if t == 5:
                            chunk_done(dve, c, i * 6)
                            dve.wait_ge(S["y_ready"], i * 8 + (GROUPS + 2 * q))
                            both_parts(g_pr[:, :, :], b0 + 2).then_inc(pair_read[q % 2], 1)
                        if not on_pool(c + SLOTS):
                            split_lo(dve, c + SLOTS, i * 6)
                        if t == 5:
                            dve.wait_ge(pair_read[q % 2], i * 2 + (q // 2 + 2))
                            dve.wait_ge(S["gate_sig"], i * 4 + (GROUPS + q + 1))
                            tt_(g_y[:, :, :], g_pr[:, :, :], g_sig[:, :, :], ALU.mult).then_inc(S["y_ready"], 1)
                            dve.wait_ge(S["y_ready"], i * 8 + (GROUPS + 2 * q + 1))
                            y = yT[:, bass.ds(i * 4 + 2 * j, 2), :]
                            tt_(y, y, g_y[:, :, :], ALU.add).then_inc(S["y_ready"], 1)
                        c += 1

            with dve.Fori(0, GROUPS // 2 - 1) as i:
                gates_round(i)
            gates_round(GROUPS // 2 - 1, last=True)
            with dve.Fori(0, KT // 2 - 1) as i:
                for j in range(4):
                    if not on_pool(N2 + SLOTS + j):
                        split_lo(dve, N2 + SLOTS + j, i)
                    if j % 2:
                        side_lo(2 + j // 2, i * 2, yT[:, bass.ds(i * 2 + (2 + j // 2), 1), :].rearrange("p a b -> p (a b)"), j // 2)

            def add_quarter(p, c0, tt, half):
                quarter_written(dve, p, c0, tt, half)
                x = x1[:, tt, CHUNK * half:CHUNK * half + CHUNK]
                tt_(x, x, ps[:, 4 * tt + 2 * half:4 * tt + 2 * half + 2, :].rearrange("p a b -> p (a b)"),
                    ALU.add).then_inc(S["x1_ready"], 1)

            def norm_rows(p, c0, before_last):
                for tt in range(NT):
                    for half in range(2):
                        add_quarter(p, c0, tt, half)
                    if tt == 1:
                        before_last()
                    dve.wait_ge(S["sums_ready"], 2 + 2 * p + tt + 1)
                    r = rstd[:, 1, 2 * p + tt:2 * p + tt + 1]
                    dve.reciprocal(r, r).then_inc(S["rstd_ready"], 1)
                    dve.wait_ge(S["rstd_ready"], 2 * p + tt + 1)
                    for a, b in (((0, 1024),), ((0, 512), (512, 1024), (1024, 1536)))[tt]:
                        dve.scalar_tensor_tensor(xs[:, tt, a:b], x1[:, tt, a:b], r, (gfin if p else gffn)[:, a:b],
                                                 ALU.mult, ALU.mult).then_inc(S["xs_ready"], 1)

            dve.wait_ge(S["x_again"], 16)
            dve.wait_ge(S["gffn_loaded"], 16)
            norm_rows(0, N3 - 4, lambda: split_lo(dve, N3))
            for n, (tt, b) in enumerate(TURNS):
                dve.wait_ge(S["xt_hi"], 4 + n + 1)
                dst, src = turned(tt, b, SEQ)
                tt_(dst, src, turned(tt, b)[0], ALU.subtract).then_inc(S["xt_ready"], 1)
                if n in (2, 3):
                    split_lo(dve, N3 + 2 * n - 3)
            chain(dve.memset(upre[:, :, :, 0:2], 0.0))
            for v in range(2):
                dve.sem_inc(up_read[v], 1)

            def up_round(i, last=False):
                if last:
                    for kt in range(2):
                        side_lo(KT + kt, 0, hT[:, kt, :], kt)
                for v in range(2):
                    for j in range(8):
                        c = N3 + 8 * v + j
                        w = j // 4
                        if j % 4 == 3:
                            chunk_done(dve, c, i * 4)
                            both_parts(upre[:, w, :, 2:2 + SEQ], 4 * v + 2 * w).then_inc(up_read[v] if w else S["gate_pre"], 1)
                        if not on_pool(c + SLOTS):
                            split_lo(dve, c + SLOTS, i * 4)
                        if j % 4 == 3:
                            if w == 0:
                                dve.wait_ge(S["gate_pre"], i * 2 + (v + 1))
                            else:
                                dve.wait_ge(up_read[v], i + 2)
                            for tap in (2, 1, 0):
                                for b in range(2):
                                    at = i * 4 + (tap * 2 * FKT + FKT * (1 - w) + 2 * v + b)
                                    cw = fcc[:, bass.ds(at, 1)]
                                    src = upre[:, w, b, tap:tap + SEQ]
                                    if tap == 2:
                                        ins = dve.tensor_scalar(uacc[:, w, b, :], src, cw, None, ALU.mult)
                                    else:
                                        ins = dve.scalar_tensor_tensor(uacc[:, w, b, :], src, cw, uacc[:, w, b, :], ALU.mult, ALU.add)
                                if tap:
                                    ins.then_inc(S["up_tap"], 1)
                                    dve.wait_ge(S["up_tap"], i * 8 + (4 * v + 2 * w + 3 - tap))
                                elif w == 0:
                                    ins.then_inc(S["gate_conv"], 1)
                                else:
                                    ins.then_inc(S["u_conv"], 1)
                                    dve.wait_ge(S["u_conv"], i * 2 + (v + 1))
                            if w:
                                dve.wait_ge(S["up_silu"], i * 2 + (v + 1))
                                tt_(hT[:, bass.ds(i * 4 + 2 * v, 2), :], uacc[:, 1, :, :], usil[:, :, :], ALU.mult).then_inc(S["h_ready"], 1)

            with dve.Fori(0, FF // 512 - 1) as i:
                up_round(i)
            up_round(FF // 512 - 1, last=True)
            with dve.Fori(0, FKT // 2 - 1) as i:
                for j in range(4):
                    if not on_pool(N4 + SLOTS + j):
                        split_lo(dve, N4 + SLOTS + j, i)
                    if j % 2:
                        side_lo(KT + 2 + j // 2, i * 2, hT[:, bass.ds(i * 2 + (2 + j // 2), 1), :].rearrange("p a b -> p (a b)"), j // 2)
            dve.wait_ge(S["gfin_loaded"], 16)
            norm_rows(1, N5 - 4, lambda: None)

        @block.gpsimd
        def _(pool):
            order = [0]

            def chain(ins):
                order[0] += 1
                ins.then_inc(S["pool_chain"], 1)
                pool.wait_ge(S["pool_chain"], order[0])

            def keep(t, cmp, base, pattern, chan, fill=0.0):
                chain(pool.affine_select(out=t, in_=t, compare_op=cmp, fill=fill, base=base, pattern=pattern,
                                         channel_multiplier=chan))

            pool.memset(eps_c[:, 0:1], EPS)
            pool.memset(eps_c[:, 1:2], 1.0)
            chain(pool.memset(bias5[:, :, :], 0.0))
            chain(pool.memset(ident[:, :], 0.0))
            pool.memset(tiny[:, :, :], 0.0).then_inc(S["consts"], 1)
            keep(ident[:, :], ALU.not_equal, 0, [[-1, P]], 1, fill=1.0)
            pool.memset(ones[:, :], 1.0).then_inc(S["consts"], 1)
            chain(pool.memset(upto[:, :], 1.0))
            keep(upto[:, :], ALU.is_ge, 0, [[1, P]], -1)
            two = [[-L, 2], [0, L]]
            for t in (same_c, upto_c, last_c):
                chain(pool.memset(t[:, :], 1.0))
                v = t[:, :].rearrange("p (c r) -> p c r", c=2)
                if t is last_c:
                    keep(v, ALU.is_equal, -(L - 1), two, 1)
                else:
                    keep(v, ALU.is_ge, 0, two, 1)
                    keep(v, ALU.is_ge, L - 1, [[L, 2], [0, L]], -1)
            keep(upto_c[:, :], ALU.is_ge, 0, [[1, P]], -1)
            for b in range(2):
                chain(pool.memset(sel[:, b, :], 1.0))
                keep(sel[:, b, :], ALU.is_equal, -(L * b + L - 1), [[0, P]], 1)
            for lv in range(LEVELS):
                b = 1 << lv
                n = P // (2 * b)
                chain(pool.memset(level[:, lv, :], 1.0))
                v = level[:, lv, :].rearrange("p (n w) -> p n w", w=2 * b)
                keep(v, ALU.is_ge, 0, [[-2 * b, n], [0, 2 * b]], 1)
                keep(v, ALU.is_ge, b - 1, [[2 * b, n], [0, 2 * b]], -1)
                keep(v, ALU.is_ge, -b, [[0, n], [1, 2 * b]], 0)
            chain(pool.memset(tiny[:, 1, :], 0.0))
            pool.memset(tiny[:, 1, :], 0.0).then_inc(S["consts"], 1)
            split_lo(pool, SLOTS - 1)

            def masked(lv, tt):
                pool.tensor_tensor(nlv[:, tt, :, :], nt_[:, tt, :, :], over_heads(level[:, lv, :], H),
                                   ALU.mult).then_inc(S["level_ready"], 1)

            def item(k):
                _, name, args = ITEMS[k]
                if name == "norm" and args == (1,):
                    pass
                elif name == "gam":
                    tt, = args
                    pool.wait_ge(S["gam_raw"], tt + 1)
                    e = ed[:, tt, :, :]
                    pool.affine_select(out=e, in_=e, compare_op=ALU.is_ge, fill=NEG, base=0,
                                       pattern=[[0, H], [1, P]], channel_multiplier=-1).then_inc(S["e_masked"], 1)
                    pool.wait_ge(S["e_masked"], 2 * tt + 1)
                    pool.memset(ed[0:L, tt, :, L:P], NEG).then_inc(S["e_masked"], 1)
                    pool.wait_ge(S["e_masked"], 2 * tt + 2)
                elif name == "qk":
                    tt, = args
                    item_read(pool, "kk", tt)
                    n = nt_[:, tt, :, :]
                    chain(pool.affine_select(out=n, in_=n, compare_op=ALU.is_ge, fill=0.0, base=-1,
                                             pattern=[[0, H], [1, P]], channel_multiplier=-1))
                    item_read(pool, "qk", tt)
                    if tt == 1:
                        for t2 in range(NT):
                            masked(0, t2)
                elif name == "solve_p":
                    tt, lv = args
                    if lv < LEVELS - 1:
                        item_written(pool, k)
                        masked(lv + 1, tt)
                elif name == "fbc" and args == (1,):
                    for kt in range(NT):
                        item_read(pool, "fbc", kt)
                    m = mf0[:, :, :]
                    pool.affine_select(out=m, in_=m, compare_op=ALU.is_ge, fill=NEG, base=0,
                                       pattern=[[0, H], [-1, P]], channel_multiplier=1).then_inc(S["mf_ready"], 1)
                    m = mf1[:, :, P:SEQ]
                    pool.affine_select(out=m, in_=m, compare_op=ALU.is_ge, fill=NEG, base=0,
                                       pattern=[[0, H], [-1, P]], channel_multiplier=1).then_inc(S["mf_ready"], 1)
                elif name == "vbc":
                    tt, = args
                    item_read(pool, "vbc", tt)
                    e = me[:, tt, :, :]
                    chain(pool.affine_select(out=e, in_=e, compare_op=ALU.is_ge, fill=NEG, base=0,
                                             pattern=[[0, H], [-1, P]], channel_multiplier=1))
                    pool.memset(me[L:P, tt, :, 0:L], NEG).then_inc(S["me_masked"], 1)
                    pool.wait_ge(S["me_masked"], tt + 1)
                elif name == "mbc":
                    tt, = args
                    item_read(pool, "mbc", tt)
                    e = me[:, tt, :, :]
                    chain(pool.affine_select(out=e, in_=e, compare_op=ALU.is_ge, fill=NEG, base=0,
                                             pattern=[[0, H], [1, P]], channel_multiplier=-1))
                    pool.memset(me[0:L, tt, :, L:P], NEG).then_inc(S["mt_masked"], 1)
                    pool.wait_ge(S["mt_masked"], tt + 1)

            k = 0
            for c in range(N1):
                if on_pool(c + SLOTS):
                    split_lo(pool, c + SLOTS)
                while k < len(ITEMS) and ITEMS[k][0] == c:
                    item(k)
                    k += 1
            assert on_pool(N3 + 2)

            def rounds(first, n, per):
                with pool.Fori(0, n) as i:
                    for j in range(per):
                        if on_pool(first + j + SLOTS):
                            split_lo(pool, first + j + SLOTS, i * (per // SLOTS))

            def scale_tile(p, tt):
                a = (1024, 1536)[tt]
                o = xs[:, tt, a:D]
                pool.wait_ge(S["x1_ready"], 4 * p + 2 * tt + 2)
                chain(pool.tensor_tensor(o, x1[:, tt, a:D], (gfin if p else gffn)[:, a:D], ALU.mult))
                pool.wait_ge(S["rstd_ready"], 2 * p + tt + 1)
                r = rstd[:, 1, 2 * p + tt:2 * p + tt + 1]
                pool.tensor_tensor(o, o, r.to_broadcast([P, D - a]), ALU.mult).then_inc(S["xs_pool"], 1)

            rounds(N1, GROUPS // 2, 24)
            rounds(N2, KT // 2 - 1, 4)
            pool.wait_ge(S["gffn_loaded"], 16)
            scale_tile(0, 0)
            split_lo(pool, N3 + 2)
            scale_tile(0, 1)
            rounds(N3, FF // 512, 16)
            rounds(N4, FKT // 2 - 1, 4)
            pool.wait_ge(S["gfin_loaded"], 16)
            for tt in range(NT):
                scale_tile(1, tt)


_INS = ['x', 'norm_mix_g', 'w_in', 'fox_f_bias', 'gdn_conv_w', 'gdn_a_log', 'gdn_dt_bias', 'gdn_norm_g',
        'ml_i_bias', 'ml_f_bias', 'ml_norm_g', 'gate_bias', 'w_fox_proj', 'w_gdn_proj', 'w_ml_proj',
        'w_out', 'norm_ffn_g', 'w_up', 'ffn_conv_w', 'w_down', 'norm_final_g']
_OUTS = [((1, SEQ, D), 'float32')]


def kernel(**inputs):
    import numpy as _np
    import concourse.bacc as _bacc
    from concourse import mybir as _mybir
    from concourse.bass_utils import run_bass_kernel_spmd as _run

    nc = _bacc.Bacc("TRN2", target_bir_lowering=False, num_devices=1)
    arrays, args = {}, []
    for name in _INS:
        a = _np.ascontiguousarray(inputs[name])
        arrays[f"in_{name}_dram"] = a
        args.append(nc.dram_tensor(f"in_{name}_dram", a.shape, _mybir.dt.from_np(a.dtype), kind="ExternalInput").ap())
    for i, (shape, dtype) in enumerate(_OUTS):
        dt = _mybir.dt.from_np(_np.dtype(dtype))
        args.append(nc.dram_tensor(f"out_{i}_dram", shape, dt, kind="ExternalOutput").ap())
    hybrid_layer_kernel(nc, *args)
    r = _run(nc, [arrays], core_ids=[0])
    return r.results[0]["out_0_dram"]
```
